# Optimizing a Trainium2 kernel written in Bass

```python
import jax, jax.numpy as jnp
from jax import lax
import numpy as np

D_MODEL = 1024
BATCH = 1
SEQ = 1024
DEPTH = 1

HEAD_DIM = 64
Q_BLOCK = 128
CONV_WIDTH = 3
CONV_CH = 256
DSA_HEADS = 4
IDX_HEADS = 4
IDX_DIM = 64
DSA_TOPK_MAX = 256
FOX_HEADS = 4
SWA_HEADS = 4
SWA_KV_HEADS = 2
WINDOW = 128
N_BRANCH = 4
BRANCH_WIDTH = 256
D_FF = -(-8 * D_MODEL // (3 * 256)) * 256
RMS_EPS = 1e-6
N_MOD = 6

IN_SIZES = (
    CONV_CH, CONV_CH, CONV_CH,
    DSA_HEADS * HEAD_DIM, HEAD_DIM, HEAD_DIM,
    IDX_HEADS * IDX_DIM, IDX_DIM, IDX_HEADS,
    FOX_HEADS * HEAD_DIM, FOX_HEADS * HEAD_DIM, FOX_HEADS * HEAD_DIM, FOX_HEADS,
    SWA_HEADS * HEAD_DIM, SWA_KV_HEADS * HEAD_DIM, SWA_KV_HEADS * HEAD_DIM,
    N_BRANCH * D_MODEL,
)
IN_WIDTH = sum(IN_SIZES)

kernel_name = "hybrid_gated_parallel_mixers"

def _split(z, sizes):
    offs = [int(o) for o in np.cumsum(sizes)[:-1]]
    return jnp.split(z, offs, axis=-1)

def _alibi_slopes(n):
    return jnp.asarray(2.0 ** (-8.0 * np.arange(1, n + 1) / n), dtype=jnp.float32)

def _rmsnorm(x, g):
    xf = x.astype(jnp.float32)
    y = xf * lax.rsqrt(jnp.mean(xf * xf, axis=-1, keepdims=True) + RMS_EPS)
    return (y * g.astype(jnp.float32)).astype(x.dtype)

def _to_blocks(a, bsz, nb):
    return jnp.moveaxis(a.reshape(bsz, nb, Q_BLOCK, *a.shape[2:]), 1, 0)

def _short_conv(u, b_gate, c_gate, w_conv):
    z = c_gate * u
    kern = w_conv[:, None, :].astype(z.dtype)
    y = lax.conv_general_dilated(z, kern, window_strides=(1,), padding=[(CONV_WIDTH - 1, 0)],
                                 dimension_numbers=('NWC', 'WIO', 'NWC'),
                                 feature_group_count=z.shape[-1])
    return b_gate * y

def _dsa(q, k, v, qi, ki, wi, slopes):
    bsz, L = q.shape[:2]
    nb = L // Q_BLOCK
    topk = min(DSA_TOPK_MAX, L // 4)
    scale = HEAD_DIM ** -0.5
    key_pos = jnp.arange(L)

    def blk(args):
        qb, qib, wib, t0 = args
        qpos = t0 + jnp.arange(Q_BLOCK)
        s = jnp.einsum('bqhd,bkd->bqhk', qib, ki).astype(jnp.float32)
        score = jnp.einsum('bqh,bqhk->bqk', wib.astype(jnp.float32), jax.nn.relu(s))
        causal = key_pos[None, :] <= qpos[:, None]
        score = jnp.where(causal[None], score, -jnp.inf)
        _, idx = lax.top_k(score, topk)
        kg = jax.vmap(lambda kb, ib: kb[ib])(k, idx)
        vg = jax.vmap(lambda vb, ib: vb[ib])(v, idx)
        dist = qpos[None, :, None] - idx
        logits = jnp.einsum('bqhd,bqkd->bhqk', qb, kg).astype(jnp.float32) * scale
        logits = logits - slopes[None, :, None, None] * dist[:, None].astype(jnp.float32)
        logits = jnp.where((dist >= 0)[:, None], logits, -jnp.inf)
        p = jax.nn.softmax(logits, axis=-1).astype(vg.dtype)
        return jnp.einsum('bhqk,bqkd->bqhd', p, vg)

    out = lax.map(blk, (_to_blocks(q, bsz, nb), _to_blocks(qi, bsz, nb), _to_blocks(wi, bsz, nb),
                        jnp.arange(nb) * Q_BLOCK))
    return jnp.moveaxis(out, 0, 1).reshape(bsz, L, DSA_HEADS * HEAD_DIM)

def _fox(q, k, v, f_logit):
    bsz, L = q.shape[:2]
    nb = L // Q_BLOCK
    scale = HEAD_DIM ** -0.5
    F = jnp.cumsum(jax.nn.log_sigmoid(f_logit.astype(jnp.float32)), axis=1)
    Ft = jnp.moveaxis(F, 1, 2)
    Fq_blocks = jnp.moveaxis(Ft.reshape(bsz, FOX_HEADS, nb, Q_BLOCK), 2, 0)
    key_pos = jnp.arange(L)

    def blk(args):
        qb, Fq, t0 = args
        qpos = t0 + jnp.arange(Q_BLOCK)
        logits = (jnp.einsum('bqhd,bkhd->bhqk', qb, k).astype(jnp.float32) * scale
                  + Fq[..., None] - Ft[:, :, None, :])
        causal = key_pos[None, :] <= qpos[:, None]
        logits = jnp.where(causal, logits, -jnp.inf)
        p = jax.nn.softmax(logits, axis=-1).astype(v.dtype)
        return jnp.einsum('bhqk,bkhd->bqhd', p, v)

    out = lax.map(blk, (_to_blocks(q, bsz, nb), Fq_blocks, jnp.arange(nb) * Q_BLOCK))
    return jnp.moveaxis(out, 0, 1).reshape(bsz, L, FOX_HEADS * HEAD_DIM)

def _swa(q, k, v, sinks, slopes):
    bsz, L = q.shape[:2]
    nb = L // Q_BLOCK
    G = SWA_HEADS // SWA_KV_HEADS
    scale = HEAD_DIM ** -0.5
    qb = q.reshape(bsz, nb, Q_BLOCK, SWA_KV_HEADS, G, HEAD_DIM)

    def band(a):
        a = a.reshape(bsz, nb, Q_BLOCK, SWA_KV_HEADS, HEAD_DIM)
        prev = jnp.pad(a[:, :-1], ((0, 0), (1, 0), (0, 0), (0, 0), (0, 0)))
        return jnp.concatenate([prev, a], axis=2)

    kb, vb = band(k), band(v)
    logits = jnp.einsum('bnqhgd,bnshd->bnhgqs', qb, kb).astype(jnp.float32) * scale
    i = jnp.arange(Q_BLOCK)[:, None]
    j = jnp.arange(2 * Q_BLOCK)[None, :]
    dist = i - j + Q_BLOCK
    key_ok = (jnp.arange(nb)[:, None, None] * Q_BLOCK + j[None] - Q_BLOCK) >= 0
    valid = (dist >= 0)[None] & (dist < WINDOW)[None] & key_ok
    sl = slopes.reshape(SWA_KV_HEADS, G)
    logits = logits - sl[None, None, :, :, None, None] * dist.astype(jnp.float32)
    logits = jnp.where(valid[None, :, None, None], logits, -jnp.inf)
    sink = jnp.broadcast_to(sinks.astype(jnp.float32).reshape(SWA_KV_HEADS, G)[None, None, :, :, None, None],
                            logits.shape[:-1] + (1,))
    p = jax.nn.softmax(jnp.concatenate([logits, sink], axis=-1), axis=-1)[..., :-1].astype(vb.dtype)
    out = jnp.einsum('bnhgqs,bnshd->bnqhgd', p, vb)
    return out.reshape(bsz, L, SWA_HEADS * HEAD_DIM)

def _mixer(h, w_in, conv_w, fox_bias, swa_sinks, w_branch, w_o, swa_slopes, dsa_slopes):
    bsz, L, _ = h.shape
    z = h @ w_in
    (a_u, a_b, a_c, d_q, d_k, d_v, d_qi, d_ki, d_wi,
     f_q, f_k, f_v, f_f, s_q, s_k, s_v, g) = _split(z, IN_SIZES)
    heads = lambda t, n, dh: t.reshape(bsz, L, n, dh)
    y_a = _short_conv(a_u, a_b, a_c, conv_w)
    y_d = _dsa(heads(d_q, DSA_HEADS, HEAD_DIM), d_k, d_v, heads(d_qi, IDX_HEADS, IDX_DIM),
               d_ki, d_wi, dsa_slopes)
    y_f = _fox(heads(f_q, FOX_HEADS, HEAD_DIM), heads(f_k, FOX_HEADS, HEAD_DIM),
               heads(f_v, FOX_HEADS, HEAD_DIM), f_f + fox_bias)
    y_s = _swa(heads(s_q, SWA_HEADS, HEAD_DIM), heads(s_k, SWA_KV_HEADS, HEAD_DIM),
               heads(s_v, SWA_KV_HEADS, HEAD_DIM), swa_sinks, swa_slopes)
    ys = jnp.stack([y_a, y_d, y_f, y_s], axis=2)
    proj = jnp.einsum('blnc,ncd->blnd', ys, w_branch)
    gates = jax.nn.sigmoid(g.reshape(bsz, L, N_BRANCH, D_MODEL))
    return jnp.sum(gates * proj, axis=2) @ w_o

def setup_inputs(seed: int = 0) -> dict:
    key = jax.random.key(seed)
    ks = jax.random.split(key, 16)
    nrm = lambda k, shape, s: jax.random.normal(k, shape, jnp.float32) * s
    return {
        "x": nrm(ks[0], (BATCH, SEQ, D_MODEL), 1.0),
        "c": nrm(ks[1], (BATCH, D_MODEL), 1.0),
        "w_ada": nrm(ks[2], (DEPTH, D_MODEL, N_MOD * D_MODEL), 0.5 * D_MODEL ** -0.5),
        "b_ada": nrm(ks[3], (DEPTH, N_MOD * D_MODEL), 0.02),
        "norm_g": 1.0 + nrm(ks[4], (DEPTH, 4, D_MODEL), 0.05),
        "w_in": nrm(ks[5], (DEPTH, D_MODEL, IN_WIDTH), D_MODEL ** -0.5),
        "conv_w": nrm(ks[6], (DEPTH, CONV_WIDTH, CONV_CH), CONV_WIDTH ** -0.5),
        "fox_bias": 2.0 + nrm(ks[7], (DEPTH, FOX_HEADS), 0.5),
        "swa_sinks": nrm(ks[8], (DEPTH, SWA_HEADS), 0.5),
        "w_branch": nrm(ks[9], (DEPTH, N_BRANCH, BRANCH_WIDTH, D_MODEL), BRANCH_WIDTH ** -0.5),
        "w_o": nrm(ks[10], (DEPTH, D_MODEL, D_MODEL), D_MODEL ** -0.5),
        "w_gate": nrm(ks[11], (DEPTH, D_MODEL, D_FF), D_MODEL ** -0.5),
        "w_up": nrm(ks[12], (DEPTH, D_MODEL, D_FF), D_MODEL ** -0.5),
        "w_down": nrm(ks[13], (DEPTH, D_FF, D_MODEL), D_FF ** -0.5),
    }

def reference(x, c, w_ada, b_ada, norm_g, w_in, conv_w, fox_bias, swa_sinks, w_branch, w_o,
              w_gate, w_up, w_down):
    slopes = _alibi_slopes(SWA_HEADS + DSA_HEADS)
    swa_slopes, dsa_slopes = slopes[:SWA_HEADS], slopes[SWA_HEADS:]
    for l in range(DEPTH):
        mod = jax.nn.silu(c) @ w_ada[l] + b_ada[l]
        sh1, sc1, g1, sh2, sc2, g2 = [m[:, None, :] for m in jnp.split(mod, N_MOD, axis=-1)]
        h = _rmsnorm(x, norm_g[l, 0]) * (1.0 + sc1) + sh1
        y = _mixer(h, w_in[l], conv_w[l], fox_bias[l], swa_sinks[l], w_branch[l], w_o[l],
                   swa_slopes, dsa_slopes)
        x = x + g1 * _rmsnorm(y, norm_g[l, 1])
        h = _rmsnorm(x, norm_g[l, 2]) * (1.0 + sc2) + sh2
        y = (jax.nn.silu(h @ w_gate[l]) * (h @ w_up[l])) @ w_down[l]
        x = x + g2 * _rmsnorm(y, norm_g[l, 3])
    return x


_drawn_inputs = setup_inputs


def setup_inputs(seed=0):
    import zlib

    import numpy as np

    out = dict(_drawn_inputs(seed))
    spreads = {}
    factors = {'fox_bias': 2.905, 'swa_sinks': 8.0}
    for name, (base, spread) in spreads.items():
        noise = np.random.default_rng([zlib.crc32(name.encode()), seed]).standard_normal(out[name].shape)
        drawn = base * np.exp(spread * noise) if base else spread * noise
        out[name] = __import__('jax').numpy.asarray(drawn.astype(out[name].dtype))
    for name, factor in factors.items():
        out[name] = (out[name] * factor).astype(out[name].dtype)
    return out
```

```python
from contextlib import ExitStack, contextmanager

import concourse.bass as bass
from concourse import mybir

F32 = mybir.dt.float32
F32R = mybir.dt.float32r
BF16 = mybir.dt.bfloat16
ALU = mybir.AluOpType
ACT = mybir.ActivationFunctionType

P = 128
D = 1024
L = 1024
KT = D // P
TT = L // P
HALF = 512
HD = 64
HEADS = 4
BW = 256
BT = BW // P
FF = -(-8 * D // (3 * 256)) * 256
FT = FF // P
FG = FT // 2
TOPK = min(256, L // 4)
KB0 = TOPK // P
WINDOW = 128
EPS = 1e-6
BIG = 1e30
TAKEN = -3e38

VD, VF, VS, VWI, VFF = 0, 64, 320, 448, 452
VN = 456

T_IDX, T_CONV, T_FOX, T_SWA, T_AFS = 0, 3, 9, 13, 16
T_DSA = T_AFS + 3 * KT
T_GD = T_DSA + 3
T_WO = T_GD + KT
T_FFN = T_WO + KT
GT = (KT + BT) * P

U_FOX, U_SWA, U_DSA = 0, HEADS * TT, HEADS * TT + TT
O_FOX, O_SWA, O_DSA = 0, HEADS * 2, HEADS * 2 + TT


MIX0 = 1


class Order:

    def __init__(self, eng, sem):
        self.eng, self.sem, self.base, self.k = eng, sem, 0, 0

    def mark(self, ins):
        ins.then_inc(self.sem, 1)
        self.k += 1

    def wait(self):
        self.eng.wait_ge(self.sem, self.base + self.k)

    def then_wait(self, ins):
        self.mark(ins)
        self.wait()

    @contextmanager
    def loop(self, n, per):
        start = self.base + self.k
        with self.eng.Fori(0, n) as i:
            self.base, self.k = start + i * per, 0
            yield i
            assert self.k == per, (self.k, per)
        self.base, self.k = start + n * per, 0


def build(nc, x, w_z, w_v, w_gates, w_o, w_ffn, w_ada, cols, rows, per_head, consts, window_bias, distance, out):
    with ExitStack() as ctx:
        def sb(name, shape, dt=F32):
            return ctx.enter_context(nc.sbuf_tensor(name, shape, dt))

        def sem(name):
            return ctx.enter_context(nc.semaphore(name))

        h_t = sb("h_t", [P, 2, KT, L], F32R)
        w_t = sb("w_t", [P, 2, 2, GT], F32R)
        y_t = sb("y_t", [P, 2, 2, BT, L], F32R)
        raw = sb("raw", [P, 2, GT])
        region_a = sb("region_a", [P, 8 * L])
        region_b = sb("region_b", [P, 8 * L])
        region_c = sb("region_c", [P, 2 * L])
        region_d = sb("region_d", [P, L])
        col_pack = sb("col_pack", [P, 62])
        head_pack = sb("head_pack", [P, 8])
        const = sb("const", [P, 5, P])
        ident_b = sb("ident_b", [P, P], BF16)
        tri_b = sb("tri_b", [P, P], BF16)
        silu_c = sb("silu_c", [P, KT])
        mod_col = sb("mod_col", [P, 4, KT])
        stat = sb("stat", [P, 3 * TT])
        root = sb("root", [P, 3 * TT])
        rstd = sb("rstd", [P, 3 * TT])
        diag = sb("diag", [P, 2, P])
        top8 = sb("top8", [P, 8])
        mx = sb("mx", [P, 2, 4])
        neg = sb("neg", [P, 2, 4])
        den = sb("den", [P, 2, 4])
        rec = sb("rec", [P, 2, 4])
        sink_e = sb("sink_e", [P, 2, 4])
        eps = sb("eps", [P, 1])
        lf = sb("lf", [P, 3, TT * HEADS])
        ps = ctx.enter_context(nc.psum_tensor("ps", [P, 8, HALF], F32))
        mix_dram = nc.dram_tensor("mix_dram", (P, KT, L), F32, kind="Internal").ap()

        ident, tri, upper, ones, minus = (const[:, i, :] for i in range(5))
        c_col, g0_col, g2_col = col_pack[:, 0:8], col_pack[:, 8:16], col_pack[:, 16:24]
        bias_col = [col_pack[:, 24 + 8 * i:32 + 8 * i] for i in range(4)]
        conv_w = col_pack[:, 56:62].rearrange("p (c k) -> p c k", c=2)
        fox_b, sinks = head_pack[:, 0:4], head_pack[:, 4:8]
        h_hi, h_lo = h_t[:, 0], h_t[:, 1]
        xs = region_a[:, :].rearrange("p (t n) -> p t n", t=8)
        z = xs
        lg = [xs[:, 4], xs[:, 5]]
        pt = [xs[:, 6], xs[:, 7]]
        spare = xs[:, 3]
        conv_z = region_a[:, 4 * L:4 * L + L + 2]
        vn = region_b[:, 0:TT * VN].rearrange("p (t n) -> p t n", t=TT)
        sc_at, at = {}, TT * VN
        for b in range(KB0, TT):
            sc_at[b] = region_b[:, at:at + (b + 1) * P]
            at += (b + 1) * P
        raw_v = region_b[:, TT * VN:TT * VN + KT * VN]
        ada_raw = [region_b[:, i * D:(i + 1) * D] for i in range(3)]
        ada_sum2 = region_b[:, TT * VN:TT * VN + 4 * D].rearrange("p (c n) -> p c n", c=4)
        x1 = region_b[:, :].rearrange("p (t n) -> p t n", t=8)
        ada_sum1 = region_c[:, :].rearrange("p (c n) -> p c n", c=2)
        forget = ada_sum1
        y_s = region_c[:, :].rearrange("p (c n) -> p c n", c=BT)
        g_row = [region_c[:, 0:L], region_c[:, L:2 * L]]
        h_tmp = region_d[:, :]
        sig = region_d[:, 0:HALF]
        prj = region_d[:, HALF:L]
        act2 = [sig, prj]

        def y_hi(buf):
            return y_t[:, buf, 0]

        def y_lo(buf):
            return y_t[:, buf, 1]

        vw = y_t[:, :, :, :, :].rearrange("p a b c n -> p (a b c n)")
        vw_hi = vw[:, 0:KT * VN].rearrange("p (k n) -> p k n", k=KT)
        vw_lo = vw[:, 4 * L:4 * L + KT * VN].rearrange("p (k n) -> p k n", k=KT)

        s_pack = sem("s_pack")
        s_rows = sem("s_rows")
        s_x = sem("s_x")
        s_ada = [sem(f"s_ada{i}") for i in range(3)]
        s_ada_used = sem("s_ada_used")
        s_raw = [sem("s_raw0"), sem("s_raw1")]
        s_rawv = sem("s_rawv")
        s_w_hi = sem("s_w_hi")
        s_w_lo = sem("s_w_lo")
        s_vw_hi = sem("s_vw_hi")
        s_vw_lo = sem("s_vw_lo")
        s_silu = sem("s_silu")
        s_mod = sem("s_mod")
        s_root = sem("s_root")
        s_diag = sem("s_diag")
        s_ht = sem("s_ht")
        s_hval = sem("s_hval")
        pool_order = sem("pool_order")
        s_h_hi = sem("s_h_hi")
        s_h = sem("s_h")
        s_v = sem("s_v")
        s_vn = sem("s_vn")
        s_z = sem("s_z")
        s_zf = sem("s_zf")
        s_s = sem("s_s")
        s_relu = sem("s_relu")
        s_score = sem("s_score")
        s_prod = sem("s_prod")
        s_conv = sem("s_conv")
        s_ya_hi = sem("s_ya_hi")
        s_ya = sem("s_ya")
        s_fabs = sem("s_fabs")
        s_fln = sem("s_fln")
        s_fu = sem("s_fu")
        s_fp = sem("s_fp")
        s_forget = sem("s_forget")
        s_logit = sem("s_logit")
        s_lg = sem("s_lg")
        s_neg = sem("s_neg")
        s_exp = sem("s_exp")
        s_prob = sem("s_prob")
        s_t = sem("s_t")
        s_pt = sem("s_pt")
        s_pv = sem("s_pv")
        s_o_hi = sem("s_o_hi")
        s_of = sem("s_of")
        s_table = sem("s_table")
        s_ys_hi = sem("s_ys_hi")
        s_ys = sem("s_ys")
        s_mix = sem("s_mix")
        s_spill = sem("s_spill")
        s_refill = sem("s_refill")
        s_mix_hi = sem("s_mix_hi")
        s_mix_lo = sem("s_mix_lo")
        s_ot = sem("s_ot")
        s_oroot = sem("s_oroot")
        s_x1 = sem("s_x1")
        s_silu2 = sem("s_silu2")
        s_a = sem("s_a")
        s_a_hi = sem("s_a_hi")
        s_a_lo = sem("s_a_lo")
        s_y = sem("s_y")
        s_yf = sem("s_yf")
        s_zero = sem("s_zero")
        s_yroot = sem("s_yroot")
        s_final = sem("s_final")
        s_out = sem("s_out")
        dve_order = sem("dve_order")
        act_order = sem("act_order")

        fox_units = [("fox", b, h) for h in range(HEADS) for b in range(TT)]
        swa_units = [("swa", b, None) for b in range(TT)]
        dsa_units = [("dsa", b, h) for b in range(TT) for h in range(HEADS)]
        units = fox_units + swa_units + dsa_units

        def group_of(u):
            kind, b, h = units[u]
            if kind == "fox":
                return O_FOX + 2 * h + b // 4, b % 4 == 0, b % 4 == 3
            if kind == "swa":
                return O_SWA + b, True, True
            return O_DSA + b, h == 0, h == HEADS - 1

        def group_out(u, y):
            kind, b, h = units[u]
            g, _, _ = group_of(u)
            bank = ps[:, 2 + g % 2, :]
            if kind == "fox":
                pp = slice((h % 2) * HD, (h % 2 + 1) * HD)
                c0 = (b // 4) * HALF
                return y[pp, h // 2, c0:c0 + HALF], bank[pp, :]
            return y[:, :, b * P:(b + 1) * P], bank[:, 0:BT * P].rearrange("p (c n) -> p c n", c=BT)

        def window_cols(ap, b):
            v = ap.rearrange("p (h n) -> p h n", h=HEADS)
            return v[:, :, P:2 * P] if b == 0 else v

        def logits_ps(u):
            return ps[:, 4 + 2 * (u % 2):6 + 2 * (u % 2), :].rearrange("p a n -> p (a n)")

        def z_dest(T, half):
            c = slice(half * HALF, (half + 1) * HALF)
            if T < T_CONV:
                return z[:, T, c], 1.0
            if T < T_FOX:
                j = T - T_CONV
                return z[:, (0, 1, 2, 3, 0, 2)[j], c], 1.0
            if T < T_SWA:
                j = T - T_FOX
            elif T < T_AFS:
                j = T - T_SWA
            elif T < T_GD:
                j = T - T_DSA
            else:
                return z[:, T - T_WO, c], 1.0
            return z[:, j, c], HD ** -0.5 if j < 2 else 1.0

        def w_slot(T):
            return T % 2

        def gate_tiles(T):
            return T_AFS <= T < T_DSA or T_GD <= T < T_WO

        def width(T):
            return GT if gate_tiles(T) else D

        branch_buf = {"A": 0, "F": 1, "S": 0, "D": 1}
        afs = [("A", T_AFS), ("F", T_AFS + KT), ("S", T_AFS + 2 * KT)]

        block = ctx.enter_context(nc.Block())

        @block.sync
        def _(sp):
            sp.dma_start(col_pack[:, :], cols).then_inc(s_pack, 16)
            sp.dma_start(head_pack[:, :], per_head).then_inc(s_pack, 16)
            sp.dma_start(const[:, :, :], consts).then_inc(s_pack, 16)
            for t in range(TT):
                sp.dma_start(xs[:, t], x[t * P:(t + 1) * P, :]).then_inc(s_x, 16)
            sp.dma_start(raw_v, w_v).then_inc(s_rawv, 16)

            def ada_load(n, chunk, k):
                if n >= 3:
                    sp.wait_ge(s_ada_used, n - 2)
                sp.dma_start(ada_raw[n % 3], w_ada[chunk, k]).then_inc(s_ada[n % 3], 16)

            def tile_load(T, src, i=0, step=0):
                if T >= 2:
                    sp.wait_ge(s_w_lo, T - 1 + i * step)
                sp.dma_start(raw[:, T % 2, 0:src.shape[-1]], src).then_inc(s_raw[T % 2], 16)

            for k in range(KT):
                for chunk in range(2):
                    ada_load(2 * k + chunk, chunk, k)
            for T in range(T_AFS):
                tile_load(T, w_z[T])
                if T == T_CONV:
                    sp.wait_ge(s_h, 2 * TT)
                    sp.dma_start(region_d[:, :], window_bias).then_inc(s_table, 16)
            with sp.Fori(0, 3 * KT // 2) as i:
                for j in range(2):
                    tile_load(T_AFS + j, w_gates[i * 2 + j], i, 2)
            tile_load(T_DSA, w_z[T_AFS])
            tile_load(T_DSA + 1, w_z[T_AFS + 1])
            for dt in range(KT):
                sp.wait_ge(s_mix, MIX0 + 2 * (2 * KT + dt + 1))
                sp.dma_start(mix_dram[:, dt, :], z[:, dt]).then_inc(s_spill, 16)
            sp.dma_start(region_d[:, :], distance).then_inc(s_table, 16)
            tile_load(T_DSA + 2, w_z[T_AFS + 2])
            for j in range(2):
                tile_load(T_GD + j, w_gates[3 * KT + j])
            sp.wait_ge(s_of, O_DSA + TT)
            sp.wait_ge(s_spill, 16 * KT)
            for dt in range(KT):
                sp.dma_start(z[:, dt], mix_dram[:, dt, :]).then_inc(s_refill, 16)
            for k in range(KT):
                for j in range(4):
                    ada_load(2 * KT + 4 * k + j, 2 + j, k)
                T = T_GD + 2 + k
                tile_load(T, w_gates[3 * KT + T - T_GD] if T < T_WO else w_o[T - T_WO])
            sp.wait_ge(s_ada_used, 6 * KT)
            for j in range(2):
                sp.dma_start(ada_raw[1 + j], rows[j:j + 1, :].partition_broadcast(P)).then_inc(s_rows, 16)
                sp.dma_start(g_row[j], rows[2 + j:3 + j, :].partition_broadcast(P)).then_inc(s_rows, 16)
            for dt in range(2, 4):
                tile_load(T_WO + dt, w_o[dt])
            sp.wait_ge(s_mod, 4)
            for t in range(TT):
                sp.dma_start(x1[:, t], x[t * P:(t + 1) * P, :]).then_inc(s_x, 16)
            for dt in range(4, KT):
                tile_load(T_WO + dt, w_o[dt])
            with sp.Fori(0, FG) as i:
                for j in range(6):
                    tile_load(T_FFN + j, w_ffn[i * 6 + j], i, 6)
            for t in range(TT):
                sp.wait_ge(s_final, t + 1)
                sp.dma_start(out[t * P:(t + 1) * P, :], x1[:, t]).then_inc(s_out, 16)
            sp.wait_ge(s_out, 16 * TT)

        @block.tensor
        def _(pe):
            def product(o, a_hi, a_lo, m_hi, m_lo, first, last):
                pe.matmul(o, a_hi, m_hi, start=first, stop=False)
                pe.matmul(o, a_hi, m_lo, start=False, stop=False)
                return pe.matmul(o, a_lo, m_hi, start=False, stop=last)

            def tile_half(o, slot, half, k0=0, n=KT, m_hi=h_hi, m_lo=h_lo):
                for k in range(n):
                    w = slice((k0 + k) * P, (k0 + k + 1) * P)
                    c = slice(half * HALF, (half + 1) * HALF)
                    mm = product(o, w_t[:, slot, 0, w], w_t[:, slot, 1, w], m_hi[:, k, c], m_lo[:, k, c],
                                 k == 0, k == n - 1)
                return mm

            def norm_t(t, src, count):
                pe.wait_ge(s_diag, count + 1)
                if count >= 2:
                    pe.wait_ge(s_hval, 2 * (count - 1))
                for k in range(KT):
                    mm = pe.matmul(ps[:, 2 * (t % 2) + k // 4, (k % 4) * P:(k % 4 + 1) * P],
                                   src[:, k * P:(k + 1) * P], diag[:, count % 2, :], start=True, stop=True)
                mm.then_inc(s_ht, 1)

            pe.wait_ge(s_pack, 48)
            pe.wait_ge(s_ada_used, 2 * KT)
            for c in range(2):
                for k in range(KT):
                    mm = pe.matmul(ps[:, 5, c * KT + k:c * KT + k + 1], ada_sum1[:, c, k * P:(k + 1) * P],
                                   ones[:, 0:1], start=True, stop=True)
            mm.then_inc(s_mod, 1)

            def token_major(t):
                pe.wait_ge(s_h, 2 * (t + 1))
                if t >= 2:
                    pe.wait_ge(s_vn, t - 1)
                c = slice(t * P, (t + 1) * P)
                for k in range(KT):
                    mm = product(ps[:, 4 + t % 2, 0:VN], h_hi[:, k, c], h_lo[:, k, c], vw_hi[:, k, :],
                                 vw_lo[:, k, :], k == 0, k == KT - 1)
                mm.then_inc(s_v, 1)

            pe.wait_ge(s_x, 16 * TT)
            for t in range(2):
                norm_t(t, xs[:, t], t)
            pe.wait_ge(s_vw_lo, 1)
            pe.wait_ge(s_mod, 2)
            for t in range(2, TT):
                norm_t(t, xs[:, t], t)
                token_major(t - 2)
            token_major(TT - 2)
            token_major(TT - 1)

            def z_group(T0, n):
                for T in range(T0, T0 + n):
                    pe.wait_ge(s_w_lo, T + 1)
                    for half in range(2):
                        e = 2 * T + half
                        if e >= 2:
                            pe.wait_ge(s_zf, e - 1)
                        tile_half(ps[:, half, :], T % 2, half).then_inc(s_z, 1)

            pe.wait_ge(s_hval, 2 * TT)
            z_group(T_IDX, T_CONV - T_IDX)
            pe.wait_ge(s_zf, 2 * T_CONV)
            pe.wait_ge(s_vn, TT)
            r = 0
            for b in range(KB0, TT):
                for h in range(HEADS):
                    if r >= 2:
                        pe.wait_ge(s_relu, r - 1)
                    pp = slice((h % 2) * HD, (h % 2 + 1) * HD)
                    for c0 in range(0, (b + 1) * P, HALF):
                        c1 = min(c0 + HALF, (b + 1) * P)
                        mm = pe.matmul(logits_ps(r)[:, c0:c1], z[pp, h // 2, b * P:(b + 1) * P], z[pp, 2, c0:c1],
                                       start=True, stop=True)
                    mm.then_inc(s_s, 1)
                    r += 1
            z_group(T_CONV, T_FOX - T_CONV)
            z_group(T_FOX, T_SWA - T_FOX)

            def forget_sums(h0):
                for j in range(2):
                    pe.wait_ge(s_fu, h0 + j + 1)
                    if h0 == 0:
                        pe.wait_ge(s_relu, r)
                    for c in range(2):
                        mm = pe.matmul(ps[:, 4 + 2 * j + c, :], minus, lg[j][:, c * HALF:(c + 1) * HALF],
                                       start=True, stop=True)
                    mm.then_inc(s_fp, 1)

            def logits(u):
                kind, b, h = units[u]
                if u >= 2:
                    pe.wait_ge(s_lg, u - 1)
                o = logits_ps(u)
                q = slice(b * P, (b + 1) * P)
                if kind == "swa":
                    for hh in range(HEADS):
                        pp = slice((hh // 2) * HD, (hh // 2 + 1) * HD)
                        c0 = 0 if b else P
                        mm = pe.matmul(o[:, hh * 2 * P + c0:(hh + 1) * 2 * P], z[pp, hh % 2, q],
                                       z[pp, 2, (b - 1) * P + c0:(b + 1) * P], start=True, stop=True)
                else:
                    pp = slice((h % 2) * HD, (h % 2 + 1) * HD)
                    key = z[pp, 2 + h // 2] if kind == "fox" else z[pp, 2]
                    masked = kind == "fox" or b < KB0
                    for c0 in range(0, (b + 1) * P, HALF):
                        c1 = min(c0 + HALF, (b + 1) * P)
                        here = masked and c1 == (b + 1) * P
                        mm = pe.matmul(o[:, c0:c1], z[pp, h // 2, q], key[:, c0:c1], start=True, stop=True)
                        if here:
                            mm = pe.matmul(o[:, q], ident_b[:, :], tri_b[:, :], start=False, stop=True,
                                           skip_group_check=True)
                mm.then_inc(s_logit, 1)

            def turn(u):
                kind, b, h = units[u]
                pe.wait_ge(s_prob, u + 1)
                if u >= 1:
                    pe.wait_ge(s_pt, u)
                blocks = [2 * hh + c for hh in range(HEADS) for c in ((0, 1) if b else (1,))] \
                    if kind == "swa" else range(b + 1)
                for c in blocks:
                    mm = pe.transpose(ps[:, c // 4, (c % 4) * P:(c % 4 + 1) * P],
                                      lg[u % 2][:, c * P:(c + 1) * P], ident)
                mm.then_inc(s_t, 1)

            def values(u):
                kind, b, h = units[u]
                g, first, last = group_of(u)
                pe.wait_ge(s_pt, u + 1)
                if first and g >= 2:
                    pe.wait_ge(s_of, g - 1)
                bank = ps[:, 2 + g % 2, :]
                if kind == "swa":
                    for hh in range(HEADS):
                        kv, tau = hh // 2, hh % 2
                        cs = (0, 1) if b else (1,)
                        for c in cs:
                            mm = pe.matmul(bank[kv * HD:(kv + 1) * HD, tau * P:(tau + 1) * P],
                                           vn[:, b - 1 + c, VS + kv * HD:VS + (kv + 1) * HD],
                                           pt[u % 2][:, (2 * hh + c) * P:(2 * hh + c + 1) * P],
                                           start=c == cs[0], stop=c == 1)
                else:
                    v0 = VF + h * HD if kind == "fox" else VD
                    at = (b % 4) * P if kind == "fox" else (h // 2) * P
                    for c in range(b + 1):
                        mm = pe.matmul(bank[(h % 2) * HD:(h % 2 + 1) * HD, at:at + P], vn[:, c, v0:v0 + HD],
                                       pt[u % 2][:, c * P:(c + 1) * P], start=c == 0, stop=c == b)
                mm.then_inc(s_pv, 1)

            def attention(u0, n):
                logits(u0)
                logits(u0 + 1)
                for u in range(u0, u0 + n):
                    turn(u)
                    if u + 2 < u0 + n:
                        logits(u + 2)
                    if u > u0:
                        values(u - 1)
                values(u0 + n - 1)

            forget_sums(0)
            pe.wait_ge(s_forget, 2)
            pe.wait_ge(s_zf, 2 * T_SWA)
            attention(U_FOX, 2 * TT)
            forget_sums(2)
            pe.wait_ge(s_forget, 4)
            attention(U_FOX + 2 * TT, 2 * TT)
            pe.wait_ge(s_pt, U_SWA)
            z_group(T_SWA, T_AFS - T_SWA)
            pe.wait_ge(s_zf, 2 * T_AFS)
            attention(U_SWA, TT)
            pe.wait_ge(s_pt, U_DSA)
            pe.wait_ge(s_of, O_DSA)

            def gate_pairs(T0, buf):
                with pe.Fori(0, KT // 2) as i:
                    for j in range(2):
                        pe.wait_ge(s_w_lo, i * 2 + (T0 + j + 1))
                        for half in range(2):
                            pe.wait_ge(s_zf, i * 4 + (2 * (T0 + j) + half - 1))
                            slot = (T0 + j) % 2
                            tile_half(ps[:, half, :], slot, half)
                            tile_half(ps[:, 2 + half, :], slot, half, KT, BT, y_hi(buf), y_lo(buf)) \
                                .then_inc(s_z, 1)

            pe.wait_ge(s_ya, BT)
            gate_pairs(T_AFS, 0)
            gate_pairs(T_AFS + KT, 1)
            pe.wait_ge(s_ys, 1)
            gate_pairs(T_AFS + 2 * KT, 0)
            z_group(T_DSA, T_GD - T_DSA)
            pe.wait_ge(s_zf, 2 * T_GD)
            attention(U_DSA, HEADS * TT)
            pe.wait_ge(s_pt, U_DSA + HEADS * TT)
            pe.wait_ge(s_of, O_DSA + TT)
            gate_pairs(T_GD, 1)

            pe.wait_ge(s_ada_used, 6 * KT)
            for j, chunk in ((0, 0), (1, 3)):
                for c in range(2):
                    mm = pe.matmul(ps[:, 4 + 2 * j + c, :], ones, ada_sum2[:, chunk, c * HALF:(c + 1) * HALF],
                                   start=True, stop=True)
            pe.wait_ge(s_zf, 2 * T_WO)
            for c in range(2):
                for k in range(KT):
                    mm = pe.matmul(ps[:, 3, c * KT + k:c * KT + k + 1], ada_sum2[:, 1 + c, k * P:(k + 1) * P],
                                   ones[:, 0:1], start=True, stop=True)
            mm.then_inc(s_mod, 1)

            pe.wait_ge(s_mix_lo, KT)
            z_group(T_WO, KT)
            pe.wait_ge(s_zf, 2 * T_FFN)
            pe.wait_ge(s_mod, 4)

            def turn_o(t):
                if t >= 1:
                    pe.wait_ge(s_x1, t)
                for k in range(KT):
                    mm = pe.transpose(ps[:, 4 + k // 4, (k % 4) * P:(k % 4 + 1) * P],
                                      z[:, k, t * P:(t + 1) * P], ident)
                mm.then_inc(s_ot, 1)

            turn_o(0)
            for t in range(TT):
                if t + 1 < TT:
                    turn_o(t + 1)
                norm_t(t, x1[:, t], TT + t)

            pe.wait_ge(s_h, 4 * TT)
            with pe.Fori(0, FG) as i:
                for j in range(4):
                    f, up = j // 2, j % 2
                    pe.wait_ge(s_w_lo, i * 6 + (T_FFN + j + 1))
                    for half in range(2):
                        if f:
                            pe.wait_ge(s_a if up else s_silu2, i * 4 + (half + 1))
                        mm = tile_half(ps[:, 2 * up + half, :], (T_FFN + j) % 2, half)
                        mm.then_inc(s_z, 1)
                for j in range(2):
                    pe.wait_ge(s_w_lo, i * 6 + (T_FFN + 5 + j))
                for q in range(2 * TT):
                    t, c = q // 2, q % 2
                    if q == 0:
                        pe.wait_ge(s_a_lo, i * 4 + 3)
                    if q == TT:
                        pe.wait_ge(s_a_lo, i * 4 + 4)
                    pe.wait_ge(s_yf, i * 16 + (q + 1))
                    for f in range(2):
                        tok = slice(t * P, (t + 1) * P)
                        cc = slice(c * HALF, (c + 1) * HALF)
                        mm = product(ps[:, 4 + q % 4, :], y_t[:, 0, 0, f, tok], y_t[:, 0, 1, f, tok],
                                     y_t[:, 1, 0, f, cc], y_t[:, 1, 1, f, cc], f == 0, f == 1)
                    mm.then_inc(s_y, 1)

        @block.scalar
        def _(act):
            order = Order(act, act_order)

            def split_hi(T, i=0, step=0, n=None):
                act.wait_ge(s_raw[T % 2], 16 * (T // 2 + 1) + i * (8 * step))
                if T >= 2:
                    act.wait_ge(s_z, 2 * (T - 1) + i * (2 * step))
                n = n or width(T)
                act.activation(w_t[:, T % 2, 0, 0:n], raw[:, T % 2, 0:n], ACT.Copy).then_inc(s_w_hi, 1)

            def z_group(T0, n):
                for T in range(T0, T0 + n):
                    split_hi(T + 1)
                    for half in range(2):
                        act.wait_ge(s_z, 2 * T + half + 1)
                        if T == T_CONV + 4 and half == 0:
                            act.wait_ge(s_prod, 1)
                        if T == T_CONV + 5 and half == 0:
                            act.wait_ge(s_prod, 2)
                        if T == T_FOX and half == 0:
                            act.wait_ge(s_conv, BT)
                        if T == T_DSA and half == 0:
                            act.wait_ge(s_spill, 16 * KT)
                        dst, scale = z_dest(T, half)
                        act.activation(dst, ps[:, half, :], ACT.Copy, scale=scale).then_inc(s_zf, 1)

            def h_hi_part(v):
                act.wait_ge(s_hval, v + 1)
                t, kh = (v // 2) % TT, v % 2
                act.activation(h_hi[:, 4 * kh:4 * kh + 4, t * P:(t + 1) * P],
                               h_tmp[:, kh * HALF:(kh + 1) * HALF].rearrange("p (k n) -> p k n", k=4),
                               ACT.Copy).then_inc(s_h_hi, 1)

            def square_sum(src, col, bank=6):
                order.then_wait(act.activation(ps[:, bank:bank + 2, :].rearrange("p a n -> p (a n)"), src, ACT.Square,
                                               accum_out=stat[:, col:col + 1]))

            def roots(c0, c1, s):
                act.activation(root[:, c0:c1], stat[:, c0:c1], ACT.Sqrt, scale=1.0 / D,
                               bias=eps[:, 0:1]).then_inc(s, 1)

            act.wait_ge(s_pack, 48)
            act.activation(silu_c[:, :], c_col, ACT.Silu).then_inc(s_silu, 1)
            act.wait_ge(s_x, 16 * TT)
            for t in range(TT):
                square_sum(xs[:, t], t)
            act.wait_ge(s_mix, MIX0)
            roots(0, TT, s_root)
            act.wait_ge(s_rawv, 16)
            act.activation(vw_hi, raw_v.rearrange("p (k n) -> p k n", k=KT), ACT.Copy).then_inc(s_vw_hi, 1)

            def v_out(t):
                act.wait_ge(s_v, t + 1)
                act.activation(vn[:, t, :], ps[:, 4 + t % 2, 0:VN], ACT.Copy).then_inc(s_vn, 1)

            for t in range(TT):
                h_hi_part(2 * t)
                h_hi_part(2 * t + 1)
                if t == 1:
                    split_hi(0)
                if t >= 2:
                    v_out(t - 2)
            v_out(TT - 2)
            v_out(TT - 1)
            act.wait_ge(s_fabs, 1)
            order.then_wait(act.activation(lf[:, 1, :], lf[:, 1, :], ACT.Exp, scale=-1.0))
            act.activation(lf[:, 1, :], lf[:, 1, :], ACT.Ln, bias=ones[:, 0:1]).then_inc(s_fln, 1)
            z_group(T_IDX, T_CONV - T_IDX)
            r = 0
            for b in range(KB0, TT):
                for h in range(HEADS):
                    n = (b + 1) * P
                    act.wait_ge(s_s, r + 1)
                    if r >= 2:
                        act.wait_ge(s_score, r - 1)
                    act.activation(lg[r % 2][:, 0:n], logits_ps(r)[:, 0:n], ACT.Relu).then_inc(s_relu, 1)
                    r += 1
            z_group(T_CONV, T_FOX - T_CONV)
            for c in range(BT):
                act.wait_ge(s_conv, c + 1)
                act.activation(y_hi(0)[:, c], pt[c], ACT.Copy).then_inc(s_ya_hi, 1)
            z_group(T_FOX, T_SWA - T_FOX)

            def group_hi(u):
                kind, b, h = units[u]
                g, _, last = group_of(u)
                if not last or kind == "swa":
                    return
                act.wait_ge(s_pv, u + 1)
                dst, src = group_out(u, y_hi(1))
                act.activation(dst, src, ACT.Copy).then_inc(s_o_hi, 1)

            def attention(u0, n):
                for u in range(u0, u0 + n):
                    kind, b, h = units[u]
                    s = u % 2
                    act.wait_ge(s_neg, u + 1)
                    if kind == "swa":
                        w = window_cols(lg[s], b)
                        for hh in range(HEADS):
                            act.activation(w[:, hh], w[:, hh], ACT.Exp, bias=neg[:, s, hh:hh + 1],
                                           accum_out=den[:, s, hh:hh + 1])
                        act.activation(sink_e[:, s, :], sink_e[:, s, :], ACT.Exp).then_inc(s_exp, 1)
                    else:
                        w = lg[s][:, 0:(b + 1) * P]
                        act.activation(w, w, ACT.Exp, bias=neg[:, s, 0:1],
                                       accum_out=den[:, s, 0:1]).then_inc(s_exp, 1)
                    if u >= u0 + 2:
                        group_hi(u - 2)
                    act.wait_ge(s_t, u + 1)
                    if u >= u0 + 2:
                        act.wait_ge(s_pv, u - 1)
                    bank = ps[:, 0:2, :].rearrange("p a n -> p (a n)")
                    if kind == "swa":
                        dst, src = window_cols(pt[s], b), window_cols(bank, b)
                    else:
                        dst, src = pt[s][:, 0:(b + 1) * P], bank[:, 0:(b + 1) * P]
                    act.activation(dst, src, ACT.Copy).then_inc(s_pt, 1)
                group_hi(u0 + n - 2)
                group_hi(u0 + n - 1)

            attention(U_FOX, 2 * TT)
            attention(U_FOX + 2 * TT, 2 * TT)
            z_group(T_SWA, T_AFS - T_SWA)
            attention(U_SWA, TT)

            def gate_pairs(T0, m0):
                with act.Fori(0, KT // 2) as i:
                    for j in range(2):
                        T = T0 + j
                        split_hi(T + 1, i, 2, GT)
                        for half in range(2):
                            act.wait_ge(s_z, i * 4 + (2 * T + half + 1))
                            act.wait_ge(s_mix, i * 4 + (MIX0 + m0 + 2 * j + half))
                            act.activation(sig, ps[:, half, :], ACT.Sigmoid)
                            act.activation(prj, ps[:, 2 + half, :], ACT.Copy).then_inc(s_zf, 1)

            gate_pairs(T_AFS, 0)
            act.activation(y_hi(0), y_s, ACT.Copy).then_inc(s_ys_hi, 1)
            gate_pairs(T_AFS + KT, 2 * KT)
            gate_pairs(T_AFS + 2 * KT, 4 * KT)
            z_group(T_DSA, T_GD - T_DSA)
            attention(U_DSA, HEADS * TT)
            gate_pairs(T_GD, 6 * KT)
            act.wait_ge(s_mix, MIX0 + 8 * KT)
            for dt in range(KT):
                act.activation(h_hi[:, dt], z[:, dt], ACT.Copy).then_inc(s_mix_hi, 1)
            z_group(T_WO, KT)
            act.wait_ge(s_x, 32 * TT)
            for t in range(TT + 1):
                if t < TT:
                    act.wait_ge(s_ot, t + 1)
                    square_sum(ps[:, 4:6, :].rearrange("p a n -> p (a n)"), TT + t)
                    roots(TT + t, TT + t + 1, s_oroot)
                    act.wait_ge(s_x1, t + 1)
                    square_sum(x1[:, t], 2 * TT + t)
                    roots(2 * TT + t, 2 * TT + t + 1, s_root)
                if t >= 1:
                    h_hi_part(2 * (TT + t - 1))
                    h_hi_part(2 * (TT + t - 1) + 1)

            def ffn_group(i, last):
                def split(j):
                    T = T_FFN + j
                    act.wait_ge(s_raw[T % 2], 16 * (T // 2 + 1) + i * 48)
                    if j in (4, 5):
                        act.wait_ge(s_z, i * 8 + (2 * T_FFN + 1))
                        dst = y_hi(1)[:, j - 4, :]
                    else:
                        done = {0: -2, 1: 0, 2: 2, 3: 4, 6: 6}[j]
                        act.wait_ge(s_z, i * 8 + (2 * T_FFN + done))
                        dst = w_t[:, T % 2, 0, 0:D]
                    act.activation(dst, raw[:, T % 2, 0:D], ACT.Copy).then_inc(s_w_hi, 1)

                for j in range(6):
                    if j < 5 or not last:
                        split(j + 1)
                    f, up = j // 2, j % 2
                    for half in range(2) if j < 4 else ():
                        n = 2 * f + half
                        c = slice(half * HALF, (half + 1) * HALF)
                        if up:
                            act.wait_ge(s_a, i * 4 + (n + 1))
                            act.activation(y_hi(0)[:, f, c], act2[half], ACT.Copy).then_inc(s_a_hi, 1)
                        else:
                            act.wait_ge(s_z, i * 8 + (2 * (T_FFN + j) + half + 1))
                            if f:
                                act.wait_ge(s_a_lo, i * 4 + (half + 1))
                            act.activation(act2[half], ps[:, half, :], ACT.Silu).then_inc(s_silu2, 1)

            with act.Fori(0, FG - 1) as i:
                ffn_group(i, False)
            ffn_group(FG - 1, True)
            for t in range(TT):
                act.wait_ge(s_yf, 4 + 16 * (FG - 1) + 2 * (t + 1))
                square_sum(z[:, t], t, 0)
                roots(t, t + 1, s_yroot)

        @block.gpsimd
        def _(pool):
            order = Order(pool, pool_order)
            pool.memset(eps[:, :], EPS).then_inc(s_mix, 1)

            def split_lo(T, i=0, step=0, n=None):
                n = n or width(T)
                pool.wait_ge(s_w_hi, T + 1 + i * step)
                pool.tensor_tensor(w_t[:, T % 2, 1, 0:n], raw[:, T % 2, 0:n],
                                   w_t[:, T % 2, 0, 0:n].bitcast(F32), ALU.subtract).then_inc(s_w_lo, 1)

            def h_lo_part(v):
                pool.wait_ge(s_h_hi, v + 1)
                t, kh = (v // 2) % TT, v % 2
                at = (slice(None), slice(4 * kh, 4 * kh + 4), slice(t * P, (t + 1) * P))
                pool.tensor_tensor(h_lo[at], h_tmp[:, kh * HALF:(kh + 1) * HALF].rearrange("p (k n) -> p k n", k=4),
                                   h_hi[at].bitcast(F32), ALU.subtract).then_inc(s_h, 1)

            pool.wait_ge(s_vw_hi, 1)
            pool.tensor_tensor(vw_lo, raw_v.rearrange("p (k n) -> p k n", k=KT), vw_hi.bitcast(F32),
                               ALU.subtract).then_inc(s_vw_lo, 1)
            for t in range(TT):
                h_lo_part(2 * t)
                h_lo_part(2 * t + 1)
                if t == 1:
                    split_lo(0)
            for T in range(1, T_AFS + 1):
                split_lo(T)

            def gate_pairs(T0, first):
                with order.loop(KT // 2, 0 if first else 4) as i:
                    for j in range(2):
                        T = T0 + j
                        split_lo(T + 1, i, 2, GT)
                        for half in range(2):
                            c = slice(half * HALF, (half + 1) * HALF)
                            pool.wait_ge(s_zf, i * 4 + (2 * T + half + 1))
                            mix = z[:, i * 2 + j, c]
                            if first:
                                pool.tensor_tensor(mix, sig, prj, ALU.mult).then_inc(s_mix, 1)
                            else:
                                order.then_wait(pool.tensor_tensor(sig, sig, prj, ALU.mult))
                                pool.tensor_tensor(mix, mix, sig, ALU.add).then_inc(s_mix, 1)

            gate_pairs(T_AFS, True)
            pool.wait_ge(s_ys_hi, 1)
            pool.tensor_tensor(y_lo(0), y_s, y_hi(0).bitcast(F32), ALU.subtract).then_inc(s_ys, 1)
            pool.wait_ge(s_mix, MIX0 + 2 * KT)
            gate_pairs(T_AFS + KT, False)
            pool.wait_ge(s_mix, MIX0 + 4 * KT)
            gate_pairs(T_AFS + 2 * KT, False)
            for T in range(T_DSA + 1, T_GD + 1):
                split_lo(T)
            pool.wait_ge(s_refill, 16 * KT)
            gate_pairs(T_GD, False)
            for T in range(T_WO + 1, T_FFN + 1):
                split_lo(T)
            for v in range(2 * TT, 4 * TT):
                h_lo_part(v)
            pool.wait_ge(s_ot, TT)
            for q in range(4):
                pool.memset(region_a[:, q * 2 * L:(q + 1) * 2 * L], 0.0).then_inc(s_yf, 1)

            def ffn_group(i, last):
                def split(j):
                    T = T_FFN + j
                    pool.wait_ge(s_w_hi, i * 6 + (T + 1))
                    if j in (4, 5):
                        hi, lo = y_hi(1)[:, j - 4, :], y_lo(1)[:, j - 4, :]
                    else:
                        hi, lo = w_t[:, T % 2, 0, 0:D], w_t[:, T % 2, 1, 0:D]
                    pool.tensor_tensor(lo, raw[:, T % 2, 0:D], hi.bitcast(F32), ALU.subtract).then_inc(s_w_lo, 1)

                for j in range(6):
                    if j < 5 or not last:
                        split(j + 1)
                    for half in range(2) if j in (1, 3) else ():
                        f = j // 2
                        c = slice(half * HALF, (half + 1) * HALF)
                        pool.wait_ge(s_a_hi, i * 4 + (2 * f + half + 1))
                        pool.tensor_tensor(y_lo(0)[:, f, c], act2[half], y_hi(0)[:, f, c].bitcast(F32),
                                           ALU.subtract).then_inc(s_a_lo, 1)

            with pool.Fori(0, FG - 1) as i:
                ffn_group(i, False)
            ffn_group(FG - 1, True)

        @block.vector
        def _(dve):
            order = Order(dve, dve_order)
            dve.wait_ge(s_pack, 48)
            dve.tensor_copy(ident_b[:, :], ident)
            order.mark(dve.tensor_copy(tri_b[:, :], tri))

            def ada(n, k, dst):
                dve.wait_ge(s_ada[n % 3], 16 * (n // 3 + 1))
                src, s = ada_raw[n % 3], silu_c[:, k:k + 1]
                if k == 0:
                    ins = dve.tensor_scalar(dst, src, s, None, ALU.mult)
                else:
                    dve.wait_ge(s_ada_used, n - (1 if n < 2 * KT else 3))
                    ins = dve.scalar_tensor_tensor(dst, src, s, dst, ALU.mult, ALU.add)
                ins.then_inc(s_ada_used, 1)

            dve.wait_ge(s_silu, 1)
            for k in range(KT):
                for chunk in range(2):
                    ada(2 * k + chunk, k, ada_sum1[:, chunk])

            def mod_columns(at, i, g):
                dve.tensor_tensor(mod_col[:, i, :], at[:, 0:KT], bias_col[i], ALU.add)
                order.then_wait(dve.tensor_tensor(mod_col[:, i + 1, :], at[:, KT:2 * KT], bias_col[i + 1], ALU.add))
                return dve.scalar_tensor_tensor(mod_col[:, i + 1, :], mod_col[:, i + 1, :], 1.0, g, ALU.add, ALU.mult)

            dve.wait_ge(s_mod, 1)
            mod_columns(ps[:, 5, :], 0, g0_col).then_inc(s_mod, 1)
            dve.wait_ge(s_mod, 2)
            dve.wait_ge(s_root, 1)
            order.then_wait(dve.reciprocal(rstd[:, 0:TT], root[:, 0:TT]))

            def make_diag(count, col):
                if count >= 2:
                    dve.wait_ge(s_ht, count - 1)
                dve.tensor_scalar(diag[:, count % 2, :], ident, rstd[:, col:col + 1], None, ALU.mult) \
                   .then_inc(s_diag, 1)

            def h_values(count, i):
                dve.wait_ge(s_ht, count + 1)
                for kh in range(2):
                    v = 2 * count + kh
                    if v >= 2:
                        dve.wait_ge(s_h, v - 1)
                    for k in range(4):
                        kk = 4 * kh + k
                        ins = dve.tensor_scalar(h_tmp[:, kk * P:(kk + 1) * P],
                                                ps[:, 2 * (count % 2) + kh, k * P:(k + 1) * P],
                                                mod_col[:, i + 1, kk:kk + 1], mod_col[:, i, kk:kk + 1],
                                                ALU.mult, ALU.add)
                    ins.then_inc(s_hval, 1)

            make_diag(0, 0)
            make_diag(1, 1)
            for t in range(TT):
                h_values(t, 0)
                if t + 2 < TT:
                    make_diag(t + 2, t + 2)

            dve.wait_ge(s_vn, TT)
            f3, fa, fe = (lf[:, i, :].rearrange("p (t h) -> p t h", t=TT) for i in (0, 1, 2))
            order.then_wait(dve.tensor_tensor(f3, vn[:, :, VFF:VFF + HEADS],
                                              fox_b.unsqueeze(1).broadcast_to((P, TT, HEADS)), ALU.add))
            dve.scalar_tensor_tensor(lf[:, 1, :], lf[:, 0, :], -1.0, lf[:, 0, :], ALU.mult, ALU.max) \
               .then_inc(s_fabs, 1)
            dve.wait_ge(s_fln, 1)
            order.then_wait(dve.scalar_tensor_tensor(lf[:, 2, :], lf[:, 0, :], 0.0, lf[:, 1, :], ALU.min,
                                                     ALU.subtract))

            r = 0
            for b in range(KB0, TT):
                n = (b + 1) * P
                for h in range(HEADS):
                    dve.wait_ge(s_relu, r + 1)
                    w = vn[:, b, VWI + h:VWI + h + 1]
                    if h == 0:
                        ins = dve.tensor_scalar(sc_at[b], lg[r % 2][:, 0:n], w, None, ALU.mult)
                    else:
                        dve.wait_ge(s_score, r)
                        ins = dve.scalar_tensor_tensor(sc_at[b], lg[r % 2][:, 0:n], w, sc_at[b], ALU.mult, ALU.add)
                    ins.then_inc(s_score, 1)
                    r += 1
                dve.wait_ge(s_score, r)
                order.mark(dve.tensor_tensor(sc_at[b][:, b * P:n], sc_at[b][:, b * P:n], tri, ALU.add))

            order.mark(dve.memset(conv_z[:, 0:2], 0.0))
            for c in range(BT):
                dve.wait_ge(s_zf, 2 * (T_CONV + 2 * c + 2))
                dve.tensor_tensor(conv_z[:, 2:L + 2], z[:, 2 * c], z[:, 2 * c + 1], ALU.mult).then_inc(s_prod, 1)
                dve.wait_ge(s_prod, c + 1)
                order.wait()
                order.then_wait(dve.tensor_scalar(pt[c], conv_z[:, 0:L], conv_w[:, c, 0:1], None, ALU.mult))
                for k in (1, 2):
                    order.then_wait(dve.scalar_tensor_tensor(pt[c], conv_z[:, k:L + k], conv_w[:, c, k:k + 1],
                                                             pt[c], ALU.mult, ALU.add))
            for c in range(BT):
                dve.wait_ge(s_zf, 2 * (T_CONV + 5 + c))
                dve.tensor_tensor(pt[c], pt[c], z[:, 2 * c], ALU.mult).then_inc(s_conv, 1)
            for c in range(BT):
                dve.wait_ge(s_conv, c + 1)
                dve.wait_ge(s_ya_hi, c + 1)
                dve.tensor_tensor(y_lo(0)[:, c], pt[c], y_hi(0)[:, c].bitcast(F32), ALU.subtract).then_inc(s_ya, 1)

            def forget_sums(h0):
                for j in range(2):
                    spread = lg[j].rearrange("p (t n) -> p t n", t=TT)
                    dve.tensor_tensor(spread, upper.unsqueeze(1).broadcast_to((P, TT, P)),
                                      fe[:, :, h0 + j:h0 + j + 1].broadcast_to((P, TT, P)), ALU.mult) \
                       .then_inc(s_fu, 1)
                for j in range(2):
                    dve.wait_ge(s_fp, h0 + j + 1)
                    for b in range(TT):
                        src = ps[:, 4 + 2 * j + b // 4, (b % 4) * P:(b % 4 + 1) * P]
                        dst = forget[:, j, b * P:(b + 1) * P]
                        if b == 0:
                            ins = dve.tensor_copy(dst, src)
                        else:
                            ins = dve.tensor_scalar(dst, src, forget[:, j, b * P - 1:b * P], None, ALU.add)
                        if b < TT - 1:
                            order.then_wait(ins)
                    ins.then_inc(s_forget, 1)
                dve.wait_ge(s_forget, h0 + 2)

            def dsa_bias(u):
                _, b, h = units[u]
                n = (b + 1) * P
                slope = 2.0 ** -(HEADS + 1 + h)
                dist = region_d[:, L - n:L]
                if b < KB0:
                    order.mark(dve.tensor_scalar(spare[:, 0:n], dist, slope, None, ALU.mult))
                else:
                    order.mark(dve.scalar_tensor_tensor(spare[:, 0:n], dist, slope, sc_at[b], ALU.mult, ALU.add))

            def group_lo(u):
                kind, b, h = units[u]
                g, _, last = group_of(u)
                if not last:
                    return
                if kind == "swa":
                    dve.wait_ge(s_pv, u + 1)
                    dst, src = group_out(u, y_s)
                    dve.tensor_copy(dst, src).then_inc(s_of, 1)
                else:
                    dve.wait_ge(s_o_hi, (g if kind == "fox" else g - TT) + 1)
                    dst, src = group_out(u, y_lo(1))
                    hi, _ = group_out(u, y_hi(1))
                    dve.tensor_tensor(dst, src, hi.bitcast(F32), ALU.subtract).then_inc(s_of, 1)

            def attention(u0, n):
                if units[u0][0] == "dsa":
                    dsa_bias(u0)
                for u in range(u0, u0 + n):
                    kind, b, h = units[u]
                    s, w = u % 2, (b + 1) * P
                    o = logits_ps(u)
                    dve.wait_ge(s_logit, u + 1)
                    if u >= 2:
                        dve.wait_ge(s_t, u - 1)
                    if kind == "swa":
                        for hh in range(HEADS):
                            ins = dve.tensor_tensor_reduce(
                                window_cols(lg[s], b)[:, hh], window_cols(o, b)[:, hh],
                                window_cols(region_d[:, :], b)[:, hh], 1.0, TAKEN, ALU.add, ALU.max,
                                mx[:, s, hh:hh + 1])
                        ins.then_inc(s_lg, 1)
                        dve.wait_ge(s_lg, u + 1)
                        order.then_wait(dve.tensor_tensor(mx[:, s, :], mx[:, s, :], sinks, ALU.max))
                        order.then_wait(dve.tensor_scalar(neg[:, s, :], mx[:, s, :], -1.0, None, ALU.mult))
                        dve.tensor_tensor(sink_e[:, s, :], sinks, neg[:, s, :], ALU.add).then_inc(s_neg, 1)
                    else:
                        if kind == "dsa":
                            order.wait()
                            bias = spare[:, 0:w]
                        else:
                            bias = forget[:, h % 2, 0:w]
                        dve.tensor_tensor_reduce(lg[s][:, 0:w], o[:, 0:w], bias, 1.0, TAKEN, ALU.add, ALU.max,
                                                 mx[:, s, 0:1]).then_inc(s_lg, 1)
                        dve.wait_ge(s_lg, u + 1)
                        dve.tensor_scalar(neg[:, s, 0:1], mx[:, s, 0:1], -1.0, None, ALU.mult).then_inc(s_neg, 1)
                        if kind == "dsa" and u + 1 < u0 + n:
                            dsa_bias(u + 1)
                    dve.wait_ge(s_exp, u + 1)
                    if kind == "swa":
                        order.then_wait(dve.tensor_tensor(den[:, s, :], den[:, s, :], sink_e[:, s, :], ALU.add))
                        order.then_wait(dve.reciprocal(rec[:, s, :], den[:, s, :]))
                        p = window_cols(lg[s], b)
                        dve.tensor_tensor(p, p, rec[:, s, :].unsqueeze(2).broadcast_to((P, HEADS, p.shape[2])),
                                          ALU.mult).then_inc(s_prob, 1)
                    else:
                        order.then_wait(dve.reciprocal(rec[:, s, 0:1], den[:, s, 0:1]))
                        p = lg[s][:, 0:w]
                        dve.tensor_scalar(p, p, rec[:, s, 0:1], None, ALU.mult).then_inc(s_prob, 1)
                    if u >= u0 + 2:
                        group_lo(u - 2)
                group_lo(u0 + n - 2)
                group_lo(u0 + n - 1)

            forget_sums(0)
            attention(U_FOX, 2 * TT)
            dve.wait_ge(s_t, 2 * TT)
            forget_sums(2)
            attention(U_FOX + 2 * TT, 2 * TT)
            dve.wait_ge(s_table, 16)
            attention(U_SWA, TT)

            order.wait()
            for b in range(KB0, TT):
                with dve.Fori(0, TOPK // 8):
                    dve.max(top8[:, :], sc_at[b])
                    dve.drain()
                    dve.match_replace(sc_at[b], top8[:, :], sc_at[b], TAKEN)
                    dve.drain()
                order.mark(dve.tensor_scalar(sc_at[b], sc_at[b], TAKEN / 2, -BIG, ALU.is_gt, ALU.mult))
            order.wait()
            dve.wait_ge(s_table, 32)
            attention(U_DSA, HEADS * TT)

            for k in range(KT):
                for j in range(4):
                    ada(2 * KT + 4 * k + j, k, ada_sum2[:, j])
            for dt in range(KT):
                dve.wait_ge(s_mix_hi, dt + 1)
                dve.tensor_tensor(h_lo[:, dt], z[:, dt], h_hi[:, dt].bitcast(F32), ALU.subtract).then_inc(s_mix_lo, 1)
            dve.wait_ge(s_rows, 64)
            dve.wait_ge(s_mod, 3)
            for j in range(2):
                sums = ps[:, 4 + 2 * j:6 + 2 * j, :].rearrange("p a n -> p (a n)")
                order.then_wait(dve.tensor_tensor(ada_raw[1 + j], sums, ada_raw[1 + j], ALU.add))
                order.mark(dve.tensor_tensor(g_row[j], ada_raw[1 + j], g_row[j], ALU.mult))
            mod_columns(ps[:, 3, :], 2, g2_col).then_inc(s_mod, 1)
            dve.wait_ge(s_mod, 4)
            dve.wait_ge(s_x, 32 * TT)
            o = ps[:, 4:6, :].rearrange("p a n -> p (a n)")
            for t in range(TT + 1):
                if t < TT:
                    dve.wait_ge(s_oroot, t + 1)
                    c = TT + t
                    order.then_wait(dve.reciprocal(rstd[:, c:c + 1], root[:, c:c + 1]))
                    order.then_wait(dve.scalar_tensor_tensor(o, o, rstd[:, c:c + 1], g_row[0], ALU.mult, ALU.mult))
                    dve.tensor_tensor(x1[:, t], o, x1[:, t], ALU.add).then_inc(s_x1, 1)
                    dve.wait_ge(s_root, 2 + t)
                    c = 2 * TT + t
                    order.then_wait(dve.reciprocal(rstd[:, c:c + 1], root[:, c:c + 1]))
                    make_diag(TT + t, c)
                if t >= 1:
                    h_values(TT + t - 1, 2)

            dve.wait_ge(s_yf, 4)
            with dve.Fori(0, FG) as i:
                for f in range(2):
                    for half in range(2):
                        n = 2 * f + half
                        dve.wait_ge(s_silu2, i * 4 + (n + 1))
                        dve.wait_ge(s_z, i * 8 + (2 * (T_FFN + 2 * f + 1) + half + 1))
                        dve.tensor_tensor(act2[half], ps[:, 2 + half, :], act2[half], ALU.mult).then_inc(s_a, 1)
                for q in range(2 * TT):
                    t, c = q // 2, q % 2
                    dst = z[:, t, c * HALF:(c + 1) * HALF]
                    dve.wait_ge(s_y, i * 16 + (q + 1))
                    dve.tensor_tensor(dst, ps[:, 4 + q % 4, :], dst, ALU.add).then_inc(s_yf, 1)
            dve.wait_ge(s_yf, 4 + 16 * FG)
            for t in range(TT):
                dve.wait_ge(s_yroot, t + 1)
                order.then_wait(dve.reciprocal(rstd[:, t:t + 1], root[:, t:t + 1]))
                order.then_wait(dve.scalar_tensor_tensor(z[:, t], z[:, t], rstd[:, t:t + 1], g_row[1], ALU.mult,
                                                         ALU.mult))
                dve.tensor_tensor(x1[:, t], x1[:, t], z[:, t], ALU.add).then_inc(s_final, 1)


def _host():
    import numpy as np

    i, j = np.arange(P)[:, None], np.arange(P)[None, :]
    f = np.float32
    consts = np.stack([(i == j).astype(f), np.where(j <= i, 0, -BIG).astype(f), (i <= j).astype(f),
                       np.ones((P, P), f), -np.ones((P, P), f)], 1)
    j = np.arange(2 * P)[None, :]
    dist = i - j + P
    window = np.stack([np.where((dist >= 0) & (dist < WINDOW), -(2.0 ** -(h + 1)) * dist, -BIG)
                       for h in range(HEADS)], 1).astype(f).reshape(P, HEADS * 2 * P)
    distance = -(i + (L - P) - np.arange(L)[None, :]).astype(f)
    return consts, window, distance


def kernel(x, c, w_ada, b_ada, norm_g, w_in, conv_w, fox_bias, swa_sinks, w_branch, w_o, w_gate, w_up, w_down):
    import numpy as np
    import concourse.bacc as bacc
    from concourse.bass_utils import run_bass_kernel_spmd

    x, c, w_ada, b_ada, norm_g, w_in, conv_w, fox_bias, swa_sinks, w_branch, w_o, w_gate, w_up, w_down = (
        np.asarray(a) for a in (x, c, w_ada, b_ada, norm_g, w_in, conv_w, fox_bias, swa_sinks, w_branch, w_o,
                                w_gate, w_up, w_down))
    w_in, w_ada, b_ada, norm_g = w_in[0], w_ada[0], b_ada[0], norm_g[0]
    w_branch, w_o, w_gate, w_up, w_down = w_branch[0], w_o[0], w_gate[0], w_up[0], w_down[0]

    sizes = [256, 256, 256, 256, 64, 64, 256, 64, 4, 256, 256, 256, 4, 256, 128, 128, 4 * D]
    at = [sum(sizes[:i]) for i in range(len(sizes))]
    a_u, a_b, a_c, d_q, d_k, d_v, d_qi, d_ki, d_wi, f_q, f_k, f_v, f_f, s_q, s_k, s_v, g = at

    def span(a, n=P):
        return list(range(a, a + n))

    def tile(w, columns):
        return w[:, columns].reshape(-1, P, len(columns)).transpose(1, 0, 2).reshape(P, -1)

    z_cols = [span(d_qi), span(d_qi + P), span(d_ki, HD) * 2]
    for ch in range(2):
        z_cols += [span(a_c + ch * P), span(a_u + ch * P)]
    z_cols += [span(a_b), span(a_b + P)]
    z_cols += [span(f_q), span(f_q + P), span(f_k), span(f_k + P)]
    z_cols += [span(s_q + t * HD, HD) + span(s_q + (t + 2) * HD, HD) for t in range(2)] + [span(s_k)]
    z_cols += [span(d_q), span(d_q + P), span(d_k, HD) * 2]
    w_z = np.stack([tile(w_in, cc) for cc in z_cols])
    w_v = tile(w_in, span(d_v, 64) + span(f_v, 256) + span(s_v, 128) + span(d_wi, 4) + span(f_f, 4))
    gates = []
    for n in (0, 2, 3, 1):
        rows_n = span(0, BW)
        if n == 3:
            rows_n = [r for hh in (0, 2, 1, 3) for r in span(hh * HD, HD)]
        for dt in range(KT):
            gates.append(np.concatenate([tile(w_in, span(g + n * D + dt * P)),
                                         tile(w_branch[n][rows_n], span(dt * P))], 1))
    w_gates = np.stack(gates)
    w_ot = np.stack([tile(w_o, span(dt * P)) for dt in range(KT)])
    ffn = []
    for i in range(FG):
        for f in (2 * i, 2 * i + 1):
            ffn += [tile(w_gate, span(f * P)), tile(w_up, span(f * P))]
        ffn += [w_down[f * P:(f + 1) * P] for f in (2 * i, 2 * i + 1)]
    w_ffn = np.stack(ffn)
    w_adat = w_ada.reshape(KT, P, 6, D).transpose(2, 0, 1, 3)

    def column(v):
        return v.reshape(KT, P).T

    bias = b_ada.reshape(6, D)
    cols = np.concatenate([column(c[0]), column(norm_g[0]), column(norm_g[2]), column(bias[0]), column(bias[1]),
                           column(bias[3]), column(bias[4]),
                           conv_w[0].reshape(3, BT, P).transpose(2, 1, 0).reshape(P, 6)], 1)
    rows = np.stack([bias[2], bias[5], norm_g[1], norm_g[3]])
    per_head = np.broadcast_to(np.concatenate([fox_bias[0], swa_sinks[0]])[None, :], (P, 8))
    consts, window, distance = _host()
    feeds = {"x": x[0], "w_z": w_z, "w_v": w_v, "w_gates": w_gates, "w_o": w_ot, "w_ffn": w_ffn, "w_ada": w_adat,
             "cols": cols, "rows": rows, "per_head": per_head, "consts": consts, "window_bias": window,
             "distance": distance}
    nc = bacc.Bacc("TRN2", target_bir_lowering=False, num_devices=1)
    arrays, args = {}, {}
    for name, a in feeds.items():
        a = np.ascontiguousarray(a)
        arrays[f"in_{name}"] = a
        args[name] = nc.dram_tensor(f"in_{name}", a.shape, mybir.dt.from_np(a.dtype), kind="ExternalInput").ap()
    args["out"] = nc.dram_tensor("out", (L, D), F32, kind="ExternalOutput").ap()
    build(nc, **args)
    r = run_bass_kernel_spmd(nc, [arrays], core_ids=[0])
    return r.results[0]["out"].reshape(1, L, D)
```

```python
from contextlib import ExitStack, contextmanager

import concourse.bass as bass
from concourse import mybir

F32 = mybir.dt.float32
F32R = mybir.dt.float32r
BF16 = mybir.dt.bfloat16
ALU = mybir.AluOpType
ACT = mybir.ActivationFunctionType

P = 128
D = 1024
L = 1024
KT = D // P
TT = L // P
HALF = 512
HD = 64
HEADS = 4
BW = 256
BT = BW // P
FF = -(-8 * D // (3 * 256)) * 256
FT = FF // P
FG = FT // 2
TOPK = min(256, L // 4)
KB0 = TOPK // P
WINDOW = 128
EPS = 1e-6
BIG = 1e30
TAKEN = -3e38

VD, VF, VS, VWI, VFF = 0, 64, 320, 448, 452
VN = 456

T_IDX, T_CONV, T_FOX, T_SWA, T_AFS = 0, 3, 9, 13, 16
T_DSA = T_AFS + 3 * KT
T_GD = T_DSA + 3
T_WO = T_GD + KT
T_FFN = T_WO + KT
GT = (KT + BT) * P

FFN_AT = (0, 1, 3, 5)
FFN_AHEAD = ((1,), (2, 3), (4, 5), (6,))

U_FOX, U_SWA, U_DSA = 0, HEADS * TT, HEADS * TT + TT
O_FOX, O_SWA, O_DSA = 0, 2 * TT, 3 * TT


MIX0 = 1


class Order:

    def __init__(self, eng, sem):
        self.eng, self.sem, self.base, self.k = eng, sem, 0, 0

    def mark(self, ins):
        ins.then_inc(self.sem, 1)
        self.k += 1

    def wait(self):
        self.eng.wait_ge(self.sem, self.base + self.k)

    def then_wait(self, ins):
        self.mark(ins)
        self.wait()

    @contextmanager
    def loop(self, n, per):
        start = self.base + self.k
        with self.eng.Fori(0, n) as i:
            self.base, self.k = start + i * per, 0
            yield i
            assert self.k == per, (self.k, per)
        self.base, self.k = start + n * per, 0


def build(nc, x, w_z, w_v, w_gates, w_o, w_ffn, w_ada, cols, rows, per_head, consts, window_bias, distance, out):
    with ExitStack() as ctx:
        def sb(name, shape, dt=F32):
            return ctx.enter_context(nc.sbuf_tensor(name, shape, dt))

        def sem(name):
            return ctx.enter_context(nc.semaphore(name))

        h_t = sb("h_t", [P, 2, KT, L], F32R)
        w_t = sb("w_t", [P, 2, 2, GT], F32R)
        y_t_at = nc.sbuf_base
        y_t = sb("y_t", [P, 2, 2, BT, L], F32R)
        raw = sb("raw", [P, 2, GT])
        region_a_at = nc.sbuf_base
        region_a = sb("region_a", [P, 8 * L])
        region_b = sb("region_b", [P, 8 * L])
        region_c = sb("region_c", [P, 2 * L])
        region_d = sb("region_d", [P, L])
        col_pack = sb("col_pack", [P, 62])
        head_pack = sb("head_pack", [P, 8])
        const = sb("const", [P, 5, P])
        ident_b = sb("ident_b", [P, P], BF16)
        tri_b = sb("tri_b", [P, P], BF16)
        silu_c = sb("silu_c", [P, KT])
        mod_col = sb("mod_col", [P, 4, KT])
        stat = sb("stat", [P, 3 * TT])
        root = sb("root", [P, 3 * TT])
        rstd = sb("rstd", [P, 3 * TT])
        diag = sb("diag", [P, 2, P])
        top8 = sb("top8", [P, TT - KB0, 8])
        mx = sb("mx", [P, 2, 4])
        neg = sb("neg", [P, 2, 4])
        den = sb("den", [P, 4, 4])
        rec = sb("rec", [P, 2, 4])
        sink_e = sb("sink_e", [P, 4, 4])
        eps = sb("eps", [P, 1])
        lf = sb("lf", [P, 3, TT * HEADS])
        stack_a = nc.alloc_sbuf_tensor_at("stack_a", [P, 4, L], F32R, offset=region_a_at)
        ya_back = nc.alloc_sbuf_tensor_at("ya_back", [P, BT, L], F32, offset=y_t_at + BT * L * 4)
        ps = ctx.enter_context(nc.psum_tensor("ps", [P, 8, HALF], F32))
        ya_dram = nc.dram_tensor("ya_dram", (P, BT, L), F32, kind="Internal").ap()
        mix_dram = nc.dram_tensor("mix_dram", (P, KT, L), F32, kind="Internal").ap()

        ident, tri, upper, ones, minus = (const[:, i, :] for i in range(5))
        c_col, g0_col, g2_col = col_pack[:, 0:8], col_pack[:, 8:16], col_pack[:, 16:24]
        bias_col = [col_pack[:, 24 + 8 * i:32 + 8 * i] for i in range(4)]
        conv_w = col_pack[:, 56:62].rearrange("p (c k) -> p c k", c=2)
        fox_b, sinks = head_pack[:, 0:4], head_pack[:, 4:8]
        h_hi, h_lo = h_t[:, 0], h_t[:, 1]
        xs = region_a[:, :].rearrange("p (t n) -> p t n", t=8)
        z = xs
        lg = [xs[:, 4], xs[:, 5]]
        pt = [xs[:, 6], xs[:, 7]]
        spare = xs[:, 3]
        conv_z = region_a[:, 4 * L:4 * L + L + 2]
        vn = region_b[:, 0:TT * VN].rearrange("p (t n) -> p t n", t=TT)
        sc_at, at = {}, TT * VN
        for b in range(KB0, TT):
            sc_at[b] = region_b[:, at:at + (b + 1) * P]
            at += (b + 1) * P
        y_tok = [region_b[:, at:at + BW], diag[:, :, :].rearrange("p a n -> p (a n)")]
        raw_v = region_b[:, TT * VN:TT * VN + KT * VN]
        ada_raw = [region_b[:, i * D:(i + 1) * D] for i in range(3)]
        ada_sum2 = region_b[:, TT * VN:TT * VN + 4 * D].rearrange("p (c n) -> p c n", c=4)
        x1 = region_b[:, :].rearrange("p (t n) -> p t n", t=8)
        ada_sum1 = region_c[:, :].rearrange("p (c n) -> p c n", c=2)
        forget = ada_sum1
        y_s = region_c[:, :].rearrange("p (c n) -> p c n", c=BT)
        g_row = [region_c[:, 0:L], region_c[:, L:2 * L]]
        h_tmp = region_d[:, :]
        sig = region_d[:, 0:HALF]
        prj = region_d[:, HALF:L]
        act2 = [sig, prj]

        def y_hi(buf):
            return y_t[:, buf, 0]

        def y_lo(buf):
            return y_t[:, buf, 1]

        vw = y_t[:, :, :, :, :].rearrange("p a b c n -> p (a b c n)")
        vw_hi_flat, vw_lo_flat = vw[:, 0:KT * VN], vw[:, 4 * L:4 * L + KT * VN]
        vw_hi, vw_lo = (v.rearrange("p (k n) -> p k n", k=KT) for v in (vw_hi_flat, vw_lo_flat))
        vw_half = [slice(i * KT // 2 * VN, (i + 1) * KT // 2 * VN) for i in range(2)]

        ys = [vw[:, i * L:(i + 1) * L] for i in range(8)]

        stacks = {T_IDX: ("q", (ys[0], ys[1]), region_c[:, 0:L]), T_IDX + 1: ("q", (ys[2], ys[3]), region_c[:, L:2 * L]),
                  T_IDX + 2: ("k", (ys[4],), ys[5]),
                  T_FOX: ("q", (stack_a[:, 0], stack_a[:, 1]), region_d[:, :]),
                  T_FOX + 1: ("q", (stack_a[:, 3], ys[0]), region_d[:, :]),
                  T_FOX + 2: ("kk", (ys[5], ys[7]), stack_a[:, 2]),
                  T_FOX + 3: ("kk", (ys[1], ys[2]), ys[3]),
                  T_DSA: ("q", (ys[0], ys[1]), region_c[:, 0:L]),
                  T_DSA + 1: ("q", (ys[2], ys[3]), region_c[:, L:2 * L]),
                  T_DSA + 2: ("k", (stack_a[:, 0],), stack_a[:, 1])}
        stack_order = sorted(stacks)
        rows_of = [slice(0, HD), slice(HD, P)]

        def lo_halves(T):
            return 2 * sum(t < T for t in stack_order)

        s_pack = sem("s_pack")
        s_rows = sem("s_rows")
        s_xt = [sem(f"s_xt{t}") for t in range(TT)]
        s_x = sem("s_x")
        s_ada = [sem(f"s_ada{i}") for i in range(3)]
        s_ada_used = sem("s_ada_used")
        s_raw = [sem("s_raw0"), sem("s_raw1")]
        s_rawv = sem("s_rawv")
        s_w_hi = sem("s_w_hi")
        s_w_lo = sem("s_w_lo")
        s_vw_hi = sem("s_vw_hi")
        s_vw_lo = sem("s_vw_lo")
        s_silu = sem("s_silu")
        s_mod = sem("s_mod")
        s_root = sem("s_root")
        s_norm = sem("s_norm")
        s_ht = sem("s_ht")
        s_hval = sem("s_hval")
        pool_order = sem("pool_order")
        s_h_hi = sem("s_h_hi")
        s_h = sem("s_h")
        s_v = sem("s_v")
        s_vn = sem("s_vn")
        s_z = sem("s_z")
        s_zf = sem("s_zf")
        s_z_lo = sem("s_z_lo")
        s_moved = {T: sem(f"s_moved{T}") for T in stacks if stacks[T][0] != "k"}
        s_ya_out = sem("s_ya_out")
        s_ya_in = sem("s_ya_in")
        s_s = sem("s_s")
        s_relu = sem("s_relu")
        s_score = sem("s_score")
        s_prod = sem("s_prod")
        s_conv = sem("s_conv")
        s_ya_hi = sem("s_ya_hi")
        s_ya = sem("s_ya")
        s_fabs = sem("s_fabs")
        s_fln = sem("s_fln")
        s_fu = sem("s_fu")
        s_fp = sem("s_fp")
        s_forget = sem("s_forget")
        s_logit = sem("s_logit")
        s_lg = sem("s_lg")
        s_neg = sem("s_neg")
        s_exp = sem("s_exp")
        s_t = sem("s_t")
        s_pt = sem("s_pt")
        s_pv = sem("s_pv")
        s_y_tok = sem("s_y_tok")
        s_turned = sem("s_turned")
        s_o_hi = sem("s_o_hi")
        s_of = sem("s_of")
        s_table = sem("s_table")
        s_ys_hi = sem("s_ys_hi")
        s_ys = sem("s_ys")
        s_mix = sem("s_mix")
        s_spill = sem("s_spill")
        s_refill = sem("s_refill")
        s_mix_hi = sem("s_mix_hi")
        s_mix_lo = sem("s_mix_lo")
        s_ot = sem("s_ot")
        s_oroot = sem("s_oroot")
        s_x1 = sem("s_x1")
        s_silu2 = sem("s_silu2")
        s_a = sem("s_a")
        s_a_hi = sem("s_a_hi")
        s_a_lo = sem("s_a_lo")
        s_y = sem("s_y")
        s_yf = sem("s_yf")
        s_zero = sem("s_zero")
        s_yroot = sem("s_yroot")
        s_y_norm = sem("s_y_norm")
        s_final = sem("s_final")
        s_out = sem("s_out")
        dve_order = sem("dve_order")
        act_order = sem("act_order")

        fox_units = [("fox", b, 2 * pair + j) for pair in range(2) for b in range(TT) for j in range(2)]
        swa_units = [("swa", b, None) for b in range(TT)]
        dsa_units = [("dsa", b, h) for b in range(TT) for h in range(HEADS)]
        units = fox_units + swa_units + dsa_units

        def group_of(u):
            kind, b, h = units[u]
            if kind == "fox":
                return O_FOX + h // 2 * TT + b, h % 2 == 0, h % 2 == 1
            if kind == "swa":
                return O_SWA + b, True, True
            return O_DSA + b, h == 0, h == HEADS - 1

        def group_bank(u):
            return ps[:, 2 + group_of(u)[0] % 2, :]

        def group_turned(u, y):
            kind, b, h = units[u]
            src = group_bank(u)[:, BW:2 * BW].rearrange("p (c n) -> p c n", c=BT)
            q = slice(b * P, (b + 1) * P)
            if kind == "fox":
                return y[:, h // 2, q], src[:, 0]
            return y[:, :, q], src

        def window_cols(ap, b):
            v = ap.rearrange("p (h n) -> p h n", h=HEADS)
            return v[:, :, P:2 * P] if b == 0 else v

        def logits_ps(u):
            return ps[:, 4 + 2 * (u % 2):6 + 2 * (u % 2), :].rearrange("p a n -> p (a n)")

        def z_dest(T, half):
            c = slice(half * HALF, (half + 1) * HALF)
            if T < T_FOX:
                return z[:, (0, 1, 2, 3, 0, 2)[T - T_CONV], c], 1.0
            if T < T_AFS:
                return z[:, T - T_SWA, c], HD ** -0.5 if T < T_SWA + 2 else 1.0
            return z[:, T - T_WO, c], 1.0

        def stack_scale(T):
            return HD ** -0.5 if stacks[T][0] == "q" and T >= T_FOX else 1.0

        def stack_parts(T):
            kind, hi, _ = stacks[T]
            return [(slice(0, P), hi[0])] if kind == "k" else list(zip(rows_of, hi))

        def score_units(n):
            every = [(b, h) for b in range(KB0, TT) for h in range(HEADS)]
            return [(i, *every[i]) for i in range(3 * n, min(3 * n + 3, len(every)))]

        def gate_tiles(T):
            return T_AFS <= T < T_DSA or T_GD <= T < T_WO

        def width(T):
            return GT if gate_tiles(T) else D

        branch_buf = {"A": 0, "F": 1, "S": 0, "D": 1}
        afs = [("A", T_AFS), ("F", T_AFS + KT), ("S", T_AFS + 2 * KT)]

        block = ctx.enter_context(nc.Block())

        @block.sync
        def _(sp):
            sp.dma_start(col_pack[:, :], cols).then_inc(s_pack, 16)
            sp.dma_start(head_pack[:, :], per_head).then_inc(s_pack, 16)
            sp.dma_start(const[:, :, :], consts).then_inc(s_pack, 16)

            def ada_load(n, chunk, k):
                if n >= 3:
                    sp.wait_ge(s_ada_used, n - 2)
                sp.dma_start(ada_raw[n % 3], w_ada[chunk, k]).then_inc(s_ada[n % 3], 16)

            def tile_load(T, src, i=0, step=0):
                if T >= 2:
                    sp.wait_ge(s_w_lo, T - 1 + i * step)
                sp.dma_start(raw[:, T % 2, 0:src.shape[-1]], src).then_inc(s_raw[T % 2], 16)

            def x_load(t):
                sp.dma_start(xs[:, t], x[t * P:(t + 1) * P, :]).then_inc(s_xt[t], 16)

            x_load(0)
            x_load(1)
            for chunk in range(2):
                for k in range(KT):
                    ada_load(chunk * KT + k, chunk, k)
                sp.dma_start(raw_v[:, vw_half[chunk]], w_v[:, vw_half[chunk]]).then_inc(s_rawv, 16)
            for t in range(2, TT):
                x_load(t)
            for T in range(T_AFS):
                tile_load(T, w_z[T])
                if T == T_FOX:
                    for ch in range(BT):
                        sp.wait_ge(s_conv, ch + 1)
                        sp.dma_start(ya_dram[:, ch, :], pt[ch]).then_inc(s_ya_out, 16)
            sp.wait_ge(s_moved[T_FOX + 1], 32)
            sp.dma_start(region_d[:, :], window_bias).then_inc(s_table, 16)
            sp.wait_ge(s_of, O_SWA)
            sp.wait_ge(s_ya_out, 16 * BT)
            for ch in range(BT):
                sp.dma_start(ya_back[:, ch], ya_dram[:, ch, :]).then_inc(s_ya_in, 16)
            with sp.Fori(0, 3 * KT // 2) as i:
                for j in range(2):
                    tile_load(T_AFS + j, w_gates[i * 2 + j], i, 2)
            tile_load(T_DSA, w_z[T_AFS])
            tile_load(T_DSA + 1, w_z[T_AFS + 1])
            for dt in range(KT):
                sp.wait_ge(s_mix, MIX0 + 2 * (2 * KT + dt + 1))
                sp.dma_start(mix_dram[:, dt, :], z[:, dt]).then_inc(s_spill, 16)
            sp.dma_start(region_d[:, :], distance).then_inc(s_table, 16)
            tile_load(T_DSA + 2, w_z[T_AFS + 2])
            for j in range(2):
                tile_load(T_GD + j, w_gates[3 * KT + j])
            sp.wait_ge(s_of, O_DSA + TT)
            sp.wait_ge(s_spill, 16 * KT)
            for dt in range(KT):
                sp.dma_start(z[:, dt], mix_dram[:, dt, :]).then_inc(s_refill, 16)
            for k in range(KT):
                for j in range(4):
                    ada_load(2 * KT + 4 * k + j, 2 + j, k)
                T = T_GD + 2 + k
                tile_load(T, w_gates[3 * KT + T - T_GD] if T < T_WO else w_o[T - T_WO])
            sp.wait_ge(s_ada_used, 6 * KT)
            for j in range(2):
                sp.dma_start(ada_raw[1 + j], rows[j:j + 1, :].partition_broadcast(P)).then_inc(s_rows, 16)
                sp.dma_start(g_row[j], rows[2 + j:3 + j, :].partition_broadcast(P)).then_inc(s_rows, 16)
            for dt in range(2, 4):
                tile_load(T_WO + dt, w_o[dt])
            sp.wait_ge(s_mod, 4)
            for t in range(TT):
                sp.dma_start(x1[:, t], x[t * P:(t + 1) * P, :]).then_inc(s_x, 16)
            for dt in range(4, KT):
                tile_load(T_WO + dt, w_o[dt])
            with sp.Fori(0, FG) as i:
                for j in range(6):
                    tile_load(T_FFN + j, w_ffn[i * 6 + j], i, 6)
            for t in range(TT):
                sp.wait_ge(s_final, t + 1)
                sp.dma_start(out[t * P:(t + 1) * P, :], x1[:, t]).then_inc(s_out, 16)
            sp.wait_ge(s_out, 16 * TT)

        @block.tensor
        def _(pe):
            def product(o, a_hi, a_lo, m_hi, m_lo, first, last):
                pe.matmul(o, a_hi, m_hi, start=first, stop=False)
                pe.matmul(o, a_hi, m_lo, start=False, stop=False)
                return pe.matmul(o, a_lo, m_hi, start=False, stop=last)

            def tile_half(o, slot, half, k0=0, n=KT, m_hi=h_hi, m_lo=h_lo):
                for k in range(n):
                    w = slice((k0 + k) * P, (k0 + k + 1) * P)
                    c = slice(half * HALF, (half + 1) * HALF)
                    mm = product(o, w_t[:, slot, 0, w], w_t[:, slot, 1, w], m_hi[:, k, c], m_lo[:, k, c],
                                 k == 0, k == n - 1)
                return mm

            def turn_x(t):
                pe.wait_ge(s_norm, t + 1)
                if t >= 2:
                    pe.wait_ge(s_hval, 2 * (t - 1))
                for k in range(KT):
                    mm = pe.transpose(ps[:, 2 * (t % 2) + k // 4, (k % 4) * P:(k % 4 + 1) * P],
                                      xs[:, t, k * P:(k + 1) * P], ident)
                mm.then_inc(s_ht, 1)

            def norm_x1(t):
                pe.wait_ge(s_norm, TT + t + 1)
                pe.wait_ge(s_hval, 2 * (TT + t - 1))
                for k in range(KT):
                    mm = pe.matmul(ps[:, 2 * (t % 2) + k // 4, (k % 4) * P:(k % 4 + 1) * P],
                                   x1[:, t, k * P:(k + 1) * P], diag[:, t % 2, :], start=True, stop=True)
                mm.then_inc(s_ht, 1)

            pe.wait_ge(s_pack, 48)
            for t in range(2):
                turn_x(t)
            for c in range(2):
                pe.wait_ge(s_ada_used, (c + 1) * KT)
                for k in range(KT):
                    mm = pe.matmul(ps[:, 5, c * KT + k:c * KT + k + 1], ada_sum1[:, c, k * P:(k + 1) * P],
                                   ones[:, 0:1], start=True, stop=True)
            mm.then_inc(s_mod, 1)

            def token_major(t):
                pe.wait_ge(s_h, 2 * (t + 1))
                if t >= 2:
                    pe.wait_ge(s_vn, t - 1)
                c = slice(t * P, (t + 1) * P)
                for k in range(KT):
                    if t == 0 and k == KT // 2:
                        pe.wait_ge(s_vw_lo, 2)
                    mm = product(ps[:, 4 + t % 2, 0:VN], h_hi[:, k, c], h_lo[:, k, c], vw_hi[:, k, :],
                                 vw_lo[:, k, :], k == 0, k == KT - 1)
                mm.then_inc(s_v, 1)

            pe.wait_ge(s_vw_lo, 1)
            pe.wait_ge(s_mod, 2)
            for t in range(2, TT):
                turn_x(t)
                token_major(t - 2)
            token_major(TT - 2)
            token_major(TT - 1)

            def z_half(T, half):
                e = 2 * T + half
                if half == 0:
                    pe.wait_ge(s_w_lo, T + 1)
                if e >= 2:
                    pe.wait_ge(s_zf, e - 1)
                if T - 1 in stacks:
                    pe.wait_ge(s_z_lo, lo_halves(T - 1) + half + 1)
                tile_half(ps[:, half, :], T % 2, half).then_inc(s_z, 1)

            def z_group(T0, n):
                for T in range(T0, T0 + n):
                    z_half(T, 0)
                    z_half(T, 1)

            def stack_product(o, Tq, Tk, head, q, k):
                i = head % 2
                _, keys, keys_lo = stacks[Tk]
                queries, hi_rows = stacks[Tq][1][i], rows_of[i]
                pe.matmul(o, queries[:, q], keys[i % len(keys)][:, k], start=True, stop=False)
                return pe.matmul(o, queries[hi_rows, q], keys_lo[hi_rows, k], start=False, stop=True)

            pe.wait_ge(s_hval, 2 * TT)
            z_group(T_IDX, T_CONV - T_IDX)
            for n in range(2 * (T_FOX - T_CONV)):
                z_half(T_CONV + n // 2, n % 2)
                for r, b, h in score_units(n):
                    if r == 0:
                        pe.wait_ge(s_z_lo, lo_halves(T_CONV))
                        pe.wait_ge(s_moved[T_IDX], 32)
                        pe.wait_ge(s_moved[T_IDX + 1], 32)
                        pe.wait_ge(s_vn, TT)
                    if r >= 2:
                        pe.wait_ge(s_relu, r - 1)
                    for c0 in range(0, (b + 1) * P, HALF):
                        c1 = min(c0 + HALF, (b + 1) * P)
                        mm = stack_product(logits_ps(r)[:, c0:c1], T_IDX + h // 2, T_IDX + 2, h,
                                           slice(b * P, (b + 1) * P), slice(c0, c1))
                    mm.then_inc(s_s, 1)
            r = HEADS * (TT - KB0)
            z_group(T_FOX, T_SWA - T_FOX)

            def forget_sums(h0):
                for j in range(2):
                    pe.wait_ge(s_fu, h0 + j + 1)
                    if h0 == 0:
                        pe.wait_ge(s_relu, r)
                    for c in range(2):
                        mm = pe.matmul(ps[:, 4 + 2 * j + c, :], minus, lg[j][:, c * HALF:(c + 1) * HALF],
                                       start=True, stop=True)
                    mm.then_inc(s_fp, 1)

            def logits(u):
                kind, b, h = units[u]
                if u >= 2:
                    pe.wait_ge(s_lg, u - 1)
                o = logits_ps(u)
                q = slice(b * P, (b + 1) * P)
                if kind == "swa":
                    for hh in range(HEADS):
                        pp = slice((hh // 2) * HD, (hh // 2 + 1) * HD)
                        c0 = 0 if b else P
                        mm = pe.matmul(o[:, hh * 2 * P + c0:(hh + 1) * 2 * P], z[pp, hh % 2, q],
                                       z[pp, 2, (b - 1) * P + c0:(b + 1) * P], start=True, stop=True)
                else:
                    if kind == "fox":
                        Tq, Tk = T_FOX + h // 2, T_FOX + 2 + h // 2
                    else:
                        Tq, Tk = T_DSA + h // 2, T_DSA + 2
                    masked = kind == "fox" or b < KB0
                    for c0 in range(0, (b + 1) * P, HALF):
                        c1 = min(c0 + HALF, (b + 1) * P)
                        here = masked and c1 == (b + 1) * P
                        mm = stack_product(o[:, c0:c1], Tq, Tk, h, q, slice(c0, c1))
                        if here:
                            mm = pe.matmul(o[:, q], ident_b[:, :], tri_b[:, :], start=False, stop=True,
                                           skip_group_check=True)
                mm.then_inc(s_logit, 1)

            def turn(u):
                kind, b, h = units[u]
                pe.wait_ge(s_exp, u + 1)
                if u >= 1:
                    pe.wait_ge(s_pt, u)
                blocks = [2 * hh + c for hh in range(HEADS) for c in ((0, 1) if b else (1,))] \
                    if kind == "swa" else range(b + 1)
                for c in blocks:
                    mm = pe.transpose(ps[:, c // 4, (c % 4) * P:(c % 4 + 1) * P],
                                      lg[u % 2][:, c * P:(c + 1) * P], ident)
                mm.then_inc(s_t, 1)

            def values(u):
                kind, b, h = units[u]
                g, first, last = group_of(u)
                pe.wait_ge(s_pt, u + 1)
                if first and g >= 2:
                    pe.wait_ge(s_of, g - 1)
                bank = group_bank(u)
                if kind == "swa":
                    cs = (0, 1) if b else (1,)
                    parts = [(hh, [(2 * hh + c, b - 1 + c, VS + hh // 2 * HD) for c in cs]) for hh in range(HEADS)]
                elif kind == "fox":
                    parts = [(h % 2, [(c, c, VF + h * HD) for c in range(b + 1)])]
                else:
                    parts = [(h, [(c, c, VD) for c in range(b + 1)])]
                for col, terms in parts:
                    for n, (c, block_, v0) in enumerate(terms):
                        mm = pe.matmul(bank[:, col * HD:(col + 1) * HD], pt[u % 2][:, c * P:(c + 1) * P],
                                       vn[:, block_, v0:v0 + HD], start=n == 0, stop=n == len(terms) - 1)
                mm.then_inc(s_pv, 1)

            def turn_out(u):
                g, _, last = group_of(u)
                if not last:
                    return
                pe.wait_ge(s_y_tok, g + 1)
                for c in range(1 if units[u][0] == "fox" else BT):
                    mm = pe.transpose(group_bank(u)[:, BW + c * P:BW + (c + 1) * P],
                                      y_tok[g % 2][:, c * P:(c + 1) * P], ident)
                mm.then_inc(s_turned, 1)

            def attention(u0, n):
                end = u0 + n
                logits(u0)
                logits(u0 + 1)
                for u in range(u0, end):
                    if u + 2 < end:
                        logits(u + 2)
                    turn(u)
                    if u - 2 >= u0:
                        turn_out(u - 2)
                    if u > u0:
                        values(u - 1)
                turn_out(end - 2)
                values(end - 1)
                turn_out(end - 1)

            forget_sums(0)
            pe.wait_ge(s_forget, 2)
            pe.wait_ge(s_z_lo, lo_halves(T_SWA))
            for T in (T_FOX, T_FOX + 2):
                pe.wait_ge(s_moved[T], 32)
            attention(U_FOX, 2 * TT)
            for T in (T_FOX + 1, T_FOX + 3):
                pe.wait_ge(s_moved[T], 32)
            forget_sums(2)
            pe.wait_ge(s_forget, 4)
            attention(U_FOX + 2 * TT, 2 * TT)
            pe.wait_ge(s_pt, U_SWA)
            z_group(T_SWA, T_AFS - T_SWA)
            pe.wait_ge(s_zf, 2 * T_AFS)
            attention(U_SWA, TT)
            pe.wait_ge(s_pt, U_DSA)
            pe.wait_ge(s_of, O_DSA)

            def gate_pairs(T0, buf):
                with pe.Fori(0, KT // 2) as i:
                    for j in range(2):
                        pe.wait_ge(s_w_lo, i * 2 + (T0 + j + 1))
                        for half in range(2):
                            pe.wait_ge(s_zf, i * 4 + (2 * (T0 + j) + half - 1))
                            slot = (T0 + j) % 2
                            tile_half(ps[:, half, :], slot, half)
                            tile_half(ps[:, 2 + half, :], slot, half, KT, BT, y_hi(buf), y_lo(buf)) \
                                .then_inc(s_z, 1)

            pe.wait_ge(s_ya, 1)
            gate_pairs(T_AFS, 0)
            gate_pairs(T_AFS + KT, 1)
            pe.wait_ge(s_ys, 1)
            gate_pairs(T_AFS + 2 * KT, 0)
            z_group(T_DSA, T_GD - T_DSA)
            pe.wait_ge(s_z_lo, lo_halves(T_GD))
            for T in (T_DSA, T_DSA + 1):
                pe.wait_ge(s_moved[T], 32)
            attention(U_DSA, HEADS * TT)
            pe.wait_ge(s_pt, U_DSA + HEADS * TT)
            pe.wait_ge(s_of, O_DSA + TT)
            gate_pairs(T_GD, 1)

            pe.wait_ge(s_ada_used, 6 * KT)
            for j, chunk in ((0, 0), (1, 3)):
                for c in range(2):
                    mm = pe.matmul(ps[:, 4 + 2 * j + c, :], ones, ada_sum2[:, chunk, c * HALF:(c + 1) * HALF],
                                   start=True, stop=True)
            pe.wait_ge(s_zf, 2 * T_WO)
            for c in range(2):
                for k in range(KT):
                    mm = pe.matmul(ps[:, 3, c * KT + k:c * KT + k + 1], ada_sum2[:, 1 + c, k * P:(k + 1) * P],
                                   ones[:, 0:1], start=True, stop=True)
            mm.then_inc(s_mod, 1)

            pe.wait_ge(s_mix_lo, KT)
            z_group(T_WO, KT)
            pe.wait_ge(s_zf, 2 * T_FFN)
            pe.wait_ge(s_mod, 4)

            def turn_o(t):
                if t >= 1:
                    pe.wait_ge(s_x1, t)
                for k in range(KT):
                    mm = pe.transpose(ps[:, 4 + k // 4, (k % 4) * P:(k % 4 + 1) * P],
                                      z[:, k, t * P:(t + 1) * P], ident)
                mm.then_inc(s_ot, 1)

            turn_o(0)
            for t in range(TT):
                if t + 1 < TT:
                    turn_o(t + 1)
                norm_x1(t)

            pe.wait_ge(s_h, 4 * TT)
            with pe.Fori(0, FG) as i:
                for j in range(4):
                    f, up = j // 2, j % 2
                    pe.wait_ge(s_w_lo, i * 6 + (T_FFN + FFN_AT[j] + 1))
                    for half in range(2):
                        if f:
                            pe.wait_ge(s_a if up else s_silu2, i * 4 + (half + 1))
                        mm = tile_half(ps[:, 2 * up + half, :], (T_FFN + j) % 2, half)
                        mm.then_inc(s_z, 1)
                for q in range(2 * TT):
                    t, c = q // 2, q % 2
                    if q == 0:
                        pe.wait_ge(s_a_lo, i * 4 + 3)
                    if q == TT:
                        pe.wait_ge(s_a_lo, i * 4 + 4)
                    pe.wait_ge(s_yf, i * 16 + (q + 1))
                    for f in range(2):
                        tok = slice(t * P, (t + 1) * P)
                        cc = slice(c * HALF, (c + 1) * HALF)
                        mm = product(ps[:, 4 + q % 4, :], y_t[:, 0, 0, f, tok], y_t[:, 0, 1, f, tok],
                                     y_t[:, 1, 0, f, cc], y_t[:, 1, 1, f, cc], f == 0, f == 1)
                    mm.then_inc(s_y, 1)

        @block.scalar
        def _(act):
            order = Order(act, act_order)

            def split_hi(T, i=0, step=0, n=None):
                act.wait_ge(s_raw[T % 2], 16 * (T // 2 + 1) + i * (8 * step))
                if T >= 2:
                    act.wait_ge(s_z, 2 * (T - 1) + i * (2 * step))
                n = n or width(T)
                act.activation(w_t[:, T % 2, 0, 0:n], raw[:, T % 2, 0:n], ACT.Copy).then_inc(s_w_hi, 1)

            def z_half(T, half):
                if half == 0:
                    split_hi(T + 1)
                act.wait_ge(s_z, 2 * T + half + 1)
                if T in stacks:
                    c = slice(half * HALF, (half + 1) * HALF)
                    if T == T_FOX and half == 0:
                        act.wait_ge(s_conv, BT)
                    if T == T_DSA + 2 and half == 0:
                        act.wait_ge(s_spill, 16 * KT)
                    for rows_, dst in stack_parts(T):
                        ins = act.activation(dst[rows_, c], ps[rows_, half, :], ACT.Copy, scale=stack_scale(T))
                    ins.then_inc(s_zf, 1)
                    return
                if T == T_CONV + 4 and half == 0:
                    act.wait_ge(s_prod, 1)
                if T == T_CONV + 5 and half == 0:
                    act.wait_ge(s_prod, 2)
                dst, scale = z_dest(T, half)
                act.activation(dst, ps[:, half, :], ACT.Copy, scale=scale).then_inc(s_zf, 1)

            def z_group(T0, n):
                for T in range(T0, T0 + n):
                    z_half(T, 0)
                    z_half(T, 1)

            def h_hi_part(v):
                act.wait_ge(s_hval, v + 1)
                t, kh = (v // 2) % TT, v % 2
                act.activation(h_hi[:, 4 * kh:4 * kh + 4, t * P:(t + 1) * P],
                               h_tmp[:, kh * HALF:(kh + 1) * HALF].rearrange("p (k n) -> p k n", k=4),
                               ACT.Copy).then_inc(s_h_hi, 1)

            def square_sum(src, col, bank=6):
                order.then_wait(act.activation(ps[:, bank:bank + 2, :].rearrange("p a n -> p (a n)"), src, ACT.Square,
                                               accum_out=stat[:, col:col + 1]))

            def roots(c0, c1, s):
                act.activation(root[:, c0:c1], stat[:, c0:c1], ACT.Sqrt, scale=1.0 / D,
                               bias=eps[:, 0:1]).then_inc(s, 1)

            act.wait_ge(s_pack, 48)
            act.activation(silu_c[:, :], c_col, ACT.Silu).then_inc(s_silu, 1)
            act.wait_ge(s_mix, MIX0)

            def vw_hi_half(i):
                act.wait_ge(s_rawv, 16 * (i + 1))
                act.activation(vw_hi_flat[:, vw_half[i]], raw_v[:, vw_half[i]], ACT.Copy).then_inc(s_vw_hi, 1)

            def x_root(t):
                act.wait_ge(s_xt[t], 16)
                square_sum(xs[:, t], t)
                roots(t, t + 1, s_root)

            def v_out(t):
                act.wait_ge(s_v, t + 1)
                act.activation(vn[:, t, :], ps[:, 4 + t % 2, 0:VN], ACT.Copy).then_inc(s_vn, 1)

            x_root(0)
            x_root(1)
            vw_hi_half(0)
            vw_hi_half(1)
            x_root(2)
            for t in range(1, TT + 1):
                h_hi_part(2 * (t - 1))
                h_hi_part(2 * (t - 1) + 1)
                if t + 2 < TT:
                    x_root(t + 2)
                if t == 3:
                    split_hi(0)
                if t >= 3:
                    v_out(t - 3)
            v_out(TT - 2)
            v_out(TT - 1)
            act.wait_ge(s_fabs, 1)
            order.then_wait(act.activation(lf[:, 1, :], lf[:, 1, :], ACT.Exp, scale=-1.0))
            act.activation(lf[:, 1, :], lf[:, 1, :], ACT.Ln, bias=ones[:, 0:1]).then_inc(s_fln, 1)
            z_group(T_IDX, T_CONV - T_IDX)
            for half in range(2 * (T_FOX - T_CONV)):
                z_half(T_CONV + half // 2, half % 2)
                for r, b, h in score_units(half):
                    n = (b + 1) * P
                    act.wait_ge(s_s, r + 1)
                    if r >= 2:
                        act.wait_ge(s_score, r - 1)
                    act.activation(lg[r % 2][:, 0:n], logits_ps(r)[:, 0:n], ACT.Relu).then_inc(s_relu, 1)
            z_group(T_FOX, T_SWA - T_FOX)

            def group_hi(u):
                g, _, last = group_of(u)
                if not last or units[u][0] == "swa":
                    return
                act.wait_ge(s_turned, g + 1)
                dst, src = group_turned(u, y_hi(1))
                act.activation(dst, src, ACT.Copy).then_inc(s_o_hi, 1)

            def exponentials(u):
                kind, b, h = units[u]
                g, first, _ = group_of(u)
                s = u % 2
                act.wait_ge(s_neg, u + 1)
                if first and g >= 4:
                    act.wait_ge(s_y_tok, g - 3)
                if kind == "swa":
                    w = window_cols(lg[s], b)
                    for hh in range(HEADS):
                        act.activation(w[:, hh], w[:, hh], ACT.Exp, bias=neg[:, s, hh:hh + 1],
                                       accum_out=den[:, g % 4, hh:hh + 1])
                    act.activation(sink_e[:, u % 4, :], sink_e[:, u % 4, :], ACT.Exp).then_inc(s_exp, 1)
                else:
                    w = lg[s][:, 0:(b + 1) * P]
                    col = h % 2 if kind == "fox" else h
                    act.activation(w, w, ACT.Exp, bias=neg[:, s, 0:1],
                                   accum_out=den[:, g % 4, col:col + 1]).then_inc(s_exp, 1)

            def attention(u0, n):
                end = u0 + n
                exponentials(u0)
                for u in range(u0, end):
                    kind, b, h = units[u]
                    if u + 1 < end:
                        exponentials(u + 1)
                    act.wait_ge(s_t, u + 1)
                    if u >= u0 + 2:
                        act.wait_ge(s_pv, u - 1)
                    bank = ps[:, 0:2, :].rearrange("p a n -> p (a n)")
                    if kind == "swa":
                        dst, src = window_cols(pt[u % 2], b), window_cols(bank, b)
                    else:
                        dst, src = pt[u % 2][:, 0:(b + 1) * P], bank[:, 0:(b + 1) * P]
                    act.activation(dst, src, ACT.Copy).then_inc(s_pt, 1)
                    if u >= u0 + 2:
                        group_hi(u - 2)
                group_hi(end - 2)
                group_hi(end - 1)

            act.wait_ge(s_ya_out, 16 * BT)
            attention(U_FOX, 2 * TT)
            attention(U_FOX + 2 * TT, 2 * TT)
            z_group(T_SWA, T_AFS - T_SWA)
            act.wait_ge(s_ya_in, 16 * BT)
            act.activation(y_hi(0), ya_back[:, :, :], ACT.Copy).then_inc(s_ya_hi, 1)
            attention(U_SWA, TT)

            def gate_pairs(T0, m0):
                with act.Fori(0, KT // 2) as i:
                    for j in range(2):
                        T = T0 + j
                        split_hi(T + 1, i, 2, GT)
                        for half in range(2):
                            act.wait_ge(s_z, i * 4 + (2 * T + half + 1))
                            act.wait_ge(s_mix, i * 4 + (MIX0 + m0 + 2 * j + half))
                            act.activation(sig, ps[:, half, :], ACT.Sigmoid)
                            act.activation(prj, ps[:, 2 + half, :], ACT.Copy).then_inc(s_zf, 1)

            gate_pairs(T_AFS, 0)
            act.activation(y_hi(0), y_s, ACT.Copy).then_inc(s_ys_hi, 1)
            gate_pairs(T_AFS + KT, 2 * KT)
            gate_pairs(T_AFS + 2 * KT, 4 * KT)
            z_group(T_DSA, T_GD - T_DSA)
            attention(U_DSA, HEADS * TT)
            gate_pairs(T_GD, 6 * KT)
            act.wait_ge(s_mix, MIX0 + 8 * KT)
            for dt in range(KT):
                act.activation(h_hi[:, dt], z[:, dt], ACT.Copy).then_inc(s_mix_hi, 1)
            z_group(T_WO, KT)
            act.wait_ge(s_x, 16 * TT)

            def o_root(t):
                act.wait_ge(s_ot, t + 1)
                square_sum(ps[:, 4:6, :].rearrange("p a n -> p (a n)"), TT + t)
                roots(TT + t, TT + t + 1, s_oroot)

            o_root(0)
            for t in range(TT + 1):
                if t < TT:
                    act.wait_ge(s_x1, t + 1)
                    square_sum(x1[:, t], 2 * TT + t)
                    roots(2 * TT + t, 2 * TT + t + 1, s_root)
                if t + 1 < TT:
                    o_root(t + 1)
                if t >= 1:
                    h_hi_part(2 * (TT + t - 1))
                    h_hi_part(2 * (TT + t - 1) + 1)

            def ffn_group(i, last):
                def split(m):
                    T = T_FFN + m
                    act.wait_ge(s_raw[T % 2], 16 * (T // 2 + 1) + i * 48)
                    if m in (2, 4):
                        dst = y_hi(1)[:, m // 2 - 1, :]
                    else:
                        j = {0: 0, 1: 1, 3: 2, 5: 3, 6: 4}[m]
                        act.wait_ge(s_z, i * 8 + (2 * (T_FFN + j) - 2))
                        dst = w_t[:, (T_FFN + j) % 2, 0, 0:D]
                    act.activation(dst, raw[:, T % 2, 0:D], ACT.Copy).then_inc(s_w_hi, 1)

                for j in range(4):
                    for m in FFN_AHEAD[j]:
                        if m < 6 or not last:
                            split(m)
                    f, up = j // 2, j % 2
                    for half in range(2):
                        n = 2 * f + half
                        c = slice(half * HALF, (half + 1) * HALF)
                        if up:
                            act.wait_ge(s_a, i * 4 + (n + 1))
                            act.activation(y_hi(0)[:, f, c], act2[half], ACT.Copy).then_inc(s_a_hi, 1)
                        else:
                            act.wait_ge(s_z, i * 8 + (2 * (T_FFN + j) + half + 1))
                            if f:
                                act.wait_ge(s_a_lo, i * 4 + (half + 1))
                            act.activation(act2[half], ps[:, half, :], ACT.Silu).then_inc(s_silu2, 1)

            with act.Fori(0, FG - 1) as i:
                ffn_group(i, False)
            ffn_group(FG - 1, True)
            for t in range(TT):
                act.wait_ge(s_yf, 4 + 16 * (FG - 1) + 2 * (t + 1))
                square_sum(z[:, t], t, 0)
                roots(t, t + 1, s_yroot)

        @block.gpsimd
        def _(pool):
            order = Order(pool, pool_order)
            pool.memset(eps[:, :], EPS).then_inc(s_mix, 1)

            def split_lo(T, i=0, step=0, n=None):
                n = n or width(T)
                pool.wait_ge(s_w_hi, T + 1 + i * step)
                pool.tensor_tensor(w_t[:, T % 2, 1, 0:n], raw[:, T % 2, 0:n],
                                   w_t[:, T % 2, 0, 0:n].bitcast(F32), ALU.subtract).then_inc(s_w_lo, 1)

            def h_lo_part(v):
                pool.wait_ge(s_h_hi, v + 1)
                t, kh = (v // 2) % TT, v % 2
                at = (slice(None), slice(4 * kh, 4 * kh + 4), slice(t * P, (t + 1) * P))
                pool.tensor_tensor(h_lo[at], h_tmp[:, kh * HALF:(kh + 1) * HALF].rearrange("p (k n) -> p k n", k=4),
                                   h_hi[at].bitcast(F32), ALU.subtract).then_inc(s_h, 1)

            for i, part in enumerate(vw_half):
                pool.wait_ge(s_vw_hi, i + 1)
                pool.tensor_tensor(vw_lo_flat[:, part], raw_v[:, part], vw_hi_flat[:, part].bitcast(F32),
                                   ALU.subtract).then_inc(s_vw_lo, 1)
            for t in range(TT):
                h_lo_part(2 * t)
                h_lo_part(2 * t + 1)
                if t == 2:
                    split_lo(0)

            def stack_moves(T):
                kind, hi, lo = stacks[T]
                if kind == "q":
                    pool.wait_ge(s_z_lo, lo_halves(T) + 2)
                else:
                    pool.wait_ge(s_zf, 2 * T + 2)
                for i in range(2):
                    src = (lo if kind == "q" else hi[i])[rows_of[i]]
                    pool.dma_start(hi[i][rows_of[1 - i]], src).then_inc(s_moved[T], 16)

            for T in range(1, T_AFS + 1):
                split_lo(T)
                if T - 1 in s_moved:
                    stack_moves(T - 1)

            def gate_pairs(T0, first):
                with order.loop(KT // 2, 0 if first else 4) as i:
                    for j in range(2):
                        T = T0 + j
                        split_lo(T + 1, i, 2, GT)
                        for half in range(2):
                            c = slice(half * HALF, (half + 1) * HALF)
                            pool.wait_ge(s_zf, i * 4 + (2 * T + half + 1))
                            mix = z[:, i * 2 + j, c]
                            if first:
                                pool.tensor_tensor(mix, sig, prj, ALU.mult).then_inc(s_mix, 1)
                            else:
                                order.then_wait(pool.tensor_tensor(sig, sig, prj, ALU.mult))
                                pool.tensor_tensor(mix, mix, sig, ALU.add).then_inc(s_mix, 1)

            pool.wait_ge(s_ya_hi, 1)
            pool.tensor_tensor(y_lo(0), ya_back[:, :, :], y_hi(0).bitcast(F32), ALU.subtract).then_inc(s_ya, 1)
            gate_pairs(T_AFS, True)
            pool.wait_ge(s_ys_hi, 1)
            pool.tensor_tensor(y_lo(0), y_s, y_hi(0).bitcast(F32), ALU.subtract).then_inc(s_ys, 1)
            pool.wait_ge(s_mix, MIX0 + 2 * KT)
            gate_pairs(T_AFS + KT, False)
            pool.wait_ge(s_mix, MIX0 + 4 * KT)
            gate_pairs(T_AFS + 2 * KT, False)
            for T in range(T_DSA + 1, T_GD + 1):
                split_lo(T)
                if T - 1 in s_moved:
                    stack_moves(T - 1)
            pool.wait_ge(s_refill, 16 * KT)
            gate_pairs(T_GD, False)
            for T in range(T_WO + 1, T_FFN + 1):
                split_lo(T)
            for v in range(2 * TT, 4 * TT):
                h_lo_part(v)
            pool.wait_ge(s_ot, TT)
            for q in range(4):
                pool.memset(region_a[:, q * 2 * L:(q + 1) * 2 * L], 0.0).then_inc(s_yf, 1)

            def ffn_group(i, last):
                def split(m):
                    T = T_FFN + m
                    pool.wait_ge(s_w_hi, i * 6 + (T + 1))
                    if m in (2, 4):
                        hi, lo = y_hi(1)[:, m // 2 - 1, :], y_lo(1)[:, m // 2 - 1, :]
                    else:
                        slot = (T_FFN + {0: 0, 1: 1, 3: 2, 5: 3, 6: 4}[m]) % 2
                        hi, lo = w_t[:, slot, 0, 0:D], w_t[:, slot, 1, 0:D]
                    pool.tensor_tensor(lo, raw[:, T % 2, 0:D], hi.bitcast(F32), ALU.subtract).then_inc(s_w_lo, 1)

                for j in range(4):
                    for m in FFN_AHEAD[j]:
                        if m < 6 or not last:
                            split(m)
                    for half in range(2) if j in (1, 3) else ():
                        f = j // 2
                        c = slice(half * HALF, (half + 1) * HALF)
                        pool.wait_ge(s_a_hi, i * 4 + (2 * f + half + 1))
                        pool.tensor_tensor(y_lo(0)[:, f, c], act2[half], y_hi(0)[:, f, c].bitcast(F32),
                                           ALU.subtract).then_inc(s_a_lo, 1)

            with pool.Fori(0, FG - 1) as i:
                ffn_group(i, False)
            ffn_group(FG - 1, True)
            for t in range(TT):
                pool.wait_ge(s_y_norm, t + 1)
                pool.tensor_tensor(x1[:, t], x1[:, t], z[:, t], ALU.add).then_inc(s_final, 1)

        @block.vector
        def _(dve):
            order = Order(dve, dve_order)
            dve.wait_ge(s_pack, 48)
            dve.tensor_copy(ident_b[:, :], ident)
            order.mark(dve.tensor_copy(tri_b[:, :], tri))

            def ada(n, k, dst):
                dve.wait_ge(s_ada[n % 3], 16 * (n // 3 + 1))
                src, s = ada_raw[n % 3], silu_c[:, k:k + 1]
                if k == 0:
                    ins = dve.tensor_scalar(dst, src, s, None, ALU.mult)
                else:
                    dve.wait_ge(s_ada_used, n - (0 if n < 2 * KT else 3))
                    ins = dve.scalar_tensor_tensor(dst, src, s, dst, ALU.mult, ALU.add)
                ins.then_inc(s_ada_used, 1)

            def normed_x(t):
                dve.wait_ge(s_root, t + 1)
                order.then_wait(dve.reciprocal(rstd[:, t:t + 1], root[:, t:t + 1]))
                dve.tensor_scalar(xs[:, t], xs[:, t], rstd[:, t:t + 1], None, ALU.mult).then_inc(s_norm, 1)

            dve.wait_ge(s_silu, 1)
            for k in range(KT):
                ada(k, k, ada_sum1[:, 0])
            normed_x(0)
            normed_x(1)
            for k in range(KT):
                ada(KT + k, k, ada_sum1[:, 1])

            def mod_columns(at, i, g):
                dve.tensor_tensor(mod_col[:, i, :], at[:, 0:KT], bias_col[i], ALU.add)
                order.then_wait(dve.tensor_tensor(mod_col[:, i + 1, :], at[:, KT:2 * KT], bias_col[i + 1], ALU.add))
                return dve.scalar_tensor_tensor(mod_col[:, i + 1, :], mod_col[:, i + 1, :], 1.0, g, ALU.add, ALU.mult)

            dve.wait_ge(s_mod, 1)
            mod_columns(ps[:, 5, :], 0, g0_col).then_inc(s_mod, 1)
            dve.wait_ge(s_mod, 2)

            def make_diag(t, col):
                if t >= 2:
                    dve.wait_ge(s_ht, TT + t - 1)
                dve.tensor_scalar(diag[:, t % 2, :], ident, rstd[:, col:col + 1], None, ALU.mult) \
                   .then_inc(s_norm, 1)

            def h_values(count, i):
                dve.wait_ge(s_ht, count + 1)
                for kh in range(2):
                    v = 2 * count + kh
                    if v >= 2:
                        dve.wait_ge(s_h, v - 1)
                    for k in range(4):
                        kk = 4 * kh + k
                        ins = dve.tensor_scalar(h_tmp[:, kk * P:(kk + 1) * P],
                                                ps[:, 2 * (count % 2) + kh, k * P:(k + 1) * P],
                                                mod_col[:, i + 1, kk:kk + 1], mod_col[:, i, kk:kk + 1],
                                                ALU.mult, ALU.add)
                    ins.then_inc(s_hval, 1)

            for t in range(TT):
                h_values(t, 0)
                if t + 2 < TT:
                    normed_x(t + 2)

            dve.wait_ge(s_vn, TT)
            f3, fa, fe = (lf[:, i, :].rearrange("p (t h) -> p t h", t=TT) for i in (0, 1, 2))
            order.then_wait(dve.tensor_tensor(f3, vn[:, :, VFF:VFF + HEADS],
                                              fox_b.unsqueeze(1).broadcast_to((P, TT, HEADS)), ALU.add))
            dve.scalar_tensor_tensor(lf[:, 1, :], lf[:, 0, :], -1.0, lf[:, 0, :], ALU.mult, ALU.max) \
               .then_inc(s_fabs, 1)
            dve.wait_ge(s_fln, 1)
            order.then_wait(dve.scalar_tensor_tensor(lf[:, 2, :], lf[:, 0, :], 0.0, lf[:, 1, :], ALU.min,
                                                     ALU.subtract))

            def stack_lo(T):
                lo = stacks[T][2]
                for half in range(2):
                    c = slice(half * HALF, (half + 1) * HALF)
                    dve.wait_ge(s_zf, 2 * T + half + 1)
                    if T == T_FOX + 1 and half == 0:
                        dve.wait_ge(s_moved[T_FOX], 32)
                    for rows_, hi in stack_parts(T):
                        ins = dve.scalar_tensor_tensor(lo[rows_, c], ps[rows_, half, :], stack_scale(T),
                                                       hi[rows_, c].bitcast(F32), ALU.mult, ALU.subtract)
                    ins.then_inc(s_z_lo, 1)

            for T in range(T_IDX, T_CONV):
                stack_lo(T)

            r = 0
            for b in range(KB0, TT):
                n = (b + 1) * P
                for h in range(HEADS):
                    dve.wait_ge(s_relu, r + 1)
                    w = vn[:, b, VWI + h:VWI + h + 1]
                    if h == 0:
                        ins = dve.tensor_scalar(sc_at[b], lg[r % 2][:, 0:n], w, None, ALU.mult)
                    else:
                        dve.wait_ge(s_score, r)
                        ins = dve.scalar_tensor_tensor(sc_at[b], lg[r % 2][:, 0:n], w, sc_at[b], ALU.mult, ALU.add)
                    ins.then_inc(s_score, 1)
                    r += 1
                dve.wait_ge(s_score, r)
                order.mark(dve.tensor_tensor(sc_at[b][:, b * P:n], sc_at[b][:, b * P:n], tri, ALU.add))

            order.mark(dve.memset(conv_z[:, 0:2], 0.0))
            for c in range(BT):
                dve.wait_ge(s_zf, 2 * (T_CONV + 2 * c + 2))
                dve.tensor_tensor(conv_z[:, 2:L + 2], z[:, 2 * c], z[:, 2 * c + 1], ALU.mult).then_inc(s_prod, 1)
                dve.wait_ge(s_prod, c + 1)
                order.wait()
                order.then_wait(dve.tensor_scalar(pt[c], conv_z[:, 0:L], conv_w[:, c, 0:1], None, ALU.mult))
                for k in (1, 2):
                    order.then_wait(dve.scalar_tensor_tensor(pt[c], conv_z[:, k:L + k], conv_w[:, c, k:k + 1],
                                                             pt[c], ALU.mult, ALU.add))
            for c in range(BT):
                dve.wait_ge(s_zf, 2 * (T_CONV + 5 + c))
                dve.tensor_tensor(pt[c], pt[c], z[:, 2 * c], ALU.mult).then_inc(s_conv, 1)
            for T in range(T_FOX, T_SWA):
                stack_lo(T)

            def top_k(blocks):
                order.wait()
                with dve.Fori(0, TOPK // 8):
                    for n, b in enumerate(blocks):
                        dve.max(top8[:, n, :], sc_at[b])
                    dve.drain()
                    for n, b in enumerate(blocks):
                        dve.match_replace(sc_at[b], top8[:, n, :], sc_at[b], TAKEN)
                    dve.drain()
                for b in blocks:
                    order.mark(dve.tensor_scalar(sc_at[b], sc_at[b], TAKEN / 2, -BIG, ALU.is_gt, ALU.mult))

            def forget_sums(h0):
                for j in range(2):
                    spread = lg[j].rearrange("p (t n) -> p t n", t=TT)
                    dve.tensor_tensor(spread, upper.unsqueeze(1).broadcast_to((P, TT, P)),
                                      fe[:, :, h0 + j:h0 + j + 1].broadcast_to((P, TT, P)), ALU.mult) \
                       .then_inc(s_fu, 1)
                for j in range(2):
                    dve.wait_ge(s_fp, h0 + j + 1)
                    for b in range(TT):
                        src = ps[:, 4 + 2 * j + b // 4, (b % 4) * P:(b % 4 + 1) * P]
                        dst = forget[:, j, b * P:(b + 1) * P]
                        if b == 0:
                            ins = dve.tensor_copy(dst, src)
                        else:
                            ins = dve.tensor_scalar(dst, src, forget[:, j, b * P - 1:b * P], None, ALU.add)
                        if b < TT - 1:
                            order.then_wait(ins)
                    ins.then_inc(s_forget, 1)
                dve.wait_ge(s_forget, h0 + 2)

            def dsa_bias(u):
                _, b, h = units[u]
                n = (b + 1) * P
                slope = 2.0 ** -(HEADS + 1 + h)
                dist = region_d[:, L - n:L]
                if b < KB0:
                    order.mark(dve.tensor_scalar(spare[:, 0:n], dist, slope, None, ALU.mult))
                else:
                    order.mark(dve.scalar_tensor_tensor(spare[:, 0:n], dist, slope, sc_at[b], ALU.mult, ALU.add))

            def group_norm(u):
                kind, b, h = units[u]
                g, _, last = group_of(u)
                if not last:
                    return
                nh = 2 if kind == "fox" else HEADS
                dve.wait_ge(s_pv, u + 1)
                d, r = den[:, g % 4, 0:nh], rec[:, g % 2, 0:nh]
                if kind == "swa":
                    order.then_wait(dve.tensor_tensor(d, d, sink_e[:, u % 4, :], ALU.add))
                order.then_wait(dve.reciprocal(r, d))
                if g >= 2:
                    dve.wait_ge(s_turned, g - 1)
                dve.tensor_tensor(y_tok[g % 2][:, 0:nh * HD].rearrange("p (h d) -> p h d", h=nh),
                                  group_bank(u)[:, 0:nh * HD].rearrange("p (h d) -> p h d", h=nh),
                                  r.unsqueeze(2).broadcast_to((P, nh, HD)), ALU.mult).then_inc(s_y_tok, 1)

            def group_lo(u):
                kind, b, h = units[u]
                g, _, last = group_of(u)
                if not last:
                    return
                if kind == "swa":
                    dve.wait_ge(s_turned, g + 1)
                    dst, src = group_turned(u, y_s)
                    dve.tensor_copy(dst, src).then_inc(s_of, 1)
                else:
                    dve.wait_ge(s_o_hi, (g if kind == "fox" else g - TT) + 1)
                    dst, src = group_turned(u, y_lo(1))
                    hi, _ = group_turned(u, y_hi(1))
                    dve.tensor_tensor(dst, src, hi.bitcast(F32), ALU.subtract).then_inc(s_of, 1)

            def biased(u):
                kind, b, h = units[u]
                s, w = u % 2, (b + 1) * P
                o = logits_ps(u)
                dve.wait_ge(s_logit, u + 1)
                if u >= 2:
                    dve.wait_ge(s_t, u - 1)
                if kind == "swa":
                    for hh in range(HEADS):
                        ins = dve.tensor_tensor_reduce(
                            window_cols(lg[s], b)[:, hh], window_cols(o, b)[:, hh],
                            window_cols(region_d[:, :], b)[:, hh], 1.0, TAKEN, ALU.add, ALU.max,
                            mx[:, s, hh:hh + 1])
                    ins.then_inc(s_lg, 1)
                    dve.wait_ge(s_lg, u + 1)
                    order.then_wait(dve.tensor_tensor(mx[:, s, :], mx[:, s, :], sinks, ALU.max))
                    order.then_wait(dve.tensor_scalar(neg[:, s, :], mx[:, s, :], -1.0, None, ALU.mult))
                    dve.tensor_tensor(sink_e[:, u % 4, :], sinks, neg[:, s, :], ALU.add).then_inc(s_neg, 1)
                    return
                if kind == "dsa":
                    order.wait()
                bias = spare[:, 0:w] if kind == "dsa" else forget[:, h % 2, 0:w]
                dve.tensor_tensor_reduce(lg[s][:, 0:w], o[:, 0:w], bias, 1.0, TAKEN, ALU.add, ALU.max,
                                         mx[:, s, 0:1]).then_inc(s_lg, 1)
                dve.wait_ge(s_lg, u + 1)
                dve.tensor_scalar(neg[:, s, 0:1], mx[:, s, 0:1], -1.0, None, ALU.mult).then_inc(s_neg, 1)

            def attention(u0, n):
                end = u0 + n
                dsa = units[u0][0] == "dsa"
                if dsa:
                    dsa_bias(u0)
                biased(u0)
                for u in range(u0, end):
                    if u + 1 < end:
                        if dsa:
                            dsa_bias(u + 1)
                        biased(u + 1)
                    if u >= u0 + 2:
                        group_norm(u - 2)
                    if u >= u0 + 3:
                        group_lo(u - 3)
                group_norm(end - 2)
                group_lo(end - 3)
                group_norm(end - 1)
                group_lo(end - 2)
                group_lo(end - 1)

            forget_sums(0)
            attention(U_FOX, 2 * TT)
            dve.wait_ge(s_t, 2 * TT)
            forget_sums(2)
            attention(U_FOX + 2 * TT, 2 * TT)
            dve.wait_ge(s_table, 16)
            attention(U_SWA, TT)

            top_k(range(KB0, TT))
            for T in range(T_DSA, T_GD):
                stack_lo(T)
            order.wait()
            dve.wait_ge(s_table, 32)
            attention(U_DSA, HEADS * TT)

            for k in range(KT):
                for j in range(4):
                    ada(2 * KT + 4 * k + j, k, ada_sum2[:, j])
            for dt in range(KT):
                dve.wait_ge(s_mix_hi, dt + 1)
                dve.tensor_tensor(h_lo[:, dt], z[:, dt], h_hi[:, dt].bitcast(F32), ALU.subtract).then_inc(s_mix_lo, 1)
            dve.wait_ge(s_rows, 64)
            dve.wait_ge(s_mod, 3)
            for j in range(2):
                sums = ps[:, 4 + 2 * j:6 + 2 * j, :].rearrange("p a n -> p (a n)")
                order.then_wait(dve.tensor_tensor(ada_raw[1 + j], sums, ada_raw[1 + j], ALU.add))
                order.mark(dve.tensor_tensor(g_row[j], ada_raw[1 + j], g_row[j], ALU.mult))
            mod_columns(ps[:, 3, :], 2, g2_col).then_inc(s_mod, 1)
            dve.wait_ge(s_mod, 4)
            dve.wait_ge(s_x, 16 * TT)
            o = ps[:, 4:6, :].rearrange("p a n -> p (a n)")
            for t in range(TT + 1):
                if t < TT:
                    dve.wait_ge(s_oroot, t + 1)
                    c = TT + t
                    order.then_wait(dve.reciprocal(rstd[:, c:c + 1], root[:, c:c + 1]))
                    order.then_wait(dve.scalar_tensor_tensor(o, o, rstd[:, c:c + 1], g_row[0], ALU.mult, ALU.mult))
                    dve.tensor_tensor(x1[:, t], o, x1[:, t], ALU.add).then_inc(s_x1, 1)
                if t >= 1:
                    h_values(TT + t - 1, 2)
                if t < TT:
                    dve.wait_ge(s_root, TT + t + 1)
                    c = 2 * TT + t
                    order.then_wait(dve.reciprocal(rstd[:, c:c + 1], root[:, c:c + 1]))
                    make_diag(t, c)

            dve.wait_ge(s_yf, 4)

            def y_norm(t):
                dve.wait_ge(s_yroot, t + 1)
                order.then_wait(dve.reciprocal(rstd[:, t:t + 1], root[:, t:t + 1]))
                dve.scalar_tensor_tensor(z[:, t], z[:, t], rstd[:, t:t + 1], g_row[1], ALU.mult, ALU.mult) \
                   .then_inc(s_y_norm, 1)

            def ffn_group(i, last):
                for f in range(2):
                    for half in range(2):
                        n = 2 * f + half
                        dve.wait_ge(s_silu2, i * 4 + (n + 1))
                        dve.wait_ge(s_z, i * 8 + (2 * (T_FFN + 2 * f + 1) + half + 1))
                        dve.tensor_tensor(act2[half], ps[:, 2 + half, :], act2[half], ALU.mult).then_inc(s_a, 1)
                for q in range(2 * TT):
                    t, c = q // 2, q % 2
                    dst = z[:, t, c * HALF:(c + 1) * HALF]
                    dve.wait_ge(s_y, i * 16 + (q + 1))
                    dve.tensor_tensor(dst, ps[:, 4 + q % 4, :], dst, ALU.add).then_inc(s_yf, 1)
                    if last and c and t >= 1:
                        y_norm(t - 1)

            with dve.Fori(0, FG - 1) as i:
                ffn_group(i, False)
            ffn_group(FG - 1, True)
            y_norm(TT - 1)


def _host():
    import numpy as np

    i, j = np.arange(P)[:, None], np.arange(P)[None, :]
    f = np.float32
    consts = np.stack([(i == j).astype(f), np.where(j <= i, 0, -BIG).astype(f), (i <= j).astype(f),
                       np.ones((P, P), f), -np.ones((P, P), f)], 1)
    j = np.arange(2 * P)[None, :]
    dist = i - j + P
    window = np.stack([np.where((dist >= 0) & (dist < WINDOW), -(2.0 ** -(h + 1)) * dist, -BIG)
                       for h in range(HEADS)], 1).astype(f).reshape(P, HEADS * 2 * P)
    distance = -(i + (L - P) - np.arange(L)[None, :]).astype(f)
    return consts, window, distance


def kernel(x, c, w_ada, b_ada, norm_g, w_in, conv_w, fox_bias, swa_sinks, w_branch, w_o, w_gate, w_up, w_down):
    import numpy as np
    import concourse.bacc as bacc
    from concourse.bass_utils import run_bass_kernel_spmd

    x, c, w_ada, b_ada, norm_g, w_in, conv_w, fox_bias, swa_sinks, w_branch, w_o, w_gate, w_up, w_down = (
        np.asarray(a) for a in (x, c, w_ada, b_ada, norm_g, w_in, conv_w, fox_bias, swa_sinks, w_branch, w_o,
                                w_gate, w_up, w_down))
    w_in, w_ada, b_ada, norm_g = w_in[0], w_ada[0], b_ada[0], norm_g[0]
    w_branch, w_o, w_gate, w_up, w_down = w_branch[0], w_o[0], w_gate[0], w_up[0], w_down[0]

    sizes = [256, 256, 256, 256, 64, 64, 256, 64, 4, 256, 256, 256, 4, 256, 128, 128, 4 * D]
    at = [sum(sizes[:i]) for i in range(len(sizes))]
    a_u, a_b, a_c, d_q, d_k, d_v, d_qi, d_ki, d_wi, f_q, f_k, f_v, f_f, s_q, s_k, s_v, g = at

    def span(a, n=P):
        return list(range(a, a + n))

    def tile(w, columns):
        return w[:, columns].reshape(-1, P, len(columns)).transpose(1, 0, 2).reshape(P, -1)

    z_cols = [span(d_qi), span(d_qi + P), span(d_ki, HD) * 2]
    for ch in range(2):
        z_cols += [span(a_c + ch * P), span(a_u + ch * P)]
    z_cols += [span(a_b), span(a_b + P)]
    z_cols += [span(f_q), span(f_q + P), span(f_k), span(f_k + P)]
    z_cols += [span(s_q + t * HD, HD) + span(s_q + (t + 2) * HD, HD) for t in range(2)] + [span(s_k)]
    z_cols += [span(d_q), span(d_q + P), span(d_k, HD) * 2]
    w_z = np.stack([tile(w_in, cc) for cc in z_cols])
    w_v = tile(w_in, span(d_v, 64) + span(f_v, 256) + span(s_v, 128) + span(d_wi, 4) + span(f_f, 4))
    gates = []
    for n in (0, 2, 3, 1):
        for dt in range(KT):
            gates.append(np.concatenate([tile(w_in, span(g + n * D + dt * P)),
                                         tile(w_branch[n], span(dt * P))], 1))
    w_gates = np.stack(gates)
    w_ot = np.stack([tile(w_o, span(dt * P)) for dt in range(KT)])
    ffn = []
    for i in range(FG):
        down = [w_down[f * P:(f + 1) * P] for f in (2 * i, 2 * i + 1)]
        gate, up = ([tile(w, span(f * P)) for f in (2 * i, 2 * i + 1)] for w in (w_gate, w_up))
        ffn += [gate[0], up[0], down[0], gate[1], down[1], up[1]]
    w_ffn = np.stack(ffn)
    w_adat = w_ada.reshape(KT, P, 6, D).transpose(2, 0, 1, 3)

    def column(v):
        return v.reshape(KT, P).T

    bias = b_ada.reshape(6, D)
    cols = np.concatenate([column(c[0]), column(norm_g[0]), column(norm_g[2]), column(bias[0]), column(bias[1]),
                           column(bias[3]), column(bias[4]),
                           conv_w[0].reshape(3, BT, P).transpose(2, 1, 0).reshape(P, 6)], 1)
    rows = np.stack([bias[2], bias[5], norm_g[1], norm_g[3]])
    per_head = np.broadcast_to(np.concatenate([fox_bias[0], swa_sinks[0]])[None, :], (P, 8))
    consts, window, distance = _host()
    feeds = {"x": x[0], "w_z": w_z, "w_v": w_v, "w_gates": w_gates, "w_o": w_ot, "w_ffn": w_ffn, "w_ada": w_adat,
             "cols": cols, "rows": rows, "per_head": per_head, "consts": consts, "window_bias": window,
             "distance": distance}
    nc = bacc.Bacc("TRN2", target_bir_lowering=False, num_devices=1)
    arrays, args = {}, {}
    for name, a in feeds.items():
        a = np.ascontiguousarray(a)
        arrays[f"in_{name}"] = a
        args[name] = nc.dram_tensor(f"in_{name}", a.shape, mybir.dt.from_np(a.dtype), kind="ExternalInput").ap()
    args["out"] = nc.dram_tensor("out", (L, D), F32, kind="ExternalOutput").ap()
    build(nc, **args)
    r = run_bass_kernel_spmd(nc, [arrays], core_ids=[0])
    return r.results[0]["out"].reshape(1, L, D)
```

```python
from contextlib import ExitStack, contextmanager

import concourse.bass as bass
from concourse import mybir

F32 = mybir.dt.float32
F32R = mybir.dt.float32r
BF16 = mybir.dt.bfloat16
ALU = mybir.AluOpType
ACT = mybir.ActivationFunctionType

P = 128
D = 1024
L = 1024
KT = D // P
TT = L // P
HALF = 512
HD = 64
HEADS = 4
BW = 256
BT = BW // P
FF = -(-8 * D // (3 * 256)) * 256
FT = FF // P
FG = FT // 2
TOPK = min(256, L // 4)
KB0 = TOPK // P
WINDOW = 128
EPS = 1e-6
SCORE_ROUNDS, SWA_ROUNDS = 3, (5, 7)
BIG = 1e30
TAKEN = -3e38

VD, VF, VS, VWI, VFF = 0, 64, 320, 448, 452
VN = 456

T_IDX, T_CONV, T_FOX, T_SWA, T_AFS = 0, 3, 9, 13, 16
T_DSA = T_AFS + 3 * KT
T_GD = T_DSA + 2
T_WO = T_GD + KT
T_WO2 = T_WO + KT
T_FFN = T_WO2 + KT
GT = (KT + BT) * P

FFN_AT = (0, 1, 3, 5)
FFN_AHEAD = ((1,), (2, 3), (4, 5), (6,))

U_FOX, U_SWA, U_DSA = 0, HEADS * TT, HEADS * TT + TT
O_FOX, O_SWA, O_DSA = 0, 2 * TT, 3 * TT


MIX0 = 1


class Order:

    def __init__(self, eng, sem):
        self.eng, self.sem, self.base, self.k = eng, sem, 0, 0

    def mark(self, ins):
        ins.then_inc(self.sem, 1)
        self.k += 1

    def wait(self):
        self.eng.wait_ge(self.sem, self.base + self.k)

    def then_wait(self, ins):
        self.mark(ins)
        self.wait()

    @contextmanager
    def loop(self, n, per):
        start = self.base + self.k
        with self.eng.Fori(0, n) as i:
            self.base, self.k = start + i * per, 0
            yield i
            assert self.k == per, (self.k, per)
        self.base, self.k = start + n * per, 0


def build(nc, x, w_z, w_v, w_gates, w_o, w_ffn, w_ada, cols, rows, per_head, consts, window_bias, distance, out):
    with ExitStack() as ctx:
        def sb(name, shape, dt=F32):
            return ctx.enter_context(nc.sbuf_tensor(name, shape, dt))

        def sem(name):
            return ctx.enter_context(nc.semaphore(name))

        h_t = sb("h_t", [P, 2, KT, L], F32R)
        w_t = sb("w_t", [P, 2, 2, GT], F32R)
        y_t_at = nc.sbuf_base
        y_t = sb("y_t", [P, 2, 2, BT, L], F32R)
        raw = sb("raw", [P, 2, GT])
        region_a_at = nc.sbuf_base
        region_a = sb("region_a", [P, 8 * L])
        region_b = sb("region_b", [P, 8 * L])
        region_c = sb("region_c", [P, 2 * L])
        region_d = sb("region_d", [P, L])
        col_pack = sb("col_pack", [P, 62])
        head_pack = sb("head_pack", [P, 8])
        const = sb("const", [P, 5, P])
        ident_b = sb("ident_b", [P, P], BF16)
        tri_b = sb("tri_b", [P, P], BF16)
        silu_c = sb("silu_c", [P, KT])
        mod_col = sb("mod_col", [P, 4, KT])
        stat = sb("stat", [P, 3 * TT])
        root = sb("root", [P, 3 * TT])
        rstd = sb("rstd", [P, 3 * TT])
        diag = sb("diag", [P, 2, P])
        top8 = sb("top8", [P, TT - KB0, 8])
        mx = sb("mx", [P, 2, 4])
        neg = sb("neg", [P, 2, 4])
        den = sb("den", [P, 4, 4])
        rec = sb("rec", [P, 2, 4])
        sink_e = sb("sink_e", [P, 4, 4])
        eps = sb("eps", [P, 1])
        lf = sb("lf", [P, 3, TT * HEADS])
        stack_a = nc.alloc_sbuf_tensor_at("stack_a", [P, 4, L], F32R, offset=region_a_at)
        ya_back = nc.alloc_sbuf_tensor_at("ya_back", [P, BT, L], F32, offset=y_t_at + BT * L * 4)
        ps = ctx.enter_context(nc.psum_tensor("ps", [P, 8, HALF], F32))
        ya_dram = nc.dram_tensor("ya_dram", (P, BT, L), F32, kind="Internal").ap()
        key_dram = nc.dram_tensor("key_dram", (HD, 2, L), F32, kind="Internal").ap()
        mix_dram = nc.dram_tensor("mix_dram", (P, KT, L), F32, kind="Internal").ap()

        ident, tri, upper, ones, minus = (const[:, i, :] for i in range(5))
        c_col, g0_col, g2_col = col_pack[:, 0:8], col_pack[:, 8:16], col_pack[:, 16:24]
        bias_col = [col_pack[:, 24 + 8 * i:32 + 8 * i] for i in range(4)]
        conv_w = col_pack[:, 56:62].rearrange("p (c k) -> p c k", c=2)
        fox_b, sinks = head_pack[:, 0:4], head_pack[:, 4:8]
        h_hi, h_lo = h_t[:, 0], h_t[:, 1]
        xs = region_a[:, :].rearrange("p (t n) -> p t n", t=8)
        z = xs
        lg = [xs[:, 4], xs[:, 5]]
        pt = [xs[:, 6], xs[:, 7]]
        spare = xs[:, 3]
        conv_z = region_a[:, 4 * L:4 * L + L + 2]
        vn = region_b[:, 0:TT * VN].rearrange("p (t n) -> p t n", t=TT)
        sc_at, at = {}, TT * VN
        for b in range(KB0, TT):
            sc_at[b] = region_b[:, at:at + (b + 1) * P]
            at += (b + 1) * P
        y_tok = [region_b[:, at:at + BW], diag[:, :, :].rearrange("p a n -> p (a n)")]
        raw_v = region_b[:, TT * VN:TT * VN + KT * VN]
        ada_raw = [region_b[:, i * D:(i + 1) * D] for i in range(3)]
        ada_sum2 = region_b[:, TT * VN:TT * VN + 4 * D].rearrange("p (c n) -> p c n", c=4)
        x1 = region_b[:, :].rearrange("p (t n) -> p t n", t=8)
        ada_sum1 = region_c[:, :].rearrange("p (c n) -> p c n", c=2)
        forget = ada_sum1
        y_s = region_c[:, :].rearrange("p (c n) -> p c n", c=BT)
        g_row = [region_c[:, 0:L], region_c[:, L:2 * L]]
        h_tmp = region_d[:, :]
        sig = region_d[:, 0:HALF]
        prj = region_d[:, HALF:L]
        act2 = [sig, prj]

        def y_hi(buf):
            return y_t[:, buf, 0]

        def y_lo(buf):
            return y_t[:, buf, 1]

        vw = y_t[:, :, :, :, :].rearrange("p a b c n -> p (a b c n)")
        vw_hi_flat, vw_lo_flat = vw[:, 0:KT * VN], vw[:, 4 * L:4 * L + KT * VN]
        vw_hi, vw_lo = (v.rearrange("p (k n) -> p k n", k=KT) for v in (vw_hi_flat, vw_lo_flat))
        vw_half = [slice(i * KT // 2 * VN, (i + 1) * KT // 2 * VN) for i in range(2)]

        ys = [vw[:, i * L:(i + 1) * L] for i in range(8)]

        lo_c, lo_d = [region_c[:, i * L:(i + 1) * L] for i in range(2)], region_d[:, :]
        stacks = {T_IDX: ("q", (ys[0], ys[1]), (lo_c[0], lo_c[0])),
                  T_IDX + 1: ("q", (ys[2], ys[3]), (lo_c[1], lo_c[1])),
                  T_IDX + 2: ("keys of two", (ys[4], ys[6]), (ys[5], ys[7])),
                  T_FOX: ("q", (stack_a[:, 0], stack_a[:, 1]), (lo_d, lo_d)),
                  T_FOX + 1: ("q", (stack_a[:, 3], ys[0]), (lo_d, lo_d)),
                  T_FOX + 2: ("k", (ys[5], ys[7]), (stack_a[:, 2], stack_a[:, 2])),
                  T_FOX + 3: ("k", (ys[1], ys[2]), (ys[3], ys[3])),
                  T_DSA: ("q", (ys[0], ys[1]), (lo_c[0], lo_c[0])),
                  T_DSA + 1: ("q", (ys[2], ys[3]), (lo_c[1], lo_c[1]))}
        idx_keys = (ys[4], ys[4]), ys[5]
        dsa_keys = (stack_a[:, 0], stack_a[:, 0]), stack_a[:, 1]
        fox_keys = [(stacks[T_FOX + 2 + i][1], stacks[T_FOX + 2 + i][2][0]) for i in range(2)]
        stack_order = sorted(stacks)
        rows_of = [slice(0, HD), slice(HD, P)]

        def lo_halves(T):
            return 2 * sum(t < T for t in stack_order)

        s_pack = sem("s_pack")
        s_rows = sem("s_rows")
        s_xt = [sem(f"s_xt{t}") for t in range(TT)]
        s_ada = [sem(f"s_ada{i}") for i in range(3)]
        s_ada_used = sem("s_ada_used")
        s_raw = [sem("s_raw0"), sem("s_raw1")]
        s_rawv = [sem("s_rawv0"), sem("s_rawv1")]
        s_w_hi = sem("s_w_hi")
        s_w_lo = sem("s_w_lo")
        s_vw_hi = sem("s_vw_hi")
        s_vw_lo = [sem("s_vw_lo0"), sem("s_vw_lo1")]
        s_silu = sem("s_silu")
        s_mod = sem("s_mod")
        s_root = sem("s_root")
        s_norm = sem("s_norm")
        s_ht = sem("s_ht")
        s_hval = sem("s_hval")
        s_hval_act = sem("s_hval_act")
        pool_order = sem("pool_order")
        s_h_hi = sem("s_h_hi")
        s_h = sem("s_h")
        s_v = sem("s_v")
        s_vn = sem("s_vn")
        s_z = sem("s_z")
        s_zf = sem("s_zf")
        s_z_lo = sem("s_z_lo")
        s_moved = {T: sem(f"s_moved{T}") for T in stacks }
        s_key_out = sem("s_key_out")
        s_key_in = sem("s_key_in")
        s_ya_out = sem("s_ya_out")
        s_ya_in = sem("s_ya_in")
        s_s = sem("s_s")
        s_relu = sem("s_relu")
        s_score = sem("s_score")
        s_prod = sem("s_prod")
        s_conv = sem("s_conv")
        s_ya_hi = sem("s_ya_hi")
        s_ya = sem("s_ya")
        s_fabs = sem("s_fabs")
        s_fln = sem("s_fln")
        s_fu = sem("s_fu")
        s_fp = sem("s_fp")
        s_forget = sem("s_forget")
        s_logit = sem("s_logit")
        s_lg = sem("s_lg")
        s_neg = sem("s_neg")
        s_exp = sem("s_exp")
        s_t = sem("s_t")
        s_pt = sem("s_pt")
        s_pv = sem("s_pv")
        s_y_tok = sem("s_y_tok")
        s_turned = sem("s_turned")
        s_o_hi = sem("s_o_hi")
        s_of = sem("s_of")
        s_table = sem("s_table")
        s_ys_hi = sem("s_ys_hi")
        s_ys = sem("s_ys")
        s_mix = sem("s_mix")
        s_spill = sem("s_spill")
        s_refill = sem("s_refill")
        s_mix_hi = sem("s_mix_hi")
        s_mix_lo = sem("s_mix_lo")
        s_ot = sem("s_ot")
        s_oroot = sem("s_oroot")
        s_x1 = sem("s_x1")
        s_silu2 = sem("s_silu2")
        s_a = sem("s_a")
        s_a_hi = sem("s_a_hi")
        s_a_lo = sem("s_a_lo")
        s_y = sem("s_y")
        s_yf = sem("s_yf")
        s_zero = sem("s_zero")
        s_yroot = sem("s_yroot")
        s_y_norm = sem("s_y_norm")
        s_final = sem("s_final")
        s_out = sem("s_out")
        dve_order = sem("dve_order")
        act_order = sem("act_order")

        fox_units = [("fox", b, 2 * pair + j) for pair in range(2) for b in reversed(range(TT)) for j in range(2)]
        swa_units = [("swa", b, None) for b in range(TT)]
        dsa_units = [("dsa", b, h) for b in reversed(range(TT)) for h in range(HEADS)]
        units = fox_units + swa_units + dsa_units

        def group_of(u):
            kind, b, h = units[u]
            if kind == "fox":
                return O_FOX + h // 2 * TT + TT - 1 - b, h % 2 == 0, h % 2 == 1
            if kind == "swa":
                return O_SWA + b, True, True
            return O_DSA + TT - 1 - b, h == 0, h == HEADS - 1

        def group_bank(u):
            return ps[:, 2 + group_of(u)[0] % 2, :]

        def group_turned(u, y):
            kind, b, h = units[u]
            src = group_bank(u)[:, BW:2 * BW].rearrange("p (c n) -> p c n", c=BT)
            q = slice(b * P, (b + 1) * P)
            if kind == "fox":
                return y[:, h // 2, q], src[:, 0]
            return y[:, :, q], src

        def window_cols(ap, b):
            v = ap.rearrange("p (h n) -> p h n", h=HEADS)
            return v[:, :, P:2 * P] if b == 0 else v

        def logits_ps(u):
            return ps[:, 4 + 2 * (u % 2):6 + 2 * (u % 2), :].rearrange("p a n -> p (a n)")

        def z_dest(T, half):
            c = slice(half * HALF, (half + 1) * HALF)
            if T < T_FOX:
                return z[:, (0, 1, 2, 3, 0, 2)[T - T_CONV], c], 1.0
            if T < T_AFS:
                return z[:, T - T_SWA, c], HD ** -0.5 if T < T_SWA + 2 else 1.0
            assert False, T

        def wo_place(T):
            dt, half = (T - T_WO) % KT, int(T >= T_WO2)
            return dt, half, 6 * half + dt % 2

        def o_banks(t):
            b = 6 if t > TT // 2 and t % 2 else 4
            return ps[:, b:b + 2, :]

        def stack_scale(T):
            return HD ** -0.5 if stacks[T][0] == "q" and T >= T_FOX else 1.0

        def stack_parts(T):
            _, hi, lo = stacks[T]
            return list(zip(rows_of, hi, lo))

        def score_units(n):
            every = [(b, h) for b in range(KB0, TT) for h in range(HEADS)]
            last = 2 * (T_FOX - T_CONV) - 5
            upto = [len(every) * max(m, 0) // last for m in range(last + 1)] + [len(every)] * 5
            return [(i, *every[i]) for i in range(upto[n - 1] if n else 0, upto[n])]

        def gate_tiles(T):
            return T_AFS <= T < T_DSA or T_GD <= T < T_WO

        def width(T):
            return GT if gate_tiles(T) else D

        branch_buf = {"A": 0, "F": 1, "S": 0, "D": 1}
        afs = [("A", T_AFS), ("F", T_AFS + KT), ("S", T_AFS + 2 * KT)]

        block = ctx.enter_context(nc.Block())

        @block.sync
        def _(sp):
            sp.dma_start(col_pack[:, :], cols).then_inc(s_pack, 16)
            sp.dma_start(head_pack[:, :], per_head).then_inc(s_pack, 16)
            sp.dma_start(const[:, :, :], consts).then_inc(s_pack, 16)

            def ada_load(n, chunk, k):
                if n >= 3:
                    sp.wait_ge(s_ada_used, n - 2)
                sp.dma_start(ada_raw[n % 3], w_ada[chunk, k]).then_inc(s_ada[n % 3], 16)

            def tile_load(T, src, i=0, step=0):
                if T >= 2:
                    sp.wait_ge(s_w_lo, T - 1 + i * step)
                sp.dma_start(raw[:, T % 2, 0:src.shape[-1]], src).then_inc(s_raw[T % 2], 16)

            def x_load(t):
                sp.dma_start(xs[:, t], x[t * P:(t + 1) * P, :]).then_inc(s_xt[t], 16)

            for chunk in range(2):
                for k in range(KT):
                    ada_load(chunk * KT + k, chunk, k)
            x_load(0)
            x_load(1)
            for part, s in zip(vw_half, s_rawv):
                sp.dma_start(raw_v[:, part], w_v[:, part]).then_inc(s, 16)
            for t in range(2, TT):
                x_load(t)
            for T in range(T_AFS):
                tile_load(T, w_z[T])
                if T == T_CONV + 2:
                    sp.wait_ge(s_z_lo, lo_halves(T_CONV))
                    for i, place in enumerate((stacks[T_IDX + 2][1][1], stacks[T_IDX + 2][2][1])):
                        sp.dma_start(key_dram[:, i, :], place[rows_of[1]].bitcast(F32)).then_inc(s_key_out, 16)
                if T == T_FOX:
                    for ch in range(BT):
                        sp.wait_ge(s_conv, ch + 1)
                        sp.dma_start(ya_dram[:, ch, :], pt[ch]).then_inc(s_ya_out, 16)
            sp.wait_ge(s_moved[T_FOX + 1], 32)
            sp.dma_start(region_d[:, :], window_bias).then_inc(s_table, 16)
            for j in range(2):
                tile_load(T_AFS + j, w_gates[j])
            sp.wait_ge(s_of, O_SWA)
            sp.wait_ge(s_ya_out, 16 * BT)
            for ch in range(BT):
                sp.dma_start(ya_back[:, ch], ya_dram[:, ch, :]).then_inc(s_ya_in, 16)
            with sp.Fori(0, 3 * KT // 2 - 1) as i:
                for j in range(2):
                    tile_load(T_AFS + 2 + j, w_gates[i * 2 + (2 + j)], i, 2)
            tile_load(T_DSA, w_z[T_AFS])
            tile_load(T_DSA + 1, w_z[T_AFS + 1])
            for dt in range(KT):
                sp.wait_ge(s_mix, MIX0 + 2 * (2 * KT + dt + 1))
                sp.dma_start(mix_dram[:, dt, :], z[:, dt]).then_inc(s_spill, 16)
            sp.dma_start(region_d[:, :], distance).then_inc(s_table, 16)
            for j in range(2):
                tile_load(T_GD + j, w_gates[3 * KT + j])
            sp.wait_ge(s_of, O_DSA + TT)
            sp.wait_ge(s_spill, 16 * KT)
            for dt in range(KT):
                sp.dma_start(z[:, dt], mix_dram[:, dt, :]).then_inc(s_refill, 16)
            for k in range(KT):
                for j in range(4):
                    ada_load(2 * KT + 4 * k + j, 2 + j, k)
                T = T_GD + 2 + k
                tile_load(T, w_gates[3 * KT + T - T_GD] if T < T_WO else w_o[T - T_WO])
            sp.wait_ge(s_ada_used, 6 * KT)
            for j in range(2):
                sp.dma_start(ada_raw[1 + j], rows[j:j + 1, :].partition_broadcast(P)).then_inc(s_rows, 16)
                sp.dma_start(g_row[j], rows[2 + j:3 + j, :].partition_broadcast(P)).then_inc(s_rows, 16)
            for T in range(T_WO + 2, T_FFN):
                tile_load(T, w_o[(T - T_WO) % KT])
                if T == T_WO + 4:
                    sp.wait_ge(s_mod, 4)
                for t in range(2 * (T - T_WO - 4), 2 * (T - T_WO - 3)) if T_WO + 4 <= T < T_WO2 else ():
                    sp.dma_start(x1[:, t], x[t * P:(t + 1) * P, :]).then_inc(s_xt[t], 16)
            with sp.Fori(0, FG) as i:
                for j in range(6):
                    tile_load(T_FFN + j, w_ffn[i * 6 + j], i, 6)
            for t in range(TT):
                sp.wait_ge(s_final, t + 1)
                sp.dma_start(out[t * P:(t + 1) * P, :], x1[:, t]).then_inc(s_out, 16)
            sp.wait_ge(s_out, 16 * TT)

        @block.tensor
        def _(pe):
            def product(o, a_hi, a_lo, m_hi, m_lo, first, last):
                pe.matmul(o, a_hi, m_hi, start=first, stop=False)
                pe.matmul(o, a_hi, m_lo, start=False, stop=False)
                return pe.matmul(o, a_lo, m_hi, start=False, stop=last)

            def tile_half(o, slot, half, k0=0, n=KT, m_hi=h_hi, m_lo=h_lo, ready=None):
                for k in range(n):
                    if ready is not None:
                        pe.wait_ge(ready, k + 1)
                    w = slice((k0 + k) * P, (k0 + k + 1) * P)
                    c = slice(half * HALF, (half + 1) * HALF)
                    mm = product(o, w_t[:, slot, 0, w], w_t[:, slot, 1, w], m_hi[:, k, c], m_lo[:, k, c],
                                 k == 0, k == n - 1)
                return mm

            def turn_x(t):
                pe.wait_ge(s_norm, t + 1)
                if t >= 2:
                    pe.wait_ge(s_hval, 2 * (t - 1))
                for k in range(KT):
                    mm = pe.transpose(ps[:, 2 * (t % 2) + k // 4, (k % 4) * P:(k % 4 + 1) * P],
                                      xs[:, t, k * P:(k + 1) * P], ident)
                mm.then_inc(s_ht, 1)

            def norm_x1(t):
                pe.wait_ge(s_norm, TT + t + 1)
                pe.wait_ge(s_hval, 2 * TT + max(t - 1, 0))
                if t >= 2:
                    pe.wait_ge(s_hval_act, t - 1)
                for k in range(KT):
                    mm = pe.matmul(ps[:, 2 * (t % 2) + k // 4, (k % 4) * P:(k % 4 + 1) * P],
                                   x1[:, t, k * P:(k + 1) * P], diag[:, t % 2, :], start=True, stop=True)
                mm.then_inc(s_ht, 1)

            pe.wait_ge(s_pack, 48)
            for c in range(2):
                pe.wait_ge(s_ada_used, (c + 1) * KT)
                for k in range(KT):
                    mm = pe.matmul(ps[:, 5, c * KT + k:c * KT + k + 1], ada_sum1[:, c, k * P:(k + 1) * P],
                                   ones[:, 0:1], start=True, stop=True)
            mm.then_inc(s_mod, 1)

            def token_major(t):
                pe.wait_ge(s_h, 2 * (t + 1))
                if t >= 2:
                    pe.wait_ge(s_vn, t - 1)
                c = slice(t * P, (t + 1) * P)
                for k in range(KT):
                    if t == 0 and k == KT // 2:
                        pe.wait_ge(s_vw_lo[1], 1)
                    mm = product(ps[:, 4 + t % 2, 0:VN], h_hi[:, k, c], h_lo[:, k, c], vw_hi[:, k, :],
                                 vw_lo[:, k, :], k == 0, k == KT - 1)
                mm.then_inc(s_v, 1)

            for t in range(2):
                turn_x(t)
            pe.wait_ge(s_vw_lo[0], 1)
            pe.wait_ge(s_mod, 2)
            for t in range(2, TT):
                turn_x(t)
                token_major(t - 2)
            token_major(TT - 2)
            token_major(TT - 1)

            def z_half(T, half):
                e = 2 * T + half
                if half == 0:
                    pe.wait_ge(s_w_lo, T + 1)
                if e >= 2:
                    pe.wait_ge(s_zf, e - 1)
                if T - 1 in stacks:
                    pe.wait_ge(s_z_lo, lo_halves(T - 1) + half + 1)
                tile_half(ps[:, half, :], T % 2, half).then_inc(s_z, 1)

            def z_group(T0, n):
                for T in range(T0, T0 + n):
                    z_half(T, 0)
                    z_half(T, 1)

            def wo_tile(T):
                _, half, bank = wo_place(T)
                pe.wait_ge(s_w_lo, T + 1)
                pe.wait_ge(s_zf, 2 * (T - (T > T_WO)))
                tile_half(ps[:, bank, :], T % 2, half, ready=s_mix_lo if T == T_WO else None).then_inc(s_z, 2)

            def stack_product(o, Tq, keys_of, head, q, k):
                i = head % 2
                keys, keys_lo = keys_of
                queries, hi_rows = stacks[Tq][1][i], rows_of[i]
                pe.matmul(o, queries[:, q], keys[i][:, k], start=True, stop=False)
                return pe.matmul(o, queries[hi_rows, q], keys_lo[hi_rows, k], start=False, stop=True)

            pe.wait_ge(s_hval, 2 * TT)
            z_group(T_IDX, T_CONV - T_IDX)
            for n in range(2 * (T_FOX - T_CONV)):
                z_half(T_CONV + n // 2, n % 2)
                for r, b, h in score_units(n):
                    if r == 0:
                        pe.wait_ge(s_z_lo, lo_halves(T_CONV))
                        for T in range(T_IDX, T_CONV):
                            pe.wait_ge(s_moved[T], 32)
                        pe.wait_ge(s_vn, TT)
                    if r >= 2:
                        pe.wait_ge(s_relu, r - 1)
                    for c0 in range(0, (b + 1) * P, HALF):
                        c1 = min(c0 + HALF, (b + 1) * P)
                        mm = stack_product(logits_ps(r)[:, c0:c1], T_IDX + h // 2, idx_keys, h,
                                           slice(b * P, (b + 1) * P), slice(c0, c1))
                    mm.then_inc(s_s, 1)
            r = HEADS * (TT - KB0)

            def forget_sums(h0):
                for j in range(2):
                    pe.wait_ge(s_fu, h0 + j + 1)
                    if h0 == 0:
                        pe.wait_ge(s_relu, r)
                    for c in range(2):
                        mm = pe.matmul(ps[:, 4 + 2 * j + c, :], minus, lg[j][:, c * HALF:(c + 1) * HALF],
                                       start=True, stop=True)
                    mm.then_inc(s_fp, 1)

            def logits(u):
                kind, b, h = units[u]
                if u >= 2:
                    pe.wait_ge(s_lg, u - 1)
                o = logits_ps(u)
                q = slice(b * P, (b + 1) * P)
                if kind == "swa":
                    for hh in range(HEADS):
                        pp = slice((hh // 2) * HD, (hh // 2 + 1) * HD)
                        c0 = 0 if b else P
                        mm = pe.matmul(o[:, hh * 2 * P + c0:(hh + 1) * 2 * P], z[pp, hh % 2, q],
                                       z[pp, 2, (b - 1) * P + c0:(b + 1) * P], start=True, stop=True)
                else:
                    if u == U_DSA + 2:
                        pe.wait_ge(s_moved[T_DSA + 1], 32)
                    if kind == "fox":
                        Tq, keys_of = T_FOX + h // 2, fox_keys[h // 2]
                    else:
                        Tq, keys_of = T_DSA + h // 2, dsa_keys
                    masked = kind == "fox" or b < KB0
                    for c0 in range(0, (b + 1) * P, HALF):
                        c1 = min(c0 + HALF, (b + 1) * P)
                        here = masked and c1 == (b + 1) * P
                        mm = stack_product(o[:, c0:c1], Tq, keys_of, h, q, slice(c0, c1))
                        if here:
                            mm = pe.matmul(o[:, q], ident_b[:, :], tri_b[:, :], start=False, stop=True,
                                           skip_group_check=True)
                mm.then_inc(s_logit, 1)

            def turn(u):
                kind, b, h = units[u]
                if u in (U_FOX, U_DSA):
                    pe.wait_ge(s_z_lo, lo_halves(T_SWA if u == U_FOX else T_GD))
                pe.wait_ge(s_exp, u + 1)
                if u >= 1:
                    pe.wait_ge(s_pt, u)
                blocks = [2 * hh + c for hh in range(HEADS) for c in ((0, 1) if b else (1,))] \
                    if kind == "swa" else range(b + 1)
                for c in blocks:
                    mm = pe.transpose(ps[:, c // 4, (c % 4) * P:(c % 4 + 1) * P],
                                      lg[u % 2][:, c * P:(c + 1) * P], ident)
                mm.then_inc(s_t, 1)

            def values(u):
                kind, b, h = units[u]
                g, first, last = group_of(u)
                pe.wait_ge(s_pt, u + 1)
                if first and g >= 2:
                    pe.wait_ge(s_of, g - 1)
                bank = group_bank(u)
                if kind == "swa":
                    cs = (0, 1) if b else (1,)
                    parts = [(hh, [(2 * hh + c, b - 1 + c, VS + hh // 2 * HD) for c in cs]) for hh in range(HEADS)]
                elif kind == "fox":
                    parts = [(h % 2, [(c, c, VF + h * HD) for c in range(b + 1)])]
                else:
                    parts = [(h, [(c, c, VD) for c in range(b + 1)])]
                for col, terms in parts:
                    for n, (c, block_, v0) in enumerate(terms):
                        mm = pe.matmul(bank[:, col * HD:(col + 1) * HD], pt[u % 2][:, c * P:(c + 1) * P],
                                       vn[:, block_, v0:v0 + HD], start=n == 0, stop=n == len(terms) - 1)
                mm.then_inc(s_pv, 1)

            def turn_out(u):
                g, _, last = group_of(u)
                if not last:
                    return
                pe.wait_ge(s_y_tok, g + 1)
                for c in range(1 if units[u][0] == "fox" else BT):
                    mm = pe.transpose(group_bank(u)[:, BW + c * P:BW + (c + 1) * P],
                                      y_tok[g % 2][:, c * P:(c + 1) * P], ident)
                mm.then_inc(s_turned, 1)

            def attention(u0, n):
                end = u0 + n
                logits(u0)
                logits(u0 + 1)
                for u in range(u0, end):
                    if u + 2 < end:
                        logits(u + 2)
                    turn(u)
                    if u - 2 >= u0:
                        turn_out(u - 2)
                    if u > u0:
                        values(u - 1)
                turn_out(end - 2)
                values(end - 1)
                turn_out(end - 1)

            z_group(T_FOX, 2)
            forget_sums(0)
            z_group(T_FOX + 2, 2)
            pe.wait_ge(s_forget, 2)
            for T in (T_FOX, T_FOX + 2):
                pe.wait_ge(s_moved[T], 32)
            attention(U_FOX, 2 * TT)
            pe.wait_ge(s_pt, 2 * TT)
            z_group(T_SWA, 1)
            forget_sums(2)
            z_group(T_SWA + 1, 2)
            pe.wait_ge(s_forget, 4)
            pe.wait_ge(s_zf, 2 * T_AFS)
            for T in (T_FOX + 1, T_FOX + 3):
                pe.wait_ge(s_moved[T], 32)
            attention(U_FOX + 2 * TT, 2 * TT + TT)
            pe.wait_ge(s_pt, U_DSA)
            pe.wait_ge(s_of, O_DSA)

            def gate_pairs(T0, buf):
                with pe.Fori(0, KT // 2) as i:
                    for j in range(2):
                        pe.wait_ge(s_w_lo, i * 2 + (T0 + j + 1))
                        for half in range(2):
                            pe.wait_ge(s_zf, i * 4 + (2 * (T0 + j) + half - 1))
                            slot = (T0 + j) % 2
                            tile_half(ps[:, half, :], slot, half)
                            tile_half(ps[:, 2 + half, :], slot, half, KT, BT, y_hi(buf), y_lo(buf)) \
                                .then_inc(s_z, 1)

            pe.wait_ge(s_ya, 1)
            gate_pairs(T_AFS, 0)
            gate_pairs(T_AFS + KT, 1)
            pe.wait_ge(s_ys, 1)
            gate_pairs(T_AFS + 2 * KT, 0)
            z_group(T_DSA, T_GD - T_DSA)
            pe.wait_ge(s_moved[T_DSA], 32)
            pe.wait_ge(s_key_in, 64)
            attention(U_DSA, HEADS * TT)
            pe.wait_ge(s_pt, U_DSA + HEADS * TT)
            pe.wait_ge(s_of, O_DSA + TT)
            gate_pairs(T_GD, 1)

            pe.wait_ge(s_ada_used, 6 * KT)
            for j, chunk in ((0, 0), (1, 3)):
                for c in range(2):
                    mm = pe.matmul(ps[:, 4 + 2 * j + c, :], ones, ada_sum2[:, chunk, c * HALF:(c + 1) * HALF],
                                   start=True, stop=True)
            pe.wait_ge(s_zf, 2 * T_WO)
            for c in range(2):
                for k in range(KT):
                    mm = pe.matmul(ps[:, 3, c * KT + k:c * KT + k + 1], ada_sum2[:, 1 + c, k * P:(k + 1) * P],
                                   ones[:, 0:1], start=True, stop=True)
            mm.then_inc(s_mod, 1)

            for T in range(T_WO, T_WO2):
                wo_tile(T)
            pe.wait_ge(s_mod, 4)

            def turn_o(t):
                if t >= 1:
                    pe.wait_ge(s_x1, t if t <= TT // 2 else t - 1)
                for k in range(KT):
                    mm = pe.transpose(o_banks(t)[:, k // 4, (k % 4) * P:(k % 4 + 1) * P],
                                      z[:, k, t * P:(t + 1) * P], ident)
                mm.then_inc(s_ot, 1)

            for dt in range(KT):
                wo_tile(T_WO2 + dt)
                if dt == 0:
                    pe.wait_ge(s_zf, 2 * T_WO2)
                if dt % 2 == 0:
                    turn_o(dt // 2)
                elif dt >= 3:
                    norm_x1((dt - 3) // 2)
            pe.wait_ge(s_zf, 2 * T_FFN)
            turn_o(TT // 2)
            turn_o(TT // 2 + 1)
            for t in range(TT // 2 - 1, TT):
                if TT // 2 <= t < TT - 2:
                    turn_o(t + 2)
                norm_x1(t)

            pe.wait_ge(s_h, 3 * TT)
            with pe.Fori(0, FG) as i:
                for j in range(4):
                    f, up = j // 2, j % 2
                    pe.wait_ge(s_w_lo, i * 6 + (T_FFN + FFN_AT[j] + 1))
                    for half in range(2):
                        if j == 0 and half == 1:
                            pe.wait_ge(s_h, 4 * TT)
                        if f:
                            pe.wait_ge(s_a if up else s_silu2, i * 4 + (half + 1))
                        mm = tile_half(ps[:, 2 * up + half, :], (T_FFN + j) % 2, half)
                        mm.then_inc(s_z, 1)
                for q in range(2 * TT):
                    t, c = q // 2, q % 2
                    if q == 0:
                        pe.wait_ge(s_a_lo, i * 4 + 3)
                    if q == TT:
                        pe.wait_ge(s_a_lo, i * 4 + 4)
                    pe.wait_ge(s_yf, i * 16 + (q + 1))
                    for f in range(2):
                        tok = slice(t * P, (t + 1) * P)
                        cc = slice(c * HALF, (c + 1) * HALF)
                        mm = product(ps[:, 4 + q % 4, :], y_t[:, 0, 0, f, tok], y_t[:, 0, 1, f, tok],
                                     y_t[:, 1, 0, f, cc], y_t[:, 1, 1, f, cc], f == 0, f == 1)
                    mm.then_inc(s_y, 1)

        @block.scalar
        def _(act):
            order = Order(act, act_order)

            def split_hi(T, i=0, step=0, n=None):
                act.wait_ge(s_raw[T % 2], 16 * (T // 2 + 1) + i * (8 * step))
                if T >= 2:
                    act.wait_ge(s_z, 2 * (T - 1) + i * (2 * step))
                n = n or width(T)
                act.activation(w_t[:, T % 2, 0, 0:n], raw[:, T % 2, 0:n], ACT.Copy).then_inc(s_w_hi, 1)

            def z_half(T, half):
                if half == 0:
                    split_hi(T + 1)
                act.wait_ge(s_z, 2 * T + half + 1)
                if T in stacks:
                    c = slice(half * HALF, (half + 1) * HALF)
                    if T == T_FOX and half == 0:
                        act.wait_ge(s_conv, BT)
                    if T == T_FOX + 2 and half == 0:
                        act.wait_ge(s_key_out, 32)
                    for rows_, dst, _ in stack_parts(T):
                        ins = act.activation(dst[rows_, c], ps[rows_, half, :], ACT.Copy, scale=stack_scale(T))
                    ins.then_inc(s_zf, 1)
                    return
                if T == T_CONV + 4 and half == 0:
                    act.wait_ge(s_prod, 1)
                if T == T_CONV + 5 and half == 0:
                    act.wait_ge(s_prod, 2)
                dst, scale = z_dest(T, half)
                act.activation(dst, ps[:, half, :], ACT.Copy, scale=scale).then_inc(s_zf, 1)

            def z_group(T0, n):
                for T in range(T0, T0 + n):
                    z_half(T, 0)
                    z_half(T, 1)

            def h_hi_part(v):
                t, kh = (v // 2) % TT, v % 2
                if v < 2 * TT:
                    act.wait_ge(s_hval, v + 1)
                else:
                    act.wait_ge(s_hval_act if kh else s_hval, t + 1 + (0 if kh else 2 * TT))
                act.activation(h_hi[:, 4 * kh:4 * kh + 4, t * P:(t + 1) * P],
                               h_tmp[:, kh * HALF:(kh + 1) * HALF].rearrange("p (k n) -> p k n", k=4),
                               ACT.Copy).then_inc(s_h_hi, 1)

            def square_sum(src, col, squares):
                order.then_wait(act.activation(squares, src, ACT.Square, accum_out=stat[:, col:col + 1]))

            def banks(b):
                return ps[:, b:b + 2, :].rearrange("p a n -> p (a n)")

            def roots(c0, c1, s):
                act.activation(root[:, c0:c1], stat[:, c0:c1], ACT.Sqrt, scale=1.0 / D,
                               bias=eps[:, 0:1]).then_inc(s, 1)

            act.wait_ge(s_pack, 48)
            act.activation(silu_c[:, :], c_col, ACT.Silu).then_inc(s_silu, 1)
            act.wait_ge(s_mix, MIX0)

            def vw_hi_half(i):
                act.wait_ge(s_rawv[i], 16)
                act.activation(vw_hi_flat[:, vw_half[i]], raw_v[:, vw_half[i]], ACT.Copy).then_inc(s_vw_hi, 1)

            def x_root(t):
                act.wait_ge(s_xt[t], 16)
                square_sum(xs[:, t], t, banks(6))
                roots(t, t + 1, s_root)

            def v_out(t):
                act.wait_ge(s_v, t + 1)
                act.activation(vn[:, t, :], ps[:, 4 + t % 2, 0:VN], ACT.Copy).then_inc(s_vn, 1)

            x_root(0)
            x_root(1)
            vw_hi_half(0)
            vw_hi_half(1)
            x_root(2)
            for t in range(1, TT + 1):
                h_hi_part(2 * (t - 1))
                h_hi_part(2 * (t - 1) + 1)
                if t + 2 < TT:
                    x_root(t + 2)
                if t == 3:
                    split_hi(0)
                if t >= 3:
                    v_out(t - 3)
            v_out(TT - 2)
            v_out(TT - 1)
            act.wait_ge(s_fabs, 1)
            order.then_wait(act.activation(lf[:, 1, :], lf[:, 1, :], ACT.Exp, scale=-1.0))
            act.activation(lf[:, 1, :], lf[:, 1, :], ACT.Ln, bias=ones[:, 0:1]).then_inc(s_fln, 1)
            z_group(T_IDX, T_CONV - T_IDX)
            for half in range(2 * (T_FOX - T_CONV)):
                z_half(T_CONV + half // 2, half % 2)
                for r, b, h in score_units(half):
                    n = (b + 1) * P
                    act.wait_ge(s_s, r + 1)
                    if r >= 2:
                        act.wait_ge(s_score, r - 1)
                    act.activation(lg[r % 2][:, 0:n], logits_ps(r)[:, 0:n], ACT.Relu).then_inc(s_relu, 1)
            z_group(T_FOX, T_SWA - T_FOX)

            def group_hi(u):
                g, _, last = group_of(u)
                if not last or units[u][0] == "swa":
                    return
                act.wait_ge(s_turned, g + 1)
                dst, src = group_turned(u, y_hi(1))
                act.activation(dst, src, ACT.Copy).then_inc(s_o_hi, 1)

            def exponentials(u):
                kind, b, h = units[u]
                g, first, _ = group_of(u)
                s = u % 2
                act.wait_ge(s_neg, u + 1)
                if first and g >= 4:
                    act.wait_ge(s_y_tok, g - 3)
                if kind == "swa":
                    w = window_cols(lg[s], b)
                    for hh in range(HEADS):
                        act.activation(w[:, hh], w[:, hh], ACT.Exp, bias=neg[:, s, hh:hh + 1],
                                       accum_out=den[:, g % 4, hh:hh + 1])
                    act.activation(sink_e[:, u % 4, :], sink_e[:, u % 4, :], ACT.Exp).then_inc(s_exp, 1)
                else:
                    w = lg[s][:, 0:(b + 1) * P]
                    col = h % 2 if kind == "fox" else h
                    act.activation(w, w, ACT.Exp, bias=neg[:, s, 0:1],
                                   accum_out=den[:, g % 4, col:col + 1]).then_inc(s_exp, 1)

            def attention(u0, n):
                end = u0 + n
                exponentials(u0)
                for u in range(u0, end):
                    kind, b, h = units[u]
                    if u + 1 < end:
                        exponentials(u + 1)
                    act.wait_ge(s_t, u + 1)
                    if u >= u0 + 2:
                        act.wait_ge(s_pv, u - 1)
                    bank = ps[:, 0:2, :].rearrange("p a n -> p (a n)")
                    if kind == "swa":
                        dst, src = window_cols(pt[u % 2], b), window_cols(bank, b)
                    else:
                        dst, src = pt[u % 2][:, 0:(b + 1) * P], bank[:, 0:(b + 1) * P]
                    act.activation(dst, src, ACT.Copy).then_inc(s_pt, 1)
                    if u >= u0 + 2:
                        group_hi(u - 2)
                group_hi(end - 2)
                group_hi(end - 1)

            act.wait_ge(s_ya_out, 16 * BT)
            attention(U_FOX, 2 * TT)
            z_group(T_SWA, T_AFS - T_SWA)
            attention(U_FOX + 2 * TT, 2 * TT + TT)
            act.wait_ge(s_ya_in, 16 * BT)
            act.activation(y_hi(0), ya_back[:, :, :], ACT.Copy).then_inc(s_ya_hi, 1)

            def gate_pairs(T0, m0):
                with act.Fori(0, KT // 2) as i:
                    for j in range(2):
                        T = T0 + j
                        split_hi(T + 1, i, 2, GT)
                        for half in range(2):
                            act.wait_ge(s_z, i * 4 + (2 * T + half + 1))
                            act.wait_ge(s_mix, i * 4 + (MIX0 + m0 + 2 * j + half))
                            act.activation(sig, ps[:, half, :], ACT.Sigmoid)
                            act.activation(prj, ps[:, 2 + half, :], ACT.Copy).then_inc(s_zf, 1)

            gate_pairs(T_AFS, 0)
            act.activation(y_hi(0), y_s, ACT.Copy).then_inc(s_ys_hi, 1)
            gate_pairs(T_AFS + KT, 2 * KT)
            gate_pairs(T_AFS + 2 * KT, 4 * KT)
            z_group(T_DSA, T_GD - T_DSA)
            attention(U_DSA, HEADS * TT)
            gate_pairs(T_GD, 6 * KT)
            for dt in range(KT):
                act.wait_ge(s_mix, MIX0 + 6 * KT + 2 * (dt + 1))
                act.activation(h_hi[:, dt], z[:, dt], ACT.Copy).then_inc(s_mix_hi, 1)

            def wo_tile(T):
                split_hi(T + 1)
                dt, half, bank = wo_place(T)
                act.wait_ge(s_z, 2 * T + 2)
                act.activation(z[:, dt, half * HALF:(half + 1) * HALF], ps[:, bank, :], ACT.Copy).then_inc(s_zf, 2)

            def o_root(t):
                act.wait_ge(s_ot, t + 1)
                square_sum(o_banks(t).rearrange("p a n -> p (a n)"), TT + t, ys[0])
                roots(TT + t, TT + t + 1, s_oroot)

            def x1_root(t):
                act.wait_ge(s_x1, t + 1)
                square_sum(x1[:, t], 2 * TT + t, ys[0])
                roots(2 * TT + t, 2 * TT + t + 1, s_root)

            def h_values(t):
                act.wait_ge(s_ht, TT + t + 1)
                act.wait_ge(s_h, 2 * (TT + t))
                for kk in range(KT // 2, KT):
                    ins = act.activation(h_tmp[:, kk * P:(kk + 1) * P],
                                         ps[:, 2 * (t % 2) + 1, (kk - KT // 2) * P:(kk - KT // 2 + 1) * P],
                                         ACT.Identity, scale=mod_col[:, 3, kk:kk + 1], bias=mod_col[:, 2, kk:kk + 1])
                ins.then_inc(s_hval_act, 1)

            def second_h(t):
                h_values(t)
                h_hi_part(2 * (TT + t))
                h_hi_part(2 * (TT + t) + 1)

            for T in range(T_WO, T_WO2):
                wo_tile(T)
            for dt in range(KT):
                wo_tile(T_WO2 + dt)
                if dt % 2 == 0:
                    o_root(dt // 2)
                else:
                    x1_root(dt // 2)
                    if dt >= 3:
                        second_h((dt - 3) // 2)
            o_root(TT // 2)
            for t in range(TT // 2, TT + 1):
                if t + 1 < TT:
                    o_root(t + 1)
                if t < TT:
                    x1_root(t)
                second_h(t - 1)

            def ffn_group(i, last):
                def split(m):
                    T = T_FFN + m
                    act.wait_ge(s_raw[T % 2], 16 * (T // 2 + 1) + i * 48)
                    if m in (2, 4):
                        dst = y_hi(1)[:, m // 2 - 1, :]
                    else:
                        j = {0: 0, 1: 1, 3: 2, 5: 3, 6: 4}[m]
                        act.wait_ge(s_z, i * 8 + (2 * (T_FFN + j) - 2))
                        dst = w_t[:, (T_FFN + j) % 2, 0, 0:D]
                    act.activation(dst, raw[:, T % 2, 0:D], ACT.Copy).then_inc(s_w_hi, 1)

                for j in range(4):
                    for m in FFN_AHEAD[j]:
                        if m < 6 or not last:
                            split(m)
                    f, up = j // 2, j % 2
                    for half in range(2):
                        n = 2 * f + half
                        c = slice(half * HALF, (half + 1) * HALF)
                        if up:
                            act.wait_ge(s_a, i * 4 + (n + 1))
                            act.activation(y_hi(0)[:, f, c], act2[half], ACT.Copy).then_inc(s_a_hi, 1)
                        else:
                            act.wait_ge(s_z, i * 8 + (2 * (T_FFN + j) + half + 1))
                            if n == 0:
                                act.wait_ge(s_h, 4 * TT)
                            if f:
                                act.wait_ge(s_a_lo, i * 4 + (half + 1))
                            act.activation(act2[half], ps[:, half, :], ACT.Silu).then_inc(s_silu2, 1)

            with act.Fori(0, FG - 1) as i:
                ffn_group(i, False)
            ffn_group(FG - 1, True)
            for t in range(TT):
                act.wait_ge(s_yf, 4 + 16 * (FG - 1) + 2 * (t + 1))
                square_sum(z[:, t], t, banks(0))
                roots(t, t + 1, s_yroot)

        @block.gpsimd
        def _(pool):
            order = Order(pool, pool_order)
            pool.memset(eps[:, :], EPS).then_inc(s_mix, 1)

            def split_lo(T, i=0, step=0, n=None):
                n = n or width(T)
                pool.wait_ge(s_w_hi, T + 1 + i * step)
                pool.tensor_tensor(w_t[:, T % 2, 1, 0:n], raw[:, T % 2, 0:n],
                                   w_t[:, T % 2, 0, 0:n].bitcast(F32), ALU.subtract).then_inc(s_w_lo, 1)

            def h_lo_part(v):
                pool.wait_ge(s_h_hi, v + 1)
                t, kh = (v // 2) % TT, v % 2
                at = (slice(None), slice(4 * kh, 4 * kh + 4), slice(t * P, (t + 1) * P))
                pool.tensor_tensor(h_lo[at], h_tmp[:, kh * HALF:(kh + 1) * HALF].rearrange("p (k n) -> p k n", k=4),
                                   h_hi[at].bitcast(F32), ALU.subtract).then_inc(s_h, 1)

            part = vw_half[0]
            pool.wait_ge(s_vw_hi, 1)
            pool.tensor_tensor(vw_lo_flat[:, part], raw_v[:, part], vw_hi_flat[:, part].bitcast(F32),
                               ALU.subtract).then_inc(s_vw_lo[0], 1)
            for t in range(TT):
                h_lo_part(2 * t)
                h_lo_part(2 * t + 1)
                if t == 2:
                    split_lo(0)

            def stack_moves(T):
                kind, hi, lo = stacks[T]
                if kind == "k":
                    pool.wait_ge(s_zf, 2 * T + 2)
                    moves = [(hi[i], hi[i], i) for i in range(2)]
                else:
                    pool.wait_ge(s_z_lo, lo_halves(T) + 2)
                    moves = [(hi[0], lo[0], 0), (hi[1], lo[1], 1)] if kind == "q" else [(p, p, 0) for p in (hi[0], lo[0])]
                for dst, src, i in moves:
                    pool.dma_start(dst[rows_of[1 - i]], src[rows_of[i]]).then_inc(s_moved[T], 16)

            for T in range(1, T_AFS + 1):
                split_lo(T)
                if T - 1 in s_moved:
                    stack_moves(T - 1)

            def gate_pairs(T0, first):
                with order.loop(KT // 2, 0 if first else 4) as i:
                    for j in range(2):
                        T = T0 + j
                        split_lo(T + 1, i, 2, GT)
                        for half in range(2):
                            c = slice(half * HALF, (half + 1) * HALF)
                            pool.wait_ge(s_zf, i * 4 + (2 * T + half + 1))
                            mix = z[:, i * 2 + j, c]
                            if first:
                                pool.tensor_tensor(mix, sig, prj, ALU.mult).then_inc(s_mix, 1)
                            else:
                                order.then_wait(pool.tensor_tensor(sig, sig, prj, ALU.mult))
                                pool.tensor_tensor(mix, mix, sig, ALU.add).then_inc(s_mix, 1)

            pool.wait_ge(s_ya_hi, 1)
            pool.tensor_tensor(y_lo(0), ya_back[:, :, :], y_hi(0).bitcast(F32), ALU.subtract).then_inc(s_ya, 1)
            gate_pairs(T_AFS, True)
            pool.wait_ge(s_ys_hi, 1)
            pool.tensor_tensor(y_lo(0), y_s, y_hi(0).bitcast(F32), ALU.subtract).then_inc(s_ys, 1)
            pool.wait_ge(s_mix, MIX0 + 2 * KT)
            gate_pairs(T_AFS + KT, False)
            pool.wait_ge(s_mix, MIX0 + 4 * KT)
            gate_pairs(T_AFS + 2 * KT, False)
            for T in range(T_DSA + 1, T_GD + 1):
                split_lo(T)
                if T == T_DSA + 1:
                    pool.wait_ge(s_key_out, 32)
                    pool.wait_ge(s_spill, 16 * KT)
                    for i, dst in enumerate((dsa_keys[0][0], dsa_keys[1])):
                        for half_rows in rows_of:
                            pool.dma_start(dst[half_rows], key_dram[:, i, :]).then_inc(s_key_in, 16)
                if T - 1 in s_moved:
                    stack_moves(T - 1)
            pool.wait_ge(s_refill, 16 * KT)
            gate_pairs(T_GD, False)
            for T in range(T_WO, T_FFN):
                split_lo(T + 1)
                dt = T - T_WO2
                if dt >= 3 and dt % 2:
                    for v in range(dt - 3, dt - 1):
                        h_lo_part(2 * TT + v)
            for v in range(2 * TT + KT - 2, 4 * TT):
                h_lo_part(v)

            def ffn_group(i, last):
                def split(m):
                    T = T_FFN + m
                    pool.wait_ge(s_w_hi, i * 6 + (T + 1))
                    if m in (2, 4):
                        hi, lo = y_hi(1)[:, m // 2 - 1, :], y_lo(1)[:, m // 2 - 1, :]
                    else:
                        slot = (T_FFN + {0: 0, 1: 1, 3: 2, 5: 3, 6: 4}[m]) % 2
                        hi, lo = w_t[:, slot, 0, 0:D], w_t[:, slot, 1, 0:D]
                    pool.tensor_tensor(lo, raw[:, T % 2, 0:D], hi.bitcast(F32), ALU.subtract).then_inc(s_w_lo, 1)

                for j in range(4):
                    for m in FFN_AHEAD[j]:
                        if m < 6 or not last:
                            split(m)
                    for half in range(2) if j in (1, 3) else ():
                        f = j // 2
                        c = slice(half * HALF, (half + 1) * HALF)
                        pool.wait_ge(s_a_hi, i * 4 + (2 * f + half + 1))
                        pool.tensor_tensor(y_lo(0)[:, f, c], act2[half], y_hi(0)[:, f, c].bitcast(F32),
                                           ALU.subtract).then_inc(s_a_lo, 1)

            with pool.Fori(0, FG - 1) as i:
                ffn_group(i, False)
            ffn_group(FG - 1, True)
            for t in range(TT - 1):
                pool.wait_ge(s_y_norm, t + 1)
                pool.tensor_tensor(x1[:, t], x1[:, t], z[:, t], ALU.add).then_inc(s_final, 1)

        @block.vector
        def _(dve):
            order = Order(dve, dve_order)
            dve.wait_ge(s_pack, 48)
            dve.tensor_copy(ident_b[:, :], ident)
            order.mark(dve.tensor_copy(tri_b[:, :], tri))

            def ada(n, k, dst):
                dve.wait_ge(s_ada[n % 3], 16 * (n // 3 + 1))
                src, s = ada_raw[n % 3], silu_c[:, k:k + 1]
                if k == 0:
                    ins = dve.tensor_scalar(dst, src, s, None, ALU.mult)
                else:
                    dve.wait_ge(s_ada_used, n - (0 if n < 2 * KT else 3))
                    ins = dve.scalar_tensor_tensor(dst, src, s, dst, ALU.mult, ALU.add)
                ins.then_inc(s_ada_used, 1)

            def normed_x(t):
                dve.wait_ge(s_root, t + 1)
                order.then_wait(dve.reciprocal(rstd[:, t:t + 1], root[:, t:t + 1]))
                dve.tensor_scalar(xs[:, t], xs[:, t], rstd[:, t:t + 1], None, ALU.mult).then_inc(s_norm, 1)

            dve.wait_ge(s_silu, 1)
            for chunk in range(2):
                for k in range(KT):
                    ada(chunk * KT + k, k, ada_sum1[:, chunk])
            normed_x(0)

            def mod_columns(at, i, g):
                dve.tensor_tensor(mod_col[:, i, :], at[:, 0:KT], bias_col[i], ALU.add)
                order.then_wait(dve.tensor_tensor(mod_col[:, i + 1, :], at[:, KT:2 * KT], bias_col[i + 1], ALU.add))
                return dve.scalar_tensor_tensor(mod_col[:, i + 1, :], mod_col[:, i + 1, :], 1.0, g, ALU.add, ALU.mult)

            dve.wait_ge(s_mod, 1)
            mod_columns(ps[:, 5, :], 0, g0_col).then_inc(s_mod, 1)
            dve.wait_ge(s_mod, 2)

            def make_diag(t, col):
                if t >= 2:
                    dve.wait_ge(s_ht, TT + t - 1)
                dve.tensor_scalar(diag[:, t % 2, :], ident, rstd[:, col:col + 1], None, ALU.mult) \
                   .then_inc(s_norm, 1)

            def h_values(count, i):
                dve.wait_ge(s_ht, count + 1)
                for kh in range(2 if count < TT else 1):
                    v = 2 * count + kh
                    if v >= 2:
                        dve.wait_ge(s_h, v - 1)
                    for k in range(4):
                        kk = 4 * kh + k
                        ins = dve.tensor_scalar(h_tmp[:, kk * P:(kk + 1) * P],
                                                ps[:, 2 * (count % 2) + kh, k * P:(k + 1) * P],
                                                mod_col[:, i + 1, kk:kk + 1], mod_col[:, i, kk:kk + 1],
                                                ALU.mult, ALU.add)
                    ins.then_inc(s_hval, 1)

            normed_x(1)
            for t in range(TT):
                h_values(t, 0)
                if t == 0:
                    part = vw_half[1]
                    dve.wait_ge(s_vw_hi, 2)
                    dve.tensor_tensor(vw_lo_flat[:, part], raw_v[:, part], vw_hi_flat[:, part].bitcast(F32),
                                      ALU.subtract).then_inc(s_vw_lo[1], 1)
                if t + 2 < TT:
                    normed_x(t + 2)

            dve.wait_ge(s_vn, TT)
            f3, fa, fe = (lf[:, i, :].rearrange("p (t h) -> p t h", t=TT) for i in (0, 1, 2))
            order.then_wait(dve.tensor_tensor(f3, vn[:, :, VFF:VFF + HEADS],
                                              fox_b.unsqueeze(1).broadcast_to((P, TT, HEADS)), ALU.add))
            dve.scalar_tensor_tensor(lf[:, 1, :], lf[:, 0, :], -1.0, lf[:, 0, :], ALU.mult, ALU.max) \
               .then_inc(s_fabs, 1)
            dve.wait_ge(s_fln, 1)
            order.then_wait(dve.scalar_tensor_tensor(lf[:, 2, :], lf[:, 0, :], 0.0, lf[:, 1, :], ALU.min,
                                                     ALU.subtract))

            def stack_lo_half(T, half):
                c = slice(half * HALF, (half + 1) * HALF)
                dve.wait_ge(s_zf, 2 * T + half + 1)
                if T == T_FOX + 1 and half == 0:
                    dve.wait_ge(s_moved[T_FOX], 32)
                for rows_, hi, lo in stack_parts(T):
                    ins = dve.scalar_tensor_tensor(lo[rows_, c], ps[rows_, half, :], stack_scale(T),
                                                   hi[rows_, c].bitcast(F32), ALU.mult, ALU.subtract)
                ins.then_inc(s_z_lo, 1)

            def stack_lo(T):
                for half in range(2):
                    stack_lo_half(T, half)

            for T in range(T_IDX, T_CONV):
                stack_lo(T)

            def top_k(blocks, n):
                order.wait()
                for b in blocks:
                    rounds_done[b] += n
                with dve.Fori(0, n):
                    for i, b in enumerate(blocks):
                        dve.max(top8[:, i, :], sc_at[b])
                    dve.drain()
                    for i, b in enumerate(blocks):
                        dve.match_replace(sc_at[b], top8[:, i, :], sc_at[b], TAKEN)
                    dve.drain()

            rounds_done = dict.fromkeys(range(KB0, TT), 0)
            rounds = TOPK // 8

            r = 0
            for b in range(KB0, TT):
                n = (b + 1) * P
                for h in range(HEADS):
                    dve.wait_ge(s_relu, r + 1)
                    w = vn[:, b, VWI + h:VWI + h + 1]
                    if h == 0:
                        ins = dve.tensor_scalar(sc_at[b], lg[r % 2][:, 0:n], w, None, ALU.mult)
                    else:
                        dve.wait_ge(s_score, r)
                        ins = dve.scalar_tensor_tensor(sc_at[b], lg[r % 2][:, 0:n], w, sc_at[b], ALU.mult, ALU.add)
                    ins.then_inc(s_score, 1)
                    r += 1
                dve.wait_ge(s_score, r)
                order.mark(dve.tensor_tensor(sc_at[b][:, b * P:n], sc_at[b][:, b * P:n], tri, ALU.add))
                if KB0 < b < TT - 1:
                    top_k([KB0], SCORE_ROUNDS)

            order.mark(dve.memset(conv_z[:, 0:2], 0.0))
            for c in range(BT):
                dve.wait_ge(s_zf, 2 * (T_CONV + 2 * c + 2))
                dve.tensor_tensor(conv_z[:, 2:L + 2], z[:, 2 * c], z[:, 2 * c + 1], ALU.mult).then_inc(s_prod, 1)
                dve.wait_ge(s_prod, c + 1)
                order.wait()
                order.then_wait(dve.tensor_scalar(pt[c], conv_z[:, 0:L], conv_w[:, c, 0:1], None, ALU.mult))
                for k in (1, 2):
                    order.then_wait(dve.scalar_tensor_tensor(pt[c], conv_z[:, k:L + k], conv_w[:, c, k:k + 1],
                                                             pt[c], ALU.mult, ALU.add))
            for c in range(BT):
                dve.wait_ge(s_zf, 2 * (T_CONV + 5 + c))
                dve.tensor_tensor(pt[c], pt[c], z[:, 2 * c], ALU.mult).then_inc(s_conv, 1)
            def forget_spread(h0):
                for j in range(2):
                    spread = lg[j].rearrange("p (t n) -> p t n", t=TT)
                    dve.tensor_tensor(spread, upper.unsqueeze(1).broadcast_to((P, TT, P)),
                                      fe[:, :, h0 + j:h0 + j + 1].broadcast_to((P, TT, P)), ALU.mult) \
                       .then_inc(s_fu, 1)

            def forget_sums(h0):
                for j in range(2):
                    dve.wait_ge(s_fp, h0 + j + 1)
                    for b in range(TT):
                        src = ps[:, 4 + 2 * j + b // 4, (b % 4) * P:(b % 4 + 1) * P]
                        dst = forget[:, j, b * P:(b + 1) * P]
                        if b == 0:
                            ins = dve.tensor_copy(dst, src)
                        else:
                            ins = dve.tensor_scalar(dst, src, forget[:, j, b * P - 1:b * P], None, ALU.add)
                        if b < TT - 1:
                            order.then_wait(ins)
                    ins.then_inc(s_forget, 1)
                dve.wait_ge(s_forget, h0 + 2)

            def dsa_bias(u):
                _, b, h = units[u]
                n = (b + 1) * P
                slope = 2.0 ** -(HEADS + 1 + h)
                dist = region_d[:, L - n:L]
                if b < KB0:
                    order.mark(dve.tensor_scalar(spare[:, 0:n], dist, slope, None, ALU.mult))
                else:
                    order.mark(dve.scalar_tensor_tensor(spare[:, 0:n], dist, slope, sc_at[b], ALU.mult, ALU.add))

            def group_norm(u):
                kind, b, h = units[u]
                g, _, last = group_of(u)
                if not last:
                    return
                nh = 2 if kind == "fox" else HEADS
                dve.wait_ge(s_pv, u + 1)
                d, r = den[:, g % 4, 0:nh], rec[:, g % 2, 0:nh]
                if kind == "swa":
                    order.then_wait(dve.tensor_tensor(d, d, sink_e[:, u % 4, :], ALU.add))
                order.then_wait(dve.reciprocal(r, d))
                if g >= 2:
                    dve.wait_ge(s_turned, g - 1)
                dve.tensor_tensor(y_tok[g % 2][:, 0:nh * HD].rearrange("p (h d) -> p h d", h=nh),
                                  group_bank(u)[:, 0:nh * HD].rearrange("p (h d) -> p h d", h=nh),
                                  r.unsqueeze(2).broadcast_to((P, nh, HD)), ALU.mult).then_inc(s_y_tok, 1)

            def group_lo(u):
                kind, b, h = units[u]
                g, _, last = group_of(u)
                if not last:
                    return
                if kind == "swa":
                    dve.wait_ge(s_turned, g + 1)
                    dst, src = group_turned(u, y_s)
                    dve.tensor_copy(dst, src).then_inc(s_of, 1)
                else:
                    dve.wait_ge(s_o_hi, (g if kind == "fox" else g - TT) + 1)
                    dst, src = group_turned(u, y_lo(1))
                    hi, _ = group_turned(u, y_hi(1))
                    dve.tensor_tensor(dst, src, hi.bitcast(F32), ALU.subtract).then_inc(s_of, 1)

            def biased(u):
                kind, b, h = units[u]
                s, w = u % 2, (b + 1) * P
                o = logits_ps(u)
                dve.wait_ge(s_logit, u + 1)
                if u >= 2:
                    dve.wait_ge(s_t, u - 1)
                if kind == "swa":
                    for hh in range(HEADS):
                        ins = dve.tensor_tensor_reduce(
                            window_cols(lg[s], b)[:, hh], window_cols(o, b)[:, hh],
                            window_cols(region_d[:, :], b)[:, hh], 1.0, TAKEN, ALU.add, ALU.max,
                            mx[:, s, hh:hh + 1])
                    ins.then_inc(s_lg, 1)
                    dve.wait_ge(s_lg, u + 1)
                    order.then_wait(dve.tensor_tensor(mx[:, s, :], mx[:, s, :], sinks, ALU.max))
                    order.then_wait(dve.tensor_scalar(neg[:, s, :], mx[:, s, :], -1.0, None, ALU.mult))
                    dve.tensor_tensor(sink_e[:, u % 4, :], sinks, neg[:, s, :], ALU.add).then_inc(s_neg, 1)
                    return
                if kind == "dsa":
                    order.wait()
                bias = spare[:, 0:w] if kind == "dsa" else forget[:, h % 2, 0:w]
                dve.tensor_tensor_reduce(lg[s][:, 0:w], o[:, 0:w], bias, 1.0, TAKEN, ALU.add, ALU.max,
                                         mx[:, s, 0:1]).then_inc(s_lg, 1)
                dve.wait_ge(s_lg, u + 1)
                dve.tensor_scalar(neg[:, s, 0:1], mx[:, s, 0:1], -1.0, None, ALU.mult).then_inc(s_neg, 1)

            def attention(u0, n):
                end = u0 + n
                dsa = units[u0][0] == "dsa"
                if dsa:
                    dsa_bias(u0)
                biased(u0)
                for u in range(u0, end):
                    if u + 1 < end:
                        if dsa:
                            dsa_bias(u + 1)
                        biased(u + 1)
                    if u >= u0 + 2:
                        group_norm(u - 2)
                    if u >= u0 + 3:
                        group_lo(u - 3)
                group_norm(end - 2)
                group_lo(end - 3)
                group_norm(end - 1)
                group_lo(end - 2)
                group_lo(end - 1)

            forget_spread(0)
            for T in range(T_FOX, T_SWA):
                stack_lo(T)
                if T == T_FOX + 1:
                    forget_sums(0)
            attention(U_FOX, 2 * TT)
            dve.wait_ge(s_t, 2 * TT)
            forget_spread(2)
            top_k([KB0], SWA_ROUNDS[0])
            forget_sums(2)
            top_k([KB0], SWA_ROUNDS[1])
            dve.wait_ge(s_table, 16)
            attention(U_FOX + 2 * TT, 2 * TT + TT)

            top_k(range(KB0, TT), rounds - rounds_done[KB0])
            top_k(range(KB0 + 1, TT), rounds - rounds_done[TT - 1])
            assert all(n == rounds for n in rounds_done.values())
            for b in range(KB0, TT):
                order.mark(dve.tensor_scalar(sc_at[b], sc_at[b], TAKEN / 2, -BIG, ALU.is_gt, ALU.mult))
            for T in range(T_DSA, T_GD):
                stack_lo(T)
            order.wait()
            dve.wait_ge(s_table, 32)
            dve.wait_ge(s_spill, 16 * KT)
            attention(U_DSA, HEADS * TT)

            for k in range(KT):
                for j in range(4):
                    ada(2 * KT + 4 * k + j, k, ada_sum2[:, j])
            for dt in range(KT):
                dve.wait_ge(s_mix_hi, dt + 1)
                dve.tensor_tensor(h_lo[:, dt], z[:, dt], h_hi[:, dt].bitcast(F32), ALU.subtract).then_inc(s_mix_lo, 1)
            dve.wait_ge(s_rows, 64)
            dve.wait_ge(s_mod, 3)
            for j in range(2):
                sums = ps[:, 4 + 2 * j:6 + 2 * j, :].rearrange("p a n -> p (a n)")
                order.then_wait(dve.tensor_tensor(ada_raw[1 + j], sums, ada_raw[1 + j], ALU.add))
                order.mark(dve.tensor_tensor(g_row[j], ada_raw[1 + j], g_row[j], ALU.mult))
            mod_columns(ps[:, 3, :], 2, g2_col).then_inc(s_mod, 1)
            dve.wait_ge(s_mod, 4)
            for t in range(TT + 1):
                if t < TT:
                    dve.wait_ge(s_oroot, t + 1)
                    dve.wait_ge(s_xt[t], 32)
                    c, o = TT + t, o_banks(t).rearrange("p a n -> p (a n)")
                    order.then_wait(dve.reciprocal(rstd[:, c:c + 1], root[:, c:c + 1]))
                    order.then_wait(dve.scalar_tensor_tensor(o, o, rstd[:, c:c + 1], g_row[0], ALU.mult, ALU.mult))
                    dve.tensor_tensor(x1[:, t], o, x1[:, t], ALU.add).then_inc(s_x1, 1)
                if t >= 1:
                    h_values(TT + t - 1, 2)
                if t < TT:
                    dve.wait_ge(s_root, TT + t + 1)
                    c = 2 * TT + t
                    order.then_wait(dve.reciprocal(rstd[:, c:c + 1], root[:, c:c + 1]))
                    make_diag(t, c)

            dve.wait_ge(s_ot, TT)
            for q in range(4):
                dve.memset(region_a[:, q * 2 * L:(q + 1) * 2 * L], 0.0).then_inc(s_yf, 1)
            dve.wait_ge(s_yf, 4)

            def y_norm(t):
                dve.wait_ge(s_yroot, t + 1)
                order.then_wait(dve.reciprocal(rstd[:, t:t + 1], root[:, t:t + 1]))
                dve.scalar_tensor_tensor(z[:, t], z[:, t], rstd[:, t:t + 1], g_row[1], ALU.mult, ALU.mult) \
                   .then_inc(s_y_norm, 1)

            def ffn_group(i, last):
                for f in range(2):
                    for half in range(2):
                        n = 2 * f + half
                        dve.wait_ge(s_silu2, i * 4 + (n + 1))
                        dve.wait_ge(s_z, i * 8 + (2 * (T_FFN + 2 * f + 1) + half + 1))
                        dve.tensor_tensor(act2[half], ps[:, 2 + half, :], act2[half], ALU.mult).then_inc(s_a, 1)
                for q in range(2 * TT):
                    t, c = q // 2, q % 2
                    dst = z[:, t, c * HALF:(c + 1) * HALF]
                    dve.wait_ge(s_y, i * 16 + (q + 1))
                    dve.tensor_tensor(dst, ps[:, 4 + q % 4, :], dst, ALU.add).then_inc(s_yf, 1)
                    if last and c and t >= 1:
                        y_norm(t - 1)

            with dve.Fori(0, FG - 1) as i:
                ffn_group(i, False)
            ffn_group(FG - 1, True)
            y_norm(TT - 1)
            dve.wait_ge(s_y_norm, TT)
            dve.wait_ge(s_final, TT - 1)
            dve.tensor_tensor(x1[:, TT - 1], x1[:, TT - 1], z[:, TT - 1], ALU.add).then_inc(s_final, 1)


def _host():
    import numpy as np

    i, j = np.arange(P)[:, None], np.arange(P)[None, :]
    f = np.float32
    consts = np.stack([(i == j).astype(f), np.where(j <= i, 0, -BIG).astype(f), (i <= j).astype(f),
                       np.ones((P, P), f), -np.ones((P, P), f)], 1)
    j = np.arange(2 * P)[None, :]
    dist = i - j + P
    window = np.stack([np.where((dist >= 0) & (dist < WINDOW), -(2.0 ** -(h + 1)) * dist, -BIG)
                       for h in range(HEADS)], 1).astype(f).reshape(P, HEADS * 2 * P)
    distance = -(i + (L - P) - np.arange(L)[None, :]).astype(f)
    return consts, window, distance


def kernel(x, c, w_ada, b_ada, norm_g, w_in, conv_w, fox_bias, swa_sinks, w_branch, w_o, w_gate, w_up, w_down):
    import numpy as np
    import concourse.bacc as bacc
    from concourse.bass_utils import run_bass_kernel_spmd

    x, c, w_ada, b_ada, norm_g, w_in, conv_w, fox_bias, swa_sinks, w_branch, w_o, w_gate, w_up, w_down = (
        np.asarray(a) for a in (x, c, w_ada, b_ada, norm_g, w_in, conv_w, fox_bias, swa_sinks, w_branch, w_o,
                                w_gate, w_up, w_down))
    w_in, w_ada, b_ada, norm_g = w_in[0], w_ada[0], b_ada[0], norm_g[0]
    w_branch, w_o, w_gate, w_up, w_down = w_branch[0], w_o[0], w_gate[0], w_up[0], w_down[0]

    sizes = [256, 256, 256, 256, 64, 64, 256, 64, 4, 256, 256, 256, 4, 256, 128, 128, 4 * D]
    at = [sum(sizes[:i]) for i in range(len(sizes))]
    a_u, a_b, a_c, d_q, d_k, d_v, d_qi, d_ki, d_wi, f_q, f_k, f_v, f_f, s_q, s_k, s_v, g = at

    def span(a, n=P):
        return list(range(a, a + n))

    def tile(w, columns):
        return w[:, columns].reshape(-1, P, len(columns)).transpose(1, 0, 2).reshape(P, -1)

    z_cols = [span(d_qi), span(d_qi + P), span(d_ki, HD) + span(d_k, HD)]
    for ch in range(2):
        z_cols += [span(a_c + ch * P), span(a_u + ch * P)]
    z_cols += [span(a_b), span(a_b + P)]
    z_cols += [span(f_q), span(f_q + P), span(f_k), span(f_k + P)]
    z_cols += [span(s_q + t * HD, HD) + span(s_q + (t + 2) * HD, HD) for t in range(2)] + [span(s_k)]
    z_cols += [span(d_q), span(d_q + P)]
    w_z = np.stack([tile(w_in, cc) for cc in z_cols])
    w_v = tile(w_in, span(d_v, 64) + span(f_v, 256) + span(s_v, 128) + span(d_wi, 4) + span(f_f, 4))
    gates = []
    for n in (0, 2, 3, 1):
        for dt in range(KT):
            gates.append(np.concatenate([tile(w_in, span(g + n * D + dt * P)),
                                         tile(w_branch[n], span(dt * P))], 1))
    w_gates = np.stack(gates)
    w_ot = np.stack([tile(w_o, span(dt * P)) for dt in range(KT)])
    ffn = []
    for i in range(FG):
        down = [w_down[f * P:(f + 1) * P] for f in (2 * i, 2 * i + 1)]
        gate, up = ([tile(w, span(f * P)) for f in (2 * i, 2 * i + 1)] for w in (w_gate, w_up))
        ffn += [gate[0], up[0], down[0], gate[1], down[1], up[1]]
    w_ffn = np.stack(ffn)
    w_adat = w_ada.reshape(KT, P, 6, D).transpose(2, 0, 1, 3)

    def column(v):
        return v.reshape(KT, P).T

    bias = b_ada.reshape(6, D)
    cols = np.concatenate([column(c[0]), column(norm_g[0]), column(norm_g[2]), column(bias[0]), column(bias[1]),
                           column(bias[3]), column(bias[4]),
                           conv_w[0].reshape(3, BT, P).transpose(2, 1, 0).reshape(P, 6)], 1)
    rows = np.stack([bias[2], bias[5], norm_g[1], norm_g[3]])
    per_head = np.broadcast_to(np.concatenate([fox_bias[0], swa_sinks[0]])[None, :], (P, 8))
    consts, window, distance = _host()
    feeds = {"x": x[0], "w_z": w_z, "w_v": w_v, "w_gates": w_gates, "w_o": w_ot, "w_ffn": w_ffn, "w_ada": w_adat,
             "cols": cols, "rows": rows, "per_head": per_head, "consts": consts, "window_bias": window,
             "distance": distance}
    nc = bacc.Bacc("TRN2", target_bir_lowering=False, num_devices=1)
    arrays, args = {}, {}
    for name, a in feeds.items():
        a = np.ascontiguousarray(a)
        arrays[f"in_{name}"] = a
        args[name] = nc.dram_tensor(f"in_{name}", a.shape, mybir.dt.from_np(a.dtype), kind="ExternalInput").ap()
    args["out"] = nc.dram_tensor("out", (L, D), F32, kind="ExternalOutput").ap()
    build(nc, **args)
    r = run_bass_kernel_spmd(nc, [arrays], core_ids=[0])
    return r.results[0]["out"].reshape(1, L, D)
```
